# Optimizing a Trainium2 kernel written in Bass

```python
import jax, jax.numpy as jnp
from jax import lax
import numpy as np

D_MODEL = 1024
BATCH = 1
SEQ = 1024
DEPTH = 1

CHUNK = 64
D_MIX = D_MODEL
ATT_HEADS = 8
ATT_KV_HEADS = 2
ATT_GROUP = ATT_HEADS // ATT_KV_HEADS
ATT_HEAD_DIM = 64
WINDOW = 128
WINDOW_CHUNKS = WINDOW // CHUNK
ATT_WIDTH = ATT_HEADS * ATT_HEAD_DIM
ATT_KV_WIDTH = ATT_KV_HEADS * ATT_HEAD_DIM
M_HEADS = 4
M_QK_DIM = 64
M_V_DIM = 128
M_QK_WIDTH = M_HEADS * M_QK_DIM
M_WIDTH = M_HEADS * M_V_DIM
CONV_K = 4
D_FF = ((8 * D_MODEL + 3 * 256 - 1) // (3 * 256)) * 256
SPLIT_SIZES = (ATT_WIDTH, ATT_KV_WIDTH, ATT_KV_WIDTH,
               M_QK_WIDTH, M_QK_WIDTH, M_WIDTH, M_WIDTH, M_HEADS, M_HEADS)
D_IN_PROJ = sum(SPLIT_SIZES)
EPS = 1e-6

kernel_name = "hymba_swa_sink_mlstm_swiglu"

def rms_norm(x, g):
    xf = x.astype(jnp.float32)
    y = xf * lax.rsqrt(jnp.mean(xf * xf, axis=-1, keepdims=True) + EPS)
    return (y * g.astype(jnp.float32)).astype(x.dtype)

def causal_dwconv(x, w):
    s = x.shape[1]
    xp = jnp.pad(x, ((0, 0), (CONV_K - 1, 0), (0, 0)))
    y = xp[:, 0:s] * w[0]
    for i in range(1, CONV_K):
        y = y + xp[:, i:i + s] * w[i]
    return y

def sliding_window_attention(q, k, v, sinks, slopes):
    b, s = q.shape[0], q.shape[1]
    nc = s // CHUNK
    qc = q.reshape(b, nc, CHUNK, ATT_KV_HEADS, ATT_GROUP, ATT_HEAD_DIM)

    def band(t):
        tc = t.reshape(b, nc, CHUNK, ATT_KV_HEADS, ATT_HEAD_DIM)
        tp = jnp.pad(tc, ((0, 0), (WINDOW_CHUNKS - 1, 0), (0, 0), (0, 0), (0, 0)))
        return jnp.concatenate([tp[:, i:i + nc] for i in range(WINDOW_CHUNKS)], axis=2)

    kb, vb = band(k), band(v)
    scores = jnp.einsum('bcqkgd,bcskd->bckgqs', qc, kb).astype(jnp.float32) * (ATT_HEAD_DIM ** -0.5)
    qi = jnp.arange(CHUNK)
    si = jnp.arange(WINDOW)
    dist = jnp.abs(qi[:, None] + (WINDOW_CHUNKS - 1) * CHUNK - si[None, :]).astype(jnp.float32)
    bias = -slopes.reshape(ATT_KV_HEADS, ATT_GROUP, 1, 1) * dist
    key_chunk = jnp.arange(nc)[:, None] - (WINDOW_CHUNKS - 1) + si[None, :] // CHUNK
    valid = key_chunk >= 0
    scores = jnp.where(valid[None, :, None, None, None, :], scores + bias, -jnp.inf)
    sink = jnp.broadcast_to(sinks.astype(jnp.float32).reshape(1, 1, ATT_KV_HEADS, ATT_GROUP, 1, 1),
                            scores.shape[:-1] + (1,))
    probs = jax.nn.softmax(jnp.concatenate([scores, sink], axis=-1), axis=-1)[..., :-1]
    out = jnp.einsum('bckgqs,bcskd->bcqkgd', probs.astype(vb.dtype), vb)
    return out.reshape(b, s, ATT_WIDTH)

def mlstm_chunkwise(q, k, v, i_pre, f_pre):
    b, s = q.shape[0], q.shape[1]
    nc = s // CHUNK

    def chunks(t):
        return t.reshape(b, nc, CHUNK, M_HEADS, -1).transpose(0, 3, 1, 2, 4)

    def gchunks(t):
        return t.reshape(b, nc, CHUNK, M_HEADS).transpose(0, 3, 1, 2)

    qc, kc, vc = chunks(q), chunks(k * (M_QK_DIM ** -0.5)), chunks(v)
    li = gchunks(i_pre)
    lf = jax.nn.log_sigmoid(gchunks(f_pre))
    bcum = jnp.cumsum(lf, axis=-1)
    gtot = bcum[..., -1]

    a = gtot[..., None] - bcum + li
    m_intra = jnp.max(a, axis=-1)
    wgt = jnp.exp(a - m_intra[..., None])
    c_chunk = jnp.einsum('bhcs,bhcsd,bhcsv->bhcdv', wgt, kc, vc)
    n_chunk = jnp.einsum('bhcs,bhcsd->bhcd', wgt, kc)

    def step(carry, inp):
        c_prev, n_prev, m_prev = carry
        cc, ncv, mi, g = inp
        m_new = jnp.maximum(g + m_prev, mi)
        a_old = jnp.exp(g + m_prev - m_new)
        a_new = jnp.exp(mi - m_new)
        c_new = a_old[..., None, None] * c_prev + a_new[..., None, None] * cc
        n_new = a_old[..., None] * n_prev + a_new[..., None] * ncv
        return (c_new, n_new, m_new), (c_prev, n_prev, m_prev)

    init = (jnp.zeros((b, M_HEADS, M_QK_DIM, M_V_DIM), jnp.float32),
            jnp.zeros((b, M_HEADS, M_QK_DIM), jnp.float32),
            jnp.zeros((b, M_HEADS), jnp.float32))
    xs = (jnp.moveaxis(c_chunk, 2, 0), jnp.moveaxis(n_chunk, 2, 0),
          jnp.moveaxis(m_intra, 2, 0), jnp.moveaxis(gtot, 2, 0))
    _, (c_st, n_st, m_st) = lax.scan(step, init, xs)
    c_st = jnp.moveaxis(c_st, 0, 2)
    n_st = jnp.moveaxis(n_st, 0, 2)
    m_st = jnp.moveaxis(m_st, 0, 2)

    tril = jnp.tril(jnp.ones((CHUNK, CHUNK), dtype=bool))
    d = jnp.where(tril, bcum[..., :, None] - bcum[..., None, :] + li[..., None, :], -jnp.inf)
    e = bcum + m_st[..., None]
    m_j = jnp.maximum(e, jnp.max(d, axis=-1))
    sc = jnp.einsum('bhcjd,bhcsd->bhcjs', qc, kc) * jnp.exp(d - m_j[..., None])
    inter = jnp.exp(e - m_j)
    num = inter[..., None] * jnp.einsum('bhcjd,bhcdv->bhcjv', qc, c_st) + jnp.einsum('bhcjs,bhcsv->bhcjv', sc, vc)
    den = inter * jnp.einsum('bhcjd,bhcd->bhcj', qc, n_st) + jnp.sum(sc, axis=-1)
    h = num / jnp.maximum(jnp.abs(den), jnp.exp(-m_j))[..., None]
    return h.transpose(0, 2, 3, 1, 4).reshape(b, s, M_WIDTH)

def setup_inputs(seed: int = 0) -> dict:
    key = jax.random.key(seed)
    ks = jax.random.split(key, 20)
    n = jax.random.normal
    f32 = jnp.float32
    x = n(ks[0], (BATCH, SEQ, D_MODEL), f32)
    g_mix = 1.0 + 0.02 * n(ks[1], (DEPTH, D_MODEL), f32)
    w_in = n(ks[2], (DEPTH, D_MODEL, D_IN_PROJ), f32) * D_MODEL ** -0.5
    b_i = 0.1 * n(ks[3], (DEPTH, M_HEADS), f32)
    b_f = jnp.linspace(3.0, 6.0, M_HEADS, dtype=f32)[None, :] + 0.1 * n(ks[4], (DEPTH, M_HEADS), f32)
    b_gates = jnp.concatenate([b_i, b_f], axis=-1)
    conv_qk = n(ks[5], (DEPTH, CONV_K, 2 * M_QK_WIDTH), f32) * CONV_K ** -0.5
    q_norm_gain = 1.0 + 0.02 * n(ks[6], (DEPTH, ATT_HEAD_DIM), f32)
    k_norm_gain = 1.0 + 0.02 * n(ks[7], (DEPTH, ATT_HEAD_DIM), f32)
    attn_sinks = n(ks[8], (DEPTH, ATT_HEADS), f32)
    g_attn_out = 1.0 + 0.02 * n(ks[9], (DEPTH, ATT_WIDTH), f32)
    g_mlstm_out = 1.0 + 0.02 * n(ks[10], (DEPTH, M_WIDTH), f32)
    w_out = n(ks[11], (DEPTH, D_MIX, D_MODEL), f32) * D_MIX ** -0.5
    g_ffn = 1.0 + 0.02 * n(ks[12], (DEPTH, D_MODEL), f32)
    w_gate = n(ks[13], (DEPTH, D_MODEL, D_FF), f32) * D_MODEL ** -0.5
    w_up = n(ks[14], (DEPTH, D_MODEL, D_FF), f32) * D_MODEL ** -0.5
    w_down = n(ks[15], (DEPTH, D_FF, D_MODEL), f32) * D_FF ** -0.5
    return {"x": x, "g_mix": g_mix, "w_in": w_in, "b_gates": b_gates, "conv_qk": conv_qk,
            "q_norm_gain": q_norm_gain, "k_norm_gain": k_norm_gain, "attn_sinks": attn_sinks,
            "g_attn_out": g_attn_out, "g_mlstm_out": g_mlstm_out, "w_out": w_out,
            "g_ffn": g_ffn, "w_gate": w_gate, "w_up": w_up, "w_down": w_down}

def reference(x, g_mix, w_in, b_gates, conv_qk, q_norm_gain, k_norm_gain, attn_sinks,
              g_attn_out, g_mlstm_out, w_out, g_ffn, w_gate, w_up, w_down):
    b, s = x.shape[0], x.shape[1]
    split_idx = [int(v) for v in np.cumsum(SPLIT_SIZES)[:-1]]
    slopes = jnp.exp2(-8.0 * (jnp.arange(ATT_HEADS, dtype=jnp.float32) + 1.0) / ATT_HEADS)
    for l in range(DEPTH):
        h = rms_norm(x, g_mix[l])
        p = h @ w_in[l]
        aq, ak, av, mq, mk, mv, mo, mi, mf = jnp.split(p, split_idx, axis=-1)

        aq = rms_norm(aq.reshape(b, s, ATT_HEADS, ATT_HEAD_DIM), q_norm_gain[l])
        ak = rms_norm(ak.reshape(b, s, ATT_KV_HEADS, ATT_HEAD_DIM), k_norm_gain[l])
        av = av.reshape(b, s, ATT_KV_HEADS, ATT_HEAD_DIM)
        att = sliding_window_attention(aq, ak, av, attn_sinks[l], slopes)

        qk = jax.nn.silu(causal_dwconv(jnp.concatenate([mq, mk], axis=-1), conv_qk[l]))
        mq, mk = jnp.split(qk, [M_QK_WIDTH], axis=-1)
        gates = jnp.concatenate([mi, mf], axis=-1).astype(jnp.float32) + b_gates[l].astype(jnp.float32)
        i_pre, f_pre = jnp.split(gates, [M_HEADS], axis=-1)
        f32 = jnp.float32
        mh = mlstm_chunkwise(mq.reshape(b, s, M_HEADS, M_QK_DIM).astype(f32),
                             mk.reshape(b, s, M_HEADS, M_QK_DIM).astype(f32),
                             mv.reshape(b, s, M_HEADS, M_V_DIM).astype(f32),
                             i_pre, f_pre)
        mh = (jax.nn.sigmoid(mo.astype(f32)) * mh).astype(x.dtype)

        mix = jnp.concatenate([rms_norm(att, g_attn_out[l]), rms_norm(mh, g_mlstm_out[l])], axis=-1)
        x = x + mix @ w_out[l]

        h2 = rms_norm(x, g_ffn[l])
        x = x + (jax.nn.silu(h2 @ w_gate[l]) * (h2 @ w_up[l])) @ w_down[l]
    return x


_drawn_inputs = setup_inputs


def setup_inputs(seed=0):
    import zlib

    import numpy as np

    out = dict(_drawn_inputs(seed))
    spreads = {}
    factors = {'q_norm_gain': 5.648,
     'k_norm_gain': 6.176,
     'g_attn_out': 5.147,
     'g_mlstm_out': 5.089,
     'g_ffn': 5.124}
    for name, (base, spread) in spreads.items():
        noise = np.random.default_rng([zlib.crc32(name.encode()), seed]).standard_normal(out[name].shape)
        drawn = base * np.exp(spread * noise) if base else spread * noise
        out[name] = __import__('jax').numpy.asarray(drawn.astype(out[name].dtype))
    for name, factor in factors.items():
        out[name] = (out[name] * factor).astype(out[name].dtype)
    return out
```

```python
from contextlib import ExitStack

import numpy as np

import concourse.bass as bass
from concourse import mybir

ALU = mybir.AluOpType
ACT = mybir.ActivationFunctionType
AX = mybir.AxisListType
F32 = mybir.dt.float32
F32R = mybir.dt.float32r

P = 128
CHUNK = 64
HEADS = 8
KV = 2
HD = 64
MH = 4
DK = 64
DV = 128
TAPS = 4
EPS = 1e-6
NEG = -1.0e30

C_ID, C_TRI, C_EVEN, C_ODD, C_FIRST = 0, 128, 256, 768, 1280
C_END = 1792
G_CONV, G_ATT, G_K, G_Q, G_ROWS = 0, 16, 20, 21, 22


def constants():
    c = np.zeros((P, C_END), np.float32)
    c[:, C_ID:C_ID + P] = np.eye(P)
    c[:, C_TRI:C_TRI + P] = np.triu(np.ones((P, P)))
    row = np.arange(P)
    q, i2 = row % CHUNK, row // CHUNK
    key = np.arange(P)
    for start, order in ((C_EVEN, "cur_prev"), (C_ODD, "prev_cur"), (C_FIRST, "cur_prev")):
        s = (key + CHUNK) % P if order == "cur_prev" else key
        dist = np.abs(q[:, None] + CHUNK - s[None, :])
        for kv in range(KV):
            for b in range(2):
                slope = 2.0 ** -(kv * 4 + b * 2 + i2 + 1.0)
                blk = -slope[:, None] * dist
                if start == C_FIRST:
                    blk = np.where(s[None, :] < CHUNK, NEG, blk)
                a = start + (kv * 2 + b) * P
                c[:, a:a + P] = blk
    return c


def hymba_block(nc, x, g_mix, w_in, b_gates, conv_qk, q_gain, k_gain, sinks,
                g_att, g_ml, w_out, g_ffn, w_gate, w_up, w_down, consts, out):
    S, D = x.shape[1], x.shape[2]
    DFF = w_gate.shape[2]
    T = S // P
    K = D // P
    N = 512
    F = DFF // P
    PAIRS = F // 2
    AQ, AK = 0, HEADS * HD
    MQ = AK + 2 * KV * HD
    MV = MQ + 2 * MH * DK
    MO = MV + MH * DV
    GATES = MO + MH * DV
    NKV = 2 * MH + 2 * KV * HD
    RING, RAW = 16, 2
    GROUPS = 7
    UNITS = 5 * T
    ALL = GROUPS * T
    assert T == 8 and K == 8 and F % 2 == 0 and MQ + 512 == MV

    x_t = x.rearrange("a (t p) d -> t p (a d)", p=P)
    out_t = out.rearrange("a (t p) d -> t p (a d)", p=P)
    w_in_k = w_in.rearrange("a (k p) n -> k p (a n)", p=P)
    w_out_k = w_out.rearrange("a (k p) n -> k p (a n)", p=P)
    w_gate_k = w_gate.rearrange("a (k p) n -> p (a k) n", p=P)
    w_up_k = w_up.rearrange("a (k p) n -> p (a k) n", p=P)
    w_down_r = w_down.rearrange("a f n -> (a f) n")

    ctx = ExitStack()
    with ctx:
        base = [(nc.sbuf_base + 31) // 32 * 32]

        def place(name, shape, dt=F32, at=None):
            size = 4 * int(np.prod(shape[1:]))
            start = base[0] if at is None else at
            assert start + size <= nc.sbuf_usable_end, (name, start + size - nc.sbuf_usable_end)
            t = nc.alloc_sbuf_tensor_at(name, list(shape), dt, offset=start)
            end = (start + size + 31) // 32 * 32
            if at is None:
                base[0] = end
            return t, end

        def sem(name):
            return ctx.enter_context(nc.semaphore(name))

        actT_hi, _ = place("actT_hi", [P, K, S], F32R)
        actT_lo, _ = place("actT_lo", [P, K, S], F32R)
        w_hi, _ = place("w_hi", [P, RING, N], F32R)
        w_lo, _ = place("w_lo", [P, RING, N], F32R)
        w_raw, _ = place("w_raw", [P, RAW, N])
        ident, _ = place("ident", [P, P])
        tri, _ = place("tri", [P, P])
        ones, _ = place("ones", [P, P])
        cols, _ = place("cols", [P, G_ROWS + 2])
        bias_g, _ = place("bias_g", [P, 8])
        sinks8, _ = place("sinks8", [P, 8])
        sink_b, _ = place("sink_b", [P, 8])
        g_row, _ = place("g_row", [P, D])
        stat, _ = place("stat", [P, T])
        rstd, _ = place("rstd", [P, T])
        ss2, _ = place("ss2", [P, T, 2])
        rmix, _ = place("rmix", [P, T, 2])
        gate8, _ = place("gate8", [P, T, 8])
        small = {}
        for name in ("absf", "expf", "lf", "u", "mlast", "aold", "wexp", "enm", "maxu_b"):
            small[name], _ = place(name, [P, T * MH])
        absf, expf, lf, u_col = small["absf"], small["expf"], small["lf"], small["u"]
        mlast, aold, wexp, enm = small["mlast"], small["aold"], small["wexp"], small["enm"]
        gm, maxu_b = absf, small["maxu_b"]
        bg, _ = place("bg", [P, 2 * T * MH])
        mm, _ = place("mm", [P, T + 1, MH])
        aold2, _ = place("aold2", [P, T, 2])
        den4, _ = place("den4", [P, MH])
        smx, _ = place("smx", [P, 8])
        nmx, _ = place("nmx", [P, 8])
        dsum, _ = place("dsum", [P, 8])
        esk, _ = place("esk", [P, 8])
        qss, _ = place("qss", [P, 8])
        qrs, _ = place("qrs", [P, 8])
        kss, _ = place("kss", [P, 2 * T])
        krs, _ = place("krs", [P, 2 * T])

        J = base[0]
        w0_raw, j_end = place("w0_raw", [P, K, N], at=J)
        ksq, _ = place("ksq", [P, T, P], at=J)
        cm, e = place("cm", [32, P], at=J + 4096)
        uT, e = place("uT", [32, P], at=e)
        nM, e = place("nM", [32, P], at=e)
        diag, e = place("diag", [32, 32], at=e)
        mcol, e = place("mcol", [32, 1], at=e)
        mwork = e
        dmat, e = place("dmat", [P, MH, P], at=mwork)
        scd, e = place("scd", [P, MH, P], at=e)
        itr, e = place("itr", [P, 2, P], at=e)
        kw, e = place("kw", [P, MH, DK], at=e)
        qi, e = place("qi", [P, 2, P], at=e)
        cst, e = place("cst", [P, 2, DV + 1], at=e)
        msq, e = place("msq", [P, MH * DV], at=e)
        sig0, _ = place("sig0", [P, N], at=J)
        sig1, _ = place("sig1", [P, N], at=J + 2048)
        sig = [sig0, sig1]
        assert e <= j_end, (e, j_end)
        G = j_end
        rawT, g_end = place("rawT", [P, 4, 3 + S], at=G)
        mh, _ = place("mh", [P, T, MH * DV], at=G)
        x1, _ = place("x1", [P, T, D], at=J)
        assert J + 4 * T * D <= g_end
        V = g_end
        kvs, e = place("kvs", [P, T, NKV], at=V)
        v_even, e = place("v_even", [P, T, KV * HD], at=e)
        kT, v_end = place("kT", [P, CHUNK + S], at=e)
        h2buf0, e = place("h2buf0", [P, D], at=V)
        h2buf1, e = place("h2buf1", [P, D], at=e)
        junk2, e = place("junk2", [P, D], at=e)
        h2buf = [h2buf0, h2buf1]
        assert e <= v_end
        E = v_end
        x_in0, e = place("x_in0", [P, D], at=E)
        x_in1, e = place("x_in1", [P, D], at=e)
        h_buf0, e = place("h_buf0", [P, D], at=e)
        h_buf1, e = place("h_buf1", [P, D], at=e)
        junk, e = place("junk", [P, D], at=e)
        mqraw0, e = place("mqraw0", [P, N], at=e)
        mqraw1, e = place("mqraw1", [P, N], at=e)
        prow, e = place("prow", [G_ROWS, P], at=e)
        x_in, h_buf, mqraw = [x_in0, x_in1], [h_buf0, h_buf1], [mqraw0, mqraw1]
        qkT, e = place("qkT", [P, 4, S], at=E)
        mvx, e = place("mvx", [P, T, MH, DV + 1], at=e)
        mhs, e = place("mhs", [P, MH * DV], at=e)
        bias, e = place("bias", [P, 3, N], at=E)
        qT0, e = place("qT0", [P, 4, P], at=e)
        qT1, e = place("qT1", [P, 4, P], at=e)
        prob, e = place("prob", [P, 8, P], at=e)
        pT0, e = place("pT0", [P, 8, P], at=e)
        pT1, e = place("pT1", [P, 8, P], at=e)
        aq0, e = place("aq0", [P, N], at=e)
        aq1, e = place("aq1", [P, N], at=e)
        qn, e = place("qn", [P, 4, KV, HD], at=e)
        sqb, e = place("sqb", [P, N], at=e)
        pq, e = place("pq", [P, N], at=e)
        qT, pT, aqs = [qT0, qT1], [pT0, pT1], [aq0, aq1]
        act_hi = [None, None]
        act_lo = [None, None]
        act_hi[0], e = place("act_hi0", [P, S], F32R, at=E)
        act_lo[0], e = place("act_lo0", [P, S], F32R, at=e)
        act_hi[1], e = place("act_hi1", [P, S], F32R, at=e)
        act_lo[1], e = place("act_lo1", [P, S], F32R, at=e)
        prod, e = place("prod", [P, S], at=e)
        silu0, e = place("silu0", [P, N], at=e)
        silu1, e = place("silu1", [P, N], at=e)
        silu = [silu0, silu1]

        bank = [ctx.enter_context(nc.psum_tensor(f"bank{i}", [P, N], F32)) for i in range(8)]

        x_in_s = [sem("x_loaded0"), sem("x_loaded1")]
        par_s = sem("params_loaded")
        late_s = sem("late_params_loaded")
        raw_s = [sem(f"raw_loaded{i}") for i in range(RAW)]
        w0_s = [sem(f"w0_loaded{i}") for i in range(K)]
        x1_s = [sem(f"x1_loaded{i}") for i in range(2)]
        gf_s = sem("g_ffn_loaded")
        out_s = sem("out_stored")
        ones_set = sem("ones_set")
        w0_hi = sem("w0_hi")
        w0_ready = sem("w0_ready")
        w_hi_s = sem("w_hi_done")
        w_ready = sem("w_ready")
        unit_done = sem("unit_done")
        acc_free = [sem("acc_free0"), sem("acc_free1")]
        dve_step = sem("dve_step")
        act_step = sem("act_step")
        pe_step = sem("pe_step")
        rstd_ready = sem("rstd_ready")
        h_ready = sem("h_ready")
        h_tp = sem("h_transposed")
        h_hi = sem("h_hi")
        h_split = sem("h_split")
        cols_tp = sem("cols_transposed")
        cols_ready = sem("cols_ready")
        mq_tp = sem("mq_transposed")
        mq_evac = sem("mq_evac")
        conv_ready = sem("conv_ready")
        qk_ready = sem("qk_ready")
        kv_stat = sem("kv_stat")
        kv_rs = sem("kv_rs")
        kn_ready = sem("kn_ready")
        gate_mm = sem("gate_mm")
        kT_tp = sem("kT_transposed")
        gate_v = sem("gate_v")
        gate_a = sem("gate_a")
        bc_done = sem("bc_done")
        sc_done = sem("sc_done")
        kt_done = sem("kt_done")
        d_exp = sem("d_exp")
        it_exp = sem("it_exp")
        d_masked = sem("d_masked")
        kw_ready = sem("kw_ready")
        scd_ready = sem("scd_ready")
        num_done = sem("num_done")
        cup_done = sem("cup_done")
        c_ready = sem("c_ready")
        h_done = sem("mlstm_h_done")
        sig_ready = sem("sig_ready")
        mh_ready = sem("mh_ready")
        ssb_done = sem("ssb_done")
        aq_ready = sem("aq_ready")
        q_stat = sem("q_stat")
        q_rs = sem("q_rs")
        qn_ready = sem("qn_ready")
        q_tp = sem("q_transposed")
        mh_tp = sem("mh_transposed")
        qT_ready = sem("qT_ready")
        mixb_hi = sem("mixb_hi")
        mixb_ready = sem("mixb_ready")
        s_even = sem("scores_even")
        s_odd = sem("scores_odd")
        s_evac = sem("scores_evac")
        s_max = sem("scores_max")
        p_exp = sem("p_exp")
        p_ready = sem("p_ready")
        pt_done = sem("p_transposed")
        pTa = sem("pT_act")
        pTd = sem("pT_dve")
        pv_done = sem("pv_done")
        sqa_done = sem("sqa_done")
        mixa_hi = sem("mixa_hi")
        mixa_ready = sem("mixa_ready")
        ssa_mm = sem("ssa_mm")
        ssa_ready = sem("ssa_ready")
        rmix_ready = sem("rmix_ready")
        wa_done = sem("wa_done")
        wb_done = sem("wb_done")
        wa_free = sem("wa_free")
        x1_ready = sem("x1_ready")
        r2_ready = sem("r2_ready")
        h2_ready = sem("h2_ready")
        h2_tp = sem("h2_transposed")
        h2_hi = sem("h2_hi")
        h2_split = sem("h2_split")
        gate_done = sem("gate_done")
        up_done = sem("up_done")
        silu_done = sem("silu_done")
        prod_done = sem("prod_done")
        act_hi_s = sem("act_hi_done")
        act_ready = sem("act_ready")
        down_mm = sem("down_mm")
        down_add = sem("down_add")

        def slice_source(n):
            g, k = 1 + n // K, n % K
            if g == 1:
                return [((0, 8), w_in_k[k, :, GATES:GATES + 8]),
                        ((8, NKV), w_in_k[k, :, AK:AK + 2 * KV * HD])]
            if g < 5:
                c = {2: MV, 3: MO, 4: AQ}[g]
                return [((0, N), w_in_k[k, :, c:c + N])]
            return [((0, N), w_out_k[k, :, (g - 5) * N:(g - 4) * N])]

        NS = 6 * K

        def raw_count(n):
            return sum(16 * len(slice_source(m)) for m in range(n % RAW, n + 1, RAW))

        RAW_BASE = [raw_count(NS - RAW + r) for r in range(RAW)]
        FFN_RING = {"even": 8, "odd": 12, "down": 0}

        def strip_pieces(f, s):
            w = w_gate_k if s < 2 else w_up_k
            return w[:, 4 * (s % 2):4 * (s % 2) + 4, bass.ds(f * P, P)]

        def down_piece(f, half):
            return w_down_r[bass.ds(f * P, P), half * N:(half + 1) * N]

        def bcast(ap, n):
            return ap.unsqueeze(len(ap.shape)).to_broadcast(list(ap.shape) + [n])

        block = ctx.enter_context(nc.Block())

        @block.sync
        def _(sp):
            def load_x(t):
                if t >= 2:
                    sp.wait_ge(h_ready, t - 1)
                sp.dma_start(x_in[t % 2][:, :], x_t[t]).then_inc(x_in_s[t % 2], 16)

            load_x(0)
            sp.dma_start(g_row[:, :], g_mix[0:1, :].to_broadcast([P, D])).then_inc(par_s, 16)
            sp.dma_start(ident[:, :], consts[:, C_ID:C_ID + P]).then_inc(par_s, 16)
            for k in range(K):
                sp.dma_start(w0_raw[:, k, :], w_in_k[k, :, MQ:MQ + N]).then_inc(w0_s[k], 16)
                if k == 1:
                    load_x(1)
            sp.dma_start(tri[:, :], consts[:, C_TRI:C_TRI + P]).then_inc(par_s, 16)
            sp.dma_start(prow[G_CONV:G_CONV + 16, :],
                         conv_qk.rearrange("a i (f p) -> (a i f) p", p=P)).then_inc(par_s, 16)
            sp.dma_start(prow[G_ATT:G_ATT + 4, :], g_att.rearrange("a (k p) -> (a k) p", p=P)).then_inc(par_s, 16)
            for half in range(2):
                sp.dma_start(prow[G_K:G_K + 1, half * HD:(half + 1) * HD], k_gain).then_inc(par_s, 16)
                sp.dma_start(prow[G_Q:G_Q + 1, half * HD:(half + 1) * HD], q_gain).then_inc(par_s, 16)
            sp.dma_start(bias_g[:, :], b_gates[0:1, :].to_broadcast([P, 8])).then_inc(par_s, 16)
            sp.dma_start(sinks8[:, :], sinks[0:1, :].to_broadcast([P, 8])).then_inc(par_s, 16)

            xt = 2
            for n in range(NS):
                if n >= RAW:
                    sp.wait_ge(w_ready, n - RAW + 1)
                for (a, b), src in slice_source(n):
                    sp.dma_start(w_raw[:, n % RAW, a:b], src).then_inc(raw_s[n % RAW], 16)
                if xt < T:
                    load_x(xt)
                    xt += 1
                if n == 2 * K + 4:
                    sp.wait_ge(h_ready, T)
                    sp.dma_start(g_row[:, 0:MH * DV], g_ml[0:1, :].to_broadcast([P, MH * DV])).then_inc(late_s, 16)
                if n == 4 * K + 4:
                    sp.wait_ge(mh_ready, T)
                    sp.wait_ge(cup_done, T)
                    for i, c in enumerate((C_EVEN, C_ODD, C_FIRST)):
                        sp.dma_start(bias[:, i, :], consts[:, c:c + N]).then_inc(late_s, 16)
                    sp.wait_ge(ssb_done, T)
                    for t in range(4):
                        sp.dma_start(x1[:, t, :], x_t[t]).then_inc(x1_s[0], 16)
                    sp.dma_start(g_row[:, :], g_ffn[0:1, :].to_broadcast([P, D])).then_inc(gf_s, 16)
            sp.wait_ge(mh_tp, T)
            for t in range(4, T):
                sp.dma_start(x1[:, t, :], x_t[t]).then_inc(x1_s[1], 16)

            def ffn_load(source, m, count):
                sp.wait_ge(w_ready, count + (m - RAW + 1))
                dst = w_raw[:, m % RAW, :]
                if len(source.shape) == 3:
                    dst = dst.rearrange("p (k n) -> p k n", k=4)
                sp.dma_start(dst, source).then_inc(raw_s[m % RAW], 16)

            for f in range(2):
                for s in range(4):
                    ffn_load(strip_pieces(f, s), 4 * f + s, NS)
            with sp.Fori(1, PAIRS) as i:
                count = NS + 8 + (i - 1) * 12
                for s in range(4):
                    ffn_load(strip_pieces(2 * i, s), s, count)
                for s in range(4):
                    ffn_load(down_piece(2 * i - 2 + s % 2, s // 2), 4 + s, count)
                for s in range(4):
                    ffn_load(strip_pieces(2 * i + 1, s), 8 + s, count)
            for s in range(4):
                ffn_load(down_piece(F - 2 + s % 2, s // 2), s, NS + 8 + 12 * (PAIRS - 1))

            for m in range(2 * T):
                sp.wait_ge(down_add, 2 * T * (PAIRS - 1) + m + 1)
                t, half = m % T, m // T
                sp.dma_start(out_t[t, :, half * N:(half + 1) * N],
                             x1[:, t, half * N:(half + 1) * N]).then_inc(out_s, 16)
            sp.wait_ge(out_s, 16 * 2 * T)

        @block.gpsimd
        def _(pool):
            def split(ring, raw, width, loaded, n):
                pool.wait_ge(raw_s[raw], loaded)
                nc.gpsimd.tensor_tensor(w_hi[:, ring, 0:width], w_raw[:, raw, 0:width],
                                        ones[:, 0:1].to_broadcast([P, width]), ALU.mult).then_inc(w_hi_s, 1)
                pool.wait_ge(w_hi_s, n + 1)
                nc.gpsimd.tensor_tensor(w_lo[:, ring, 0:width], w_raw[:, raw, 0:width],
                                        w_hi[:, ring, 0:width].bitcast(F32), ALU.subtract).then_inc(w_ready, 1)

            def mask(t):
                pool.wait_ge(d_exp, t + 1)
                nc.gpsimd.affine_select(out=dmat[:, :, :], in_=dmat[:, :, :], pattern=[[0, MH], [1, P]],
                                        compare_op=ALU.is_ge, fill=0.0, base=0,
                                        channel_multiplier=-1).then_inc(d_masked, 1)

            pool.wait_ge(ones_set, 1)
            for n in range(NS):
                g = 1 + n // K
                if g >= 2 and n % K == 0:
                    pool.wait_ge(unit_done, (g - 1) * T)
                split((g * K + n % K) % RING, n % RAW, NKV if g == 1 else N, raw_count(n), n)
                if g == 4:
                    mask(n % K)

            def ffn_split(kind, s, m, base_n, loads):
                split(FFN_RING[kind] + s, m % RAW, N, RAW_BASE[m % RAW] + 16 * (loads + m // RAW + 1),
                      base_n + m)

            pool.wait_ge(wb_done, T)
            for f in range(2):
                for s in range(4):
                    ffn_split(("even", "odd")[f], s, 4 * f + s, NS, 0)
            pool.wait_ge(wb_done, 2 * T)
            with pool.Fori(1, PAIRS) as i:
                base_n = NS + 8 + (i - 1) * 12
                loads = 4 + (i - 1) * 6
                pool.wait_ge(up_done, 4 * i - 2)
                for s in range(4):
                    ffn_split("even", s, s, base_n, loads)
                pool.wait_ge(up_done, 4 * i - 1)
                for s in range(4):
                    ffn_split("down", s, 4 + s, base_n, loads)
                pool.wait_ge(up_done, 4 * i)
                for s in range(4):
                    ffn_split("odd", s, 8 + s, base_n, loads)
            pool.wait_ge(down_mm, 2 * T * (PAIRS - 1))
            for s in range(4):
                ffn_split("down", s, s, NS + 8 + 12 * (PAIRS - 1), 4 + 6 * (PAIRS - 1))

        @block.tensor
        def _(pe):
            steps = [0]

            def fence(ins):
                steps[0] += 1
                ins.then_inc(pe_step, 1)
                pe.wait_ge(pe_step, steps[0])

            def three(ps, x_hi, x_lo, wh, wl, first, last):
                nc.tensor.matmul(ps, x_hi, wh, start=first, stop=False)
                nc.tensor.matmul(ps, x_hi, wl, start=False, stop=False)
                return nc.tensor.matmul(ps, x_lo, wh, start=False, stop=last)

            def transpose_h(src, t, ready, tp, split_s):
                pe.wait_ge(ready, t + 1)
                for b in range(2):
                    if t >= 1:
                        pe.wait_ge(split_s, 2 * (t - 1) + b + 1)
                    for j in range(4):
                        last = nc.tensor.transpose(bank[2 + b][:, j * P:(j + 1) * P],
                                                   src[t % 2][:, (4 * b + j) * P:(4 * b + j + 1) * P],
                                                   ident[:, :])
                    last.then_inc(tp, 1)

            def unit(U):
                g, t = U // T, U % T
                width = NKV if g == 1 else N
                ps = bank[U % 2][:, 0:width]
                if U >= 2:
                    pe.wait_ge(acc_free[U % 2], U // 2)
                if g == 0:
                    pe.wait_ge(h_split, 2 * t + 2)
                for k in range(K):
                    if t == 0:
                        if g == 0:
                            pe.wait_ge(w0_ready, k + 1)
                        else:
                            pe.wait_ge(w_ready, (g - 1) * K + k + 1)
                    r = (g * K + k) % RING
                    a = slice(t * P, (t + 1) * P)
                    last = three(ps, actT_hi[:, k, a], actT_lo[:, k, a], w_hi[:, r, 0:width],
                                 w_lo[:, r, 0:width], k == 0, k == K - 1)
                last.then_inc(unit_done, 1)

            def mq_transposes(t):
                pe.wait_ge(acc_free[t % 2], t // 2 + 1)
                if t >= 1:
                    pe.wait_ge(mq_evac, t)
                for f in range(4):
                    last = nc.tensor.transpose(bank[4][:, f * P:(f + 1) * P],
                                               mqraw[t % 2][:, f * P:(f + 1) * P], ident[:, :])
                last.then_inc(mq_tp, 1)

            def mlstm_scores(t):
                if t >= 1:
                    pe.wait_ge(it_exp, t)
                for h in range(MH):
                    c = t * MH + h
                    last = nc.tensor.matmul(bank[4][:, h * P:(h + 1) * P],
                                            ident[0:32, c:c + 1].to_broadcast([32, P]), nM[:, :],
                                            start=True, stop=True)
                last.then_inc(bc_done, 1)
                if t >= 1:
                    pe.wait_ge(scd_ready, t)
                a = slice(t * P, (t + 1) * P)
                for h in (0, 2, 1, 3):
                    rows = slice((h % 2) * DK, (h % 2 + 1) * DK)
                    last = nc.tensor.matmul(bank[5][:, h * P:(h + 1) * P], qkT[rows, 2 + h // 2, a],
                                            qkT[rows, h // 2, a], start=True, stop=True)
                    if h == 2:
                        fence(last)
                last.then_inc(sc_done, 1)
                if t >= 1:
                    pe.wait_ge(kw_ready, t)
                for p in range(2):
                    last = nc.tensor.transpose(bank[2][:, p * P:(p + 1) * P], qkT[:, 2 + p, a], ident[:, :])
                last.then_inc(kt_done, 1)

            def mlstm_products(t):
                pe.wait_ge(scd_ready, t + 1)
                pe.wait_ge(c_ready, t + 1)
                if t >= 1:
                    pe.wait_ge(h_done, t)
                for h in range(MH):
                    rows = slice((h % 2) * DK, (h % 2 + 1) * DK)
                    ps = bank[6 + h % 2][:, (h // 2) * (DV + 1):(h // 2 + 1) * (DV + 1)]
                    nc.tensor.matmul(ps, scd[:, h, :], mvx[:, t, h, :], start=True, stop=False)
                    last = nc.tensor.matmul(ps, qi[rows, h // 2, :], cst[rows, h // 2, :],
                                            start=False, stop=True)
                last.then_inc(num_done, 1)
                for h in range(MH):
                    rows = slice((h % 2) * DK, (h % 2 + 1) * DK)
                    last = nc.tensor.matmul(bank[3][rows, (h // 2) * (DV + 1):(h // 2 + 1) * (DV + 1)],
                                            kw[:, h, :], mvx[:, t, h, :], start=True, stop=True)
                last.then_inc(cup_done, 1)

            def att_sumsq(t):
                pe.wait_ge(sqa_done, t + 1)
                if t + 3 < T:
                    pe.wait_ge(mixb_ready, t + 4)
                else:
                    pe.wait_ge(mixb_ready, T)
                for kk in range(4):
                    last = nc.tensor.matmul(bank[3][:, 0:1], sqb[:, kk * P:(kk + 1) * P], ones[:, 0:1],
                                            start=(kk == 0), stop=(kk == 3))
                last.then_inc(ssa_mm, 1)

            def att_transposes(t):
                pe.wait_ge(qn_ready, t + 1)
                if t >= 4:
                    pe.wait_ge(mixa_ready, t - 3)
                blocks = bank[2][:, :].rearrange("p (b c i n) -> p b c i n", b=2, c=2, i=2)
                for i in range(4):
                    last = nc.tensor.transpose(blocks[:, i // 2, :, i % 2, :],
                                               qn[:, i, :, :].rearrange("p a b -> p (a b)"), ident[:, :])
                last.then_inc(q_tp, 1)
                if t >= 1:
                    pe.wait_ge(mixb_ready, t)
                if t >= 4:
                    pe.wait_ge(ssa_ready, t - 3)
                for kk in range(4):
                    last = nc.tensor.transpose(bank[3][:, kk * P:(kk + 1) * P],
                                               mh[:, t, kk * P:(kk + 1) * P], ident[:, :])
                last.then_inc(mh_tp, 1)

            def att_scores(t):
                pe.wait_ge(qT_ready, t + 1)
                if t >= 1:
                    pe.wait_ge(s_evac, t)
                q = qT[t % 2]
                for kv in range(KV):
                    for c2, done in ((0, s_even), (1, s_odd)):
                        rows = slice(kv * HD, (kv + 1) * HD)
                        for b in range(2):
                            lhsT = q[rows, 2 * b + c2, :]
                            o = (kv * 2 + b) * P
                            start = t * P
                            if c2 == 0:
                                nc.tensor.matmul(bank[4][:, o:o + CHUNK], lhsT,
                                                 kT[rows, start + CHUNK:start + 2 * CHUNK],
                                                 start=True, stop=True)
                                last = nc.tensor.matmul(bank[4][:, o + CHUNK:o + P], lhsT,
                                                        kT[rows, start:start + CHUNK], start=True, stop=True)
                            else:
                                last = nc.tensor.matmul(bank[5][:, o:o + P], lhsT,
                                                        kT[rows, start + CHUNK:start + CHUNK + P],
                                                        start=True, stop=True)
                        if kv == 1:
                            last.then_inc(done, 1)
                    if kv == 0:
                        fence(last)

            def att_prob_transposes(t):
                pe.wait_ge(p_ready, t + 1)
                for c2 in range(2):
                    if t >= 1:
                        pe.wait_ge((pTa, pTd)[c2], t)
                    for j in range(4):
                        last = nc.tensor.transpose(bank[6 + c2][:, j * P:(j + 1) * P],
                                                   prob[:, c2 * 4 + j, :], ident[:, :])
                last.then_inc(pt_done, 1)

            def att_values(t):
                pe.wait_ge(pTa, t + 1)
                pe.wait_ge(pTd, t + 1)
                if t + 3 < T:
                    pe.wait_ge(qT_ready, t + 4)
                elif t >= 1:
                    pe.wait_ge(mixa_ready, t)
                for c2 in range(2):
                    for kv in range(KV):
                        if c2 == 0:
                            v = v_even[:, t, kv * HD:(kv + 1) * HD]
                        else:
                            v = kvs[:, t, 2 * MH + (KV + kv) * HD:2 * MH + (KV + kv + 1) * HD]
                        for i2 in range(2):
                            rows = slice(i2 * HD, (i2 + 1) * HD)
                            b0 = c2 * 4 + kv * 2
                            rhs = pT[t % 2][:, b0:b0 + 2, i2 * CHUNK:(i2 + 1) * CHUNK]
                            o = bank[2][rows, kv * 2 * P:(kv + 1) * 2 * P].rearrange("p (b n) -> p b n", b=2)
                            last = nc.tensor.matmul(o[:, :, c2 * CHUNK:(c2 + 1) * CHUNK], v, rhs,
                                                    start=True, stop=True)
                last.then_inc(pv_done, 1)

            def out_unit(U):
                j = U - UNITS
                g, t = U // T, U % T
                pe.wait_ge(mixa_ready, t + 1)
                pe.wait_ge(mixb_ready, t + 1)
                a = slice(t * P, (t + 1) * P)
                for part, done in ((0, wa_done), (1, wb_done)):
                    if j == 0:
                        pe.wait_ge(acc_free[part], UNITS // 2)
                    else:
                        pe.wait_ge((wa_free, x1_ready)[part], j)
                    for kk in range(4):
                        k = part * 4 + kk
                        if t == 0:
                            pe.wait_ge(w_ready, (g - 1) * K + k + 1)
                        r = (g * K + k) % RING
                        last = three(bank[part][:, :], actT_hi[:, k, a], actT_lo[:, k, a], w_hi[:, r, :],
                                     w_lo[:, r, :], kk == 0, kk == 3)
                    last.then_inc(done, 1)

            pe.wait_ge(par_s, 16 * 11)
            nc.tensor.transpose(bank[4][:, 0:G_ROWS], prow[:, :], ident[0:G_ROWS, 0:G_ROWS]).then_inc(cols_tp, 1)
            transpose_h(h_buf, 0, h_ready, h_tp, h_split)
            transpose_h(h_buf, 1, h_ready, h_tp, h_split)
            for U in range(ALL):
                g, t = U // T, U % T
                if U < UNITS:
                    unit(U)
                else:
                    out_unit(U)
                if U + 2 < T:
                    transpose_h(h_buf, U + 2, h_ready, h_tp, h_split)
                if U == 0:
                    pe.wait_ge(cols_ready, 1)
                if 1 <= U <= T:
                    mq_transposes(U - 1)
                if U == 2 * T + 2:
                    pe.wait_ge(kn_ready, 1)
                    for b in range(2):
                        for j in range(4):
                            last = nc.tensor.transpose(bank[2 + b][:, j * P:(j + 1) * P],
                                                       kvs[:, 4 * b + j, 2 * MH:2 * MH + KV * HD], ident[:, :])
                    last.then_inc(kT_tp, 1)
                    pe.wait_ge(gate_v, 2)
                    nc.tensor.matmul(bank[5][:, 0:32], tri[:, :], lf[:, :], start=True, stop=True)
                    nc.tensor.matmul(bank[5][:, 32:64], ones[:, :], lf[:, :], start=True,
                                     stop=True).then_inc(gate_mm, 1)
                if U == 2 * T + 3:
                    pe.wait_ge(gate_v, 3)
                    nc.tensor.transpose(bank[6][0:32, 0:P], u_col[:, :], ident[:, :]).then_inc(gate_mm, 1)
                if U == 2 * T + 4:
                    pe.wait_ge(gate_v, 4)
                    nc.tensor.matmul(bank[7][:, 0:32], ones[0:32, :], diag[:, :], start=True,
                                     stop=True).then_inc(gate_mm, 1)
                if U == 2 * T + 5:
                    pe.wait_ge(gate_v, 5)
                    nc.tensor.transpose(bank[6][:, 0:32], nM[:, :], ident[0:32, 0:32]).then_inc(gate_mm, 1)
                s = U - 3 * T
                if s == 0:
                    pe.wait_ge(gate_v, 6)
                    pe.wait_ge(qk_ready, 4)
                    pe.wait_ge(acc_free[1], 3 * T // 2)
                if 1 <= s <= T:
                    mlstm_products(s - 1)
                if 0 <= s < T:
                    mlstm_scores(s)
                s = U - 4 * T
                if 0 <= s - 5 < T:
                    att_sumsq(s - 5)
                if s == 1:
                    pe.wait_ge(c_ready, T + 1)
                    pe.wait_ge(mh_ready, T)
                if 0 <= s - 1 < T:
                    att_transposes(s - 1)
                if 0 <= s - 3 < T:
                    att_prob_transposes(s - 3)
                if 0 <= s - 2 < T:
                    att_scores(s - 2)
                if 0 <= s - 4 < T:
                    att_values(s - 4)
                s = U - 6 * T
                if s == 2:
                    pe.wait_ge(ssa_ready, T)
                if 0 <= s - 2:
                    transpose_h(h2buf, s - 2, h2_ready, h2_tp, h2_split)

            def strip(kind, half, count, w_count, split_done=None):
                a = slice(half * N, (half + 1) * N)
                for m, (b, free, done) in enumerate(((0, silu_done, gate_done), (1, prod_done, up_done))):
                    ps = bank[2 * half + b][:, :]
                    if free is not None and split_done is None:
                        pe.wait_ge(free, count - 1)
                    for k in range(K):
                        r = FFN_RING[kind] + 2 * m + k // 4
                        if half == 0 and k % 4 == 0:
                            pe.wait_ge(w_ready, w_count + 2 * m + k // 4 + 1)
                        c = slice((k % 4) * P, (k % 4 + 1) * P)
                        last = three(ps, w_hi[:, r, c], w_lo[:, r, c], actT_hi[:, k, a], actT_lo[:, k, a],
                                     k == 0, k == K - 1)
                    last.then_inc(done, 1)

            def down(count, w_count, ready):
                pe.wait_ge(act_ready, ready)
                for half in range(2):
                    for t in range(T):
                        m = half * T + t
                        ps = bank[4 + m % 4][:, :]
                        if m >= 4:
                            pe.wait_ge(down_add, count + m - 3)
                        a = slice(t * P, (t + 1) * P)
                        for j in range(2):
                            r = FFN_RING["down"] + 2 * half + j
                            if t == 0:
                                pe.wait_ge(w_ready, w_count + 2 * half + j + 1)
                            last = three(ps, act_hi[j][:, a], act_lo[j][:, a], w_hi[:, r, :], w_lo[:, r, :],
                                         j == 0, j == 1)
                        last.then_inc(down_mm, 1)

            pe.wait_ge(x1_ready, 2 * T)
            pe.wait_ge(h2_split, 8)
            strip("even", 0, 0, NS, split_done=True)
            transpose_h(h2buf, T - 2, h2_ready, h2_tp, h2_split)
            transpose_h(h2buf, T - 1, h2_ready, h2_tp, h2_split)
            pe.wait_ge(h2_split, 2 * T)
            strip("even", 1, 1, NS, split_done=True)
            for half in range(2):
                strip("odd", half, 2 + half, NS + 4)
            with pe.Fori(1, PAIRS) as i:
                w_count = NS + 8 + (i - 1) * 12
                for half in range(2):
                    strip("even", half, 4 * i + half, w_count)
                down((i - 1) * (2 * T) + 4 - 4, w_count + 4, 2 * i)
                for half in range(2):
                    strip("odd", half, 4 * i + 2 + half, w_count + 8)
            down(2 * T * (PAIRS - 1), NS + 8 + 12 * (PAIRS - 1), 2 * PAIRS)

        @block.scalar
        def _(act):
            steps = [0]

            def step(ins):
                steps[0] += 1
                ins.then_inc(act_step, 1)

            def link(ins):
                step(ins)
                act.wait_ge(act_step, steps[0])

            def settle():
                act.wait_ge(act_step, steps[0])

            def inverse_root(out_, sumsq, n):
                link(nc.scalar.activation(out_, sumsq, ACT.Ln, bias=eps_t[0:sumsq.shape[0], 0:1], scale=1.0 / n))
                return nc.scalar.activation(out_, out_, ACT.Exp, scale=-0.5)

            eps_t = cols[:, G_ROWS:G_ROWS + 1]

            def stats(t):
                act.wait_ge(x_in_s[t % 2], 16 * (t // 2 + 1))
                if t == 0:
                    act.wait_ge(gate_v, 1)
                link(nc.scalar.activation(junk[:, :], x_in[t % 2][:, :], ACT.Square, accum_out=stat[:, t:t + 1]))
                inverse_root(rstd[:, t:t + 1], stat[:, t:t + 1], D).then_inc(rstd_ready, 1)

            def high_part(t, tp, done):
                for b in range(2):
                    act.wait_ge(tp, 2 * t + b + 1)
                    nc.scalar.activation(actT_hi[:, 4 * b:4 * b + 4, t * P:(t + 1) * P],
                                         bank[2 + b][:, :].rearrange("p (k n) -> p k n", k=4),
                                         ACT.Copy).then_inc(done, 1)

            def w0_high(k):
                act.wait_ge(w0_s[k], 16)
                nc.scalar.activation(w_hi[:, k, :], w0_raw[:, k, :], ACT.Copy).then_inc(w0_hi, 1)

            stats(0)
            w0_high(0)
            w0_high(1)
            high_part(0, h_tp, h_hi)
            w0_high(2)
            w0_high(3)
            stats(1)
            w0_high(4)
            w0_high(5)
            high_part(1, h_tp, h_hi)
            w0_high(6)
            w0_high(7)

            def evacuate(U):
                g, t = U // T, U % T
                ps = bank[U % 2]
                act.wait_ge(unit_done, U + 1)
                free = acc_free[U % 2]
                if g == 0:
                    if t >= 2:
                        act.wait_ge(mq_tp, t - 1)
                    nc.scalar.activation(mqraw[t % 2][:, :], ps[:, :], ACT.Copy).then_inc(free, 1)
                elif g == 1:
                    nc.scalar.activation(kvs[:, t, :], ps[:, 0:NKV], ACT.Copy).then_inc(free, 1)
                elif g == 2:
                    if t == 0:
                        act.wait_ge(mq_tp, T)
                        act.wait_ge(h_tp, 2 * T)
                    nc.scalar.activation(mvx[:, t, :, 0:DV], ps[:, :].rearrange("p (h d) -> p h d", h=MH),
                                         ACT.Copy).then_inc(free, 1)
                elif g == 3:
                    if t == 0:
                        act.wait_ge(gate_v, 6)
                    if t >= 2:
                        act.wait_ge(h_done, t - 1)
                    nc.scalar.activation(sig[t % 2][:, :], ps[:, :], ACT.Exp, scale=-1.0).then_inc(free, 1)
                else:
                    if t == 0:
                        act.wait_ge(mh_ready, T)
                        act.wait_ge(cup_done, T)
                    if t >= 1:
                        act.wait_ge(q_stat, t)
                    step(nc.scalar.activation(pq[:, :], ps[:, :], ACT.Square))
                    if t >= 2:
                        act.wait_ge(qn_ready, t - 1)
                    nc.scalar.activation(aqs[t % 2][:, :], ps[:, :], ACT.Copy).then_inc(free, 1)

            for U in range(ALL):
                g, t = U // T, U % T
                if U + 2 < T:
                    stats(U + 2)
                if U < UNITS:
                    evacuate(U)
                if U + 2 < T:
                    high_part(U + 2, h_tp, h_hi)
                if T + 2 <= U < T + 6:
                    f = U - T - 2
                    act.wait_ge(conv_ready, f + 1)
                    nc.scalar.activation(qkT[:, f, :], qkT[:, f, :], ACT.Silu).then_inc(qk_ready, 1)
                if U == 2 * T + 1:
                    act.wait_ge(kv_stat, 1)
                    inverse_root(krs[:, :], kss[:, :], HD).then_inc(kv_rs, 1)
                    act.wait_ge(kv_stat, 2)
                    link(nc.scalar.activation(expf[:, :], absf[:, :], ACT.Exp, scale=-1.0))
                    nc.scalar.activation(expf[:, :], expf[:, :], ACT.Ln, bias=1.0).then_inc(gate_a, 1)
                if U == 2 * T + 5:
                    act.wait_ge(gate_v, 5)
                    step(nc.scalar.activation(aold[:, :], aold[:, :], ACT.Exp))
                    nc.scalar.activation(wexp[:, :], wexp[:, :], ACT.Exp).then_inc(gate_a, 1)
                if U == 2 * T + 6:
                    act.wait_ge(kv_stat, 3)
                    nc.scalar.activation(enm[:, :], enm[:, :], ACT.Exp).then_inc(gate_a, 1)
                s = U - 3 * T
                if 0 <= s < T:
                    act.wait_ge(bc_done, s + 1)
                    if s >= 1:
                        act.wait_ge(scd_ready, s)
                    for h in range(MH):
                        c = s * MH + h
                        last = nc.scalar.activation(dmat[:, h, :], bank[4][:, h * P:(h + 1) * P], ACT.Exp,
                                                    bias=u_col[:, c:c + 1])
                    last.then_inc(d_exp, 1)
                    for h in range(MH):
                        rows = slice((h % 2) * DK, (h % 2 + 1) * DK)
                        last = nc.scalar.activation(itr[rows, h // 2, :], bank[4][rows, h * P:(h + 1) * P],
                                                    ACT.Exp, bias=mm[rows, s, h:h + 1])
                    last.then_inc(it_exp, 1)
                if 1 <= s <= T:
                    act.wait_ge(mh_ready, s)
                    if s == 1:
                        act.wait_ge(it_exp, s)
                    nc.scalar.activation(msq[:, :], mhs[:, :], ACT.Square,
                                         accum_out=ss2[:, s - 1, 1:2]).then_inc(ssb_done, 1)
                    act.wait_ge(ssb_done, s)
                s = U - 4 * T
                if 0 <= s - 1 < T:
                    tt = s - 1
                    act.wait_ge(q_tp, tt + 1)
                    if tt >= 2:
                        act.wait_ge(s_odd, tt - 1)
                    nc.scalar.activation(qT[tt % 2][:, :, :], bank[2][:, :].rearrange("p (k n) -> p k n", k=4),
                                         ACT.Copy, scale=cols[:, G_Q:G_Q + 1]).then_inc(qT_ready, 1)
                    act.wait_ge(mh_tp, tt + 1)
                    nc.scalar.activation(actT_hi[:, 4:8, tt * P:(tt + 1) * P],
                                         bank[3][:, :].rearrange("p (k n) -> p k n", k=4),
                                         ACT.Copy).then_inc(mixb_hi, 1)
                if 0 <= s - 3 < T:
                    tt = s - 3
                    act.wait_ge(pt_done, tt + 1)
                    if tt >= 2:
                        act.wait_ge(pv_done, tt - 1)
                    nc.scalar.activation(pT[tt % 2][:, 0:4, :], bank[6][:, :].rearrange("p (k n) -> p k n", k=4),
                                         ACT.Copy).then_inc(pTa, 1)
                if 0 <= s - 2 < T:
                    tt = s - 2
                    act.wait_ge(s_max, tt + 1)
                    for j in range(8):
                        step(nc.scalar.activation(prob[:, j, :], prob[:, j, :], ACT.Exp, bias=nmx[:, j:j + 1],
                                                  accum_out=dsum[:, j:j + 1]))
                    nc.scalar.activation(esk[:, :], esk[:, :], ACT.Exp).then_inc(p_exp, 1)
                if 0 <= s - 4 < T:
                    tt = s - 4
                    act.wait_ge(pv_done, tt + 1)
                    if tt >= 1:
                        act.wait_ge(ssa_mm, tt)
                    nc.scalar.activation(sqb[:, :], bank[2][:, :], ACT.Square).then_inc(sqa_done, 1)
                    for kk in range(4):
                        last = nc.scalar.activation(actT_hi[:, kk, tt * P:(tt + 1) * P],
                                                    bank[2][:, kk * P:(kk + 1) * P], ACT.Copy,
                                                    scale=cols[:, G_ATT + kk:G_ATT + kk + 1])
                    last.then_inc(mixa_hi, 1)
                if 0 <= s < T:
                    act.wait_ge(q_stat, s + 1)
                    if s >= 1:
                        act.wait_ge(qn_ready, s)
                    inverse_root(qrs[:, :], qss[:, :], HD).then_inc(q_rs, 1)
                if 0 <= s - 6 < T:
                    tt = s - 6
                    act.wait_ge(ssa_ready, tt + 1)
                    inverse_root(rmix[:, tt, :], ss2[:, tt, :], N).then_inc(rmix_ready, 1)
                s = U - 6 * T
                if s >= 0:
                    act.wait_ge(x1_ready, T + s + 1)
                    if s == 0:
                        act.wait_ge(pv_done, T)
                    link(nc.scalar.activation(junk2[:, :], x1[:, s, :], ACT.Square, accum_out=stat[:, s:s + 1]))
                    inverse_root(rstd[:, s:s + 1], stat[:, s:s + 1], D).then_inc(r2_ready, 1)
                    if s >= 2:
                        high_part(s - 2, h2_tp, h2_hi)

            def silu_half(half, count):
                act.wait_ge(gate_done, count)
                act.wait_ge(prod_done, count - 2)
                nc.scalar.activation(silu[half][:, :], bank[2 * half][:, :], ACT.Silu).then_inc(silu_done, 1)

            def high_strip(j, prods, count):
                act.wait_ge(prod_done, prods)
                nc.scalar.activation(act_hi[j][:, :], prod[:, :], ACT.Copy).then_inc(act_hi_s, 1)

            act.wait_ge(mixa_ready, T)
            act.wait_ge(gate_done, 1)
            nc.scalar.activation(silu[0][:, :], bank[0][:, :], ACT.Silu).then_inc(silu_done, 1)
            high_part(T - 2, h2_tp, h2_hi)
            high_part(T - 1, h2_tp, h2_hi)
            act.wait_ge(gate_done, 2)
            nc.scalar.activation(silu[1][:, :], bank[2][:, :], ACT.Silu).then_inc(silu_done, 1)
            high_strip(0, 2, 1)
            silu_half(0, 3)
            silu_half(1, 4)
            high_strip(1, 4, 2)
            with act.Fori(1, PAIRS) as i:
                silu_half(0, 4 * i + 1)
                silu_half(1, 4 * i + 2)
                act.wait_ge(down_mm, 2 * T * i)
                high_strip(0, 4 * i + 2, 2 * i + 1)
                silu_half(0, 4 * i + 3)
                silu_half(1, 4 * i + 4)
                high_strip(1, 4 * i + 4, 2 * i + 2)

        @block.vector
        def _(dve):
            steps = [0]
            V_ = nc.vector

            def step(ins):
                steps[0] += 1
                ins.then_inc(dve_step, 1)

            def link(ins):
                step(ins)
                dve.wait_ge(dve_step, steps[0])

            def low_part(t, hi_s, done):
                for b in range(2):
                    dve.wait_ge(hi_s, 2 * t + b + 1)
                    V_.tensor_tensor(actT_lo[:, 4 * b:4 * b + 4, t * P:(t + 1) * P],
                                     bank[2 + b][:, :].rearrange("p (k n) -> p k n", k=4),
                                     actT_hi[:, 4 * b:4 * b + 4, t * P:(t + 1) * P].bitcast(F32),
                                     ALU.subtract).then_inc(done, 1)

            def normed(dst, src, t, r_s, tp, done):
                dve.wait_ge(r_s, t + 1)
                if t >= 2:
                    dve.wait_ge(tp, 2 * (t - 1))
                V_.scalar_tensor_tensor(dst[t % 2][:, :], src, rstd[:, t:t + 1], g_row[:, :],
                                        ALU.mult, ALU.mult).then_inc(done, 1)

            def w0_low(k):
                dve.wait_ge(w0_hi, k + 1)
                V_.tensor_tensor(w_lo[:, k, :], w0_raw[:, k, :], w_hi[:, k, :].bitcast(F32),
                                 ALU.subtract).then_inc(w0_ready, 1)

            V_.memset(cols[:, G_ROWS:G_ROWS + 1], EPS).then_inc(gate_v, 1)
            V_.memset(ones[:, :], 1.0).then_inc(ones_set, 1)
            step(V_.memset(rawT[:, :, 0:3], 0.0))
            link(V_.memset(mm[:, 0, :], 0.0))
            dve.wait_ge(par_s, 16 * 11)
            for i2 in range(2):
                rows = slice(i2 * CHUNK, (i2 + 1) * CHUNK)
                heads = sinks8[rows, :].rearrange("p (m i) -> p m i", i=2)[:, :, i2]
                link(V_.tensor_copy(sink_b[rows, :].rearrange("p (c m) -> p c m", c=2),
                                    heads.unsqueeze(1).to_broadcast([CHUNK, 2, 4])))
            normed(h_buf, x_in[0][:, :], 0, rstd_ready, h_tp, h_ready)
            w0_low(0)
            w0_low(1)
            low_part(0, h_hi, h_split)
            w0_low(2)
            w0_low(3)
            normed(h_buf, x_in[1][:, :], 1, rstd_ready, h_tp, h_ready)
            w0_low(4)
            w0_low(5)
            low_part(1, h_hi, h_split)
            w0_low(6)
            w0_low(7)
            dve.wait_ge(cols_tp, 1)
            link(V_.tensor_copy(cols[:, 0:G_ROWS], bank[4][:, 0:G_ROWS]))
            V_.tensor_scalar(cols[:, G_Q:G_Q + 1], cols[:, G_Q:G_Q + 1], HD ** -0.5, None,
                             ALU.mult).then_inc(cols_ready, 1)
            dve.wait_ge(cols_ready, 1)

            def convolution(f):
                y = qkT[:, f, :]
                link(V_.tensor_scalar(y, rawT[:, f, 0:S], cols[:, f:f + 1], None, ALU.mult))
                for i in range(1, TAPS):
                    ins = V_.scalar_tensor_tensor(y, rawT[:, f, i:i + S], cols[:, 4 * i + f:4 * i + f + 1], y,
                                                  ALU.mult, ALU.add)
                    if i < TAPS - 1:
                        link(ins)
                ins.then_inc(conv_ready, 1)

            kview = kvs[:, :, 2 * MH:2 * MH + KV * HD]
            vcols = slice(2 * MH + KV * HD, 2 * MH + 2 * KV * HD)
            tril32 = ident[0:32, 0:32]

            for U in range(ALL):
                g, t = U // T, U % T
                if U + 2 < T:
                    normed(h_buf, x_in[t % 2][:, :], U + 2, rstd_ready, h_tp, h_ready)
                if 1 <= U <= T:
                    dve.wait_ge(mq_tp, U)
                    V_.tensor_copy(rawT[:, :, 3 + (U - 1) * P:3 + U * P],
                                   bank[4][:, :].rearrange("p (k n) -> p k n", k=4)).then_inc(mq_evac, 1)
                if U + 2 < T:
                    low_part(U + 2, h_hi, h_split)
                if U == T + 1:
                    dve.wait_ge(mq_evac, T)
                    dve.wait_ge(h_tp, 2 * T)
                    step(V_.memset(mvx[:, :, :, DV:DV + 1], 1.0))
                if T + 1 <= U < T + 5:
                    convolution(U - T - 1)
                if U == 2 * T:
                    dve.wait_ge(acc_free[0], T)
                    dve.wait_ge(acc_free[1], T)
                    step(V_.memset(v_even[CHUNK:P, 0, :], 0.0))
                    step(V_.memset(kT[:, 0:CHUNK], 0.0))
                    step(V_.tensor_copy(v_even[0:CHUNK, :, :], kvs[0:CHUNK, :, vcols]))
                    step(V_.tensor_copy(v_even[CHUNK:P, 1:T, :], kvs[CHUNK:P, 0:T - 1, vcols]))
                    link(V_.tensor_tensor(ksq[:, :, :], kview, kview, ALU.mult))
                    V_.tensor_reduce(kss[:, :], ksq[:, :, :].rearrange("p t (g d) -> p (t g) d", g=KV),
                                     AX.X, ALU.add).then_inc(kv_stat, 1)
                    link(V_.tensor_tensor(gate8[:, :, :], kvs[:, :, 0:8],
                                          bias_g[:, :].unsqueeze(1).to_broadcast([P, T, 8]), ALU.add))
                    fpre = gate8[:, :, MH:2 * MH]
                    absf3 = absf[:, :].rearrange("p (t h) -> p t h", h=MH)
                    V_.scalar_tensor_tensor(absf3, fpre, -1.0, fpre, ALU.mult, ALU.max).then_inc(kv_stat, 1)
                if U == 2 * T + 1:
                    dve.wait_ge(kv_rs, 1)
                    for gg in range(KV):
                        kk_ = kvs[:, :, 2 * MH + gg * HD:2 * MH + (gg + 1) * HD]
                        ins = V_.tensor_tensor(kk_, kk_,
                                               bcast(krs[:, :].rearrange("p (t g) -> p t g", g=KV)[:, :, gg], HD),
                                               ALU.mult)
                        if gg == 0:
                            step(ins)
                    ins.then_inc(kn_ready, 1)
                    dve.wait_ge(gate_a, 1)
                    V_.scalar_tensor_tensor(lf[:, :].rearrange("p (t h) -> p t h", h=MH), fpre, 0.0,
                                            expf[:, :].rearrange("p (t h) -> p t h", h=MH),
                                            ALU.min, ALU.subtract).then_inc(gate_v, 1)
                if U == 2 * T + 2:
                    dve.wait_ge(kT_tp, 1)
                    for b in range(2):
                        step(V_.tensor_scalar(kT[:, CHUNK + b * N:CHUNK + (b + 1) * N], bank[2 + b][:, :],
                                              cols[:, G_K:G_K + 1], None, ALU.mult))
                    dve.wait_ge(gate_mm, 1)
                    link(V_.tensor_copy(bg[:, :], bank[5][:, 0:64]))
                    V_.tensor_tensor(u_col[:, :].rearrange("p (t h) -> p t h", h=MH), gate8[:, :, 0:MH],
                                     bg[:, 0:32].rearrange("p (t h) -> p t h", h=MH),
                                     ALU.subtract).then_inc(gate_v, 1)
                if U == 2 * T + 3:
                    dve.wait_ge(gate_mm, 2)
                    link(V_.tensor_copy(uT[:, :], bank[6][0:32, 0:P]))
                    link(V_.tensor_tensor_scan(cm[:, :], uT[:, :], uT[:, :], -3.0e38, ALU.max, ALU.max))
                    V_.tensor_scalar(diag[:, :], tril32, cm[:, P - 1:P], None, ALU.mult).then_inc(gate_v, 1)
                if U == 2 * T + 4:
                    dve.wait_ge(gate_mm, 3)
                    link(V_.tensor_copy(maxu_b[:, :], bank[7][:, 0:32]))
                    link(V_.tensor_tensor(gm[:, :], bg[:, 32:64], maxu_b[:, :], ALU.add))
                    tot = bg[:, 32:64].rearrange("p (t h) -> p t h", h=MH)
                    gm3 = gm[:, :].rearrange("p (t h) -> p t h", h=MH)
                    for h in range(MH):
                        ins = V_.tensor_tensor_scan(mm[:, 1:T + 1, h], tot[:, :, h], gm3[:, :, h], 0.0,
                                                    ALU.add, ALU.max)
                        step(ins)
                    dve.wait_ge(dve_step, steps[0])
                    mprev = mm[:, 0:T, :].rearrange("p t h -> p (t h)")
                    link(V_.tensor_tensor(mlast[:, :], mprev, maxu_b[:, :], ALU.max))
                    step(V_.tensor_tensor(aold[:, :], mprev, mlast[:, :], ALU.subtract))
                    step(V_.tensor_tensor(wexp[:, :], u_col[:, :], mlast[:, :], ALU.subtract))
                    link(V_.tensor_tensor(diag[:, :], mm[0:32, 0:T, :].rearrange("p t h -> p (t h)"), tril32,
                                          ALU.mult))
                    link(V_.tensor_reduce(mcol[:, :], diag[:, :], AX.X, ALU.add))
                    V_.tensor_scalar(nM[:, :], cm[:, :], mcol[:, 0:1], -1.0, ALU.max, ALU.mult).then_inc(gate_v, 1)
                if U == 2 * T + 5:
                    dve.wait_ge(gate_a, 2)
                    step(V_.tensor_scalar(wexp[:, :], wexp[:, :], DK ** -0.5, None, ALU.mult))
                    a4 = aold[:, :].rearrange("p (t a b) -> p t a b", a=2, b=2)
                    step(V_.tensor_copy(aold2[0:DK, :, :], a4[0:DK, :, :, 0]))
                    step(V_.tensor_copy(aold2[DK:P, :, :], a4[DK:P, :, :, 1]))
                    dve.wait_ge(gate_mm, 4)
                    V_.tensor_tensor(enm[:, :], bank[6][:, 0:32], bg[:, 0:32], ALU.subtract).then_inc(kv_stat, 1)
                    step(V_.memset(cst[:, :, :], 0.0))
                    dve.wait_ge(dve_step, steps[0])
                    V_.memset(den4[:, :], 0.0).then_inc(c_ready, 1)
                    dve.wait_ge(c_ready, 1)
                    dve.wait_ge(kv_stat, 3)
                    V_.memset(den4[:, :], 0.0).then_inc(gate_v, 1)
                s = U - 3 * T
                if 1 <= s <= T:
                    tt = s - 1
                    dve.wait_ge(cup_done, tt + 1)
                    step(V_.scalar_tensor_tensor(cst[:, 0, :], cst[:, 0, :], aold2[:, tt, 0:1],
                                                 bank[3][:, 0:DV + 1], ALU.mult, ALU.add))
                    V_.scalar_tensor_tensor(cst[:, 1, :], cst[:, 1, :], aold2[:, tt, 1:2],
                                            bank[3][:, DV + 1:2 * (DV + 1)], ALU.mult,
                                            ALU.add).then_inc(c_ready, 1)
                    if tt == 0:
                        dve.wait_ge(gate_a, 3)
                    for p in range(2):
                        step(V_.tensor_copy(
                            den4[:, :].rearrange("p (a b) -> p b a", b=2)[:, p, :],
                            bank[6 + p][:, 0:2 * (DV + 1)].rearrange("p (h d) -> p h d", h=2)[:, :, DV]))
                    dve.wait_ge(dve_step, steps[0])
                    link(V_.scalar_tensor_tensor(den4[:, :], den4[:, :], -1.0, den4[:, :], ALU.mult, ALU.max))
                    link(V_.tensor_tensor(den4[:, :], den4[:, :], enm[:, tt * MH:(tt + 1) * MH], ALU.max))
                    link(V_.reciprocal(den4[:, :], den4[:, :]))
                    if tt >= 1:
                        dve.wait_ge(ssb_done, tt)
                    for h in range(MH):
                        ins = V_.scalar_tensor_tensor(
                            mhs[:, h * DV:(h + 1) * DV],
                            bank[6 + h % 2][:, (h // 2) * (DV + 1):(h // 2) * (DV + 1) + DV],
                            den4[:, h:h + 1], sig[tt % 2][:, h * DV:(h + 1) * DV], ALU.mult, ALU.mult)
                        if h < MH - 1:
                            step(ins)
                    ins.then_inc(h_done, 1)
                    dve.wait_ge(h_done, tt + 1)
                    if tt == 0:
                        dve.wait_ge(late_s, 16)
                    V_.tensor_tensor(mh[:, tt, :], mhs[:, :], g_row[:, 0:MH * DV], ALU.mult).then_inc(mh_ready, 1)
                if 0 <= s < T:
                    dve.wait_ge(kt_done, s + 1)
                    V_.tensor_tensor(kw[:, :, :], bank[2][:, 0:MH * DK].rearrange("p (h d) -> p h d", h=MH),
                                     bcast(wexp[:, s * MH:(s + 1) * MH], DK), ALU.mult).then_inc(kw_ready, 1)
                    dve.wait_ge(it_exp, s + 1)
                    step(V_.tensor_tensor(qi[:, :, :], qkT[:, 0:2, s * P:(s + 1) * P], itr[:, :, :], ALU.mult))
                    dve.wait_ge(d_masked, s + 1)
                    dve.wait_ge(sc_done, s + 1)
                    V_.scalar_tensor_tensor(scd[:, :, :].rearrange("p h n -> p (h n)"), bank[5][:, :], DK ** -0.5,
                                            dmat[:, :, :].rearrange("p h n -> p (h n)"), ALU.mult,
                                            ALU.mult).then_inc(scd_ready, 1)
                    dve.wait_ge(acc_free[U % 2], U // 2 + 1)
                    link(V_.tensor_scalar(sig[s % 2][:, :], sig[s % 2][:, :], 1.0, None, ALU.add))
                    link(V_.reciprocal(sig[s % 2][:, :], sig[s % 2][:, :]))
                s = U - 4 * T
                if 0 <= s - 5 < T:
                    tt = s - 5
                    dve.wait_ge(ssa_mm, tt + 1)
                    V_.tensor_copy(ss2[:, tt, 0:1], bank[3][:, 0:1]).then_inc(ssa_ready, 1)
                if 0 <= s < T:
                    dve.wait_ge(acc_free[U % 2], U // 2 + 1)
                    if s >= 1:
                        dve.wait_ge(q_rs, s)
                    V_.tensor_reduce(qss[:, :], pq[:, :].rearrange("p (h d) -> p h d", h=HEADS), AX.X,
                                     ALU.add).then_inc(q_stat, 1)
                if 0 <= s - 1 < T:
                    tt = s - 1
                    dve.wait_ge(mixb_hi, tt + 1)
                    V_.tensor_tensor(actT_lo[:, 4:8, tt * P:(tt + 1) * P],
                                     bank[3][:, :].rearrange("p (k n) -> p k n", k=4),
                                     actT_hi[:, 4:8, tt * P:(tt + 1) * P].bitcast(F32),
                                     ALU.subtract).then_inc(mixb_ready, 1)
                if 0 <= s - 3 < T:
                    tt = s - 3
                    dve.wait_ge(pt_done, tt + 1)
                    if tt >= 2:
                        dve.wait_ge(pv_done, tt - 1)
                    V_.tensor_copy(pT[tt % 2][:, 4:8, :],
                                   bank[7][:, :].rearrange("p (k n) -> p k n", k=4)).then_inc(pTd, 1)
                if 0 <= s - 2 < T:
                    tt = s - 2
                    dve.wait_ge(s_even, tt + 1)
                    if tt == 0:
                        dve.wait_ge(late_s, 16 * 4)
                    if tt >= 1:
                        dve.wait_ge(pt_done, tt)
                    which = 2 if tt == 0 else 0
                    step(V_.tensor_tensor(prob[:, 0:4, :], bank[4][:, :].rearrange("p (k n) -> p k n", k=4),
                                          bias[:, which, :].rearrange("p (k n) -> p k n", k=4), ALU.add))
                    dve.wait_ge(s_odd, tt + 1)
                    V_.tensor_tensor(prob[:, 4:8, :], bank[5][:, :].rearrange("p (k n) -> p k n", k=4),
                                     bias[:, 1, :].rearrange("p (k n) -> p k n", k=4),
                                     ALU.add).then_inc(s_evac, 1)
                    dve.wait_ge(s_evac, tt + 1)
                    link(V_.tensor_reduce(smx[:, :], prob[:, :, :], AX.X, ALU.max))
                    link(V_.tensor_tensor(smx[:, :], smx[:, :], sink_b[:, :], ALU.max))
                    link(V_.tensor_scalar(nmx[:, :], smx[:, :], -1.0, None, ALU.mult))
                    V_.tensor_tensor(esk[:, :], sink_b[:, :], nmx[:, :], ALU.add).then_inc(s_max, 1)
                    dve.wait_ge(p_exp, tt + 1)
                    link(V_.tensor_tensor(dsum[:, :], dsum[:, :], esk[:, :], ALU.add))
                    link(V_.reciprocal(dsum[:, :], dsum[:, :]))
                    V_.tensor_tensor(prob[:, :, :], prob[:, :, :], bcast(dsum[:, :], P),
                                     ALU.mult).then_inc(p_ready, 1)
                if 0 <= s - 4 < T:
                    tt = s - 4
                    dve.wait_ge(mixa_hi, tt + 1)
                    for kk in range(4):
                        ins = V_.scalar_tensor_tensor(
                            actT_lo[:, kk, tt * P:(tt + 1) * P], bank[2][:, kk * P:(kk + 1) * P],
                            cols[:, G_ATT + kk:G_ATT + kk + 1],
                            actT_hi[:, kk, tt * P:(tt + 1) * P].bitcast(F32), ALU.mult, ALU.subtract)
                        if kk < 3:
                            step(ins)
                    ins.then_inc(mixa_ready, 1)
                if 0 <= s < T:
                    dve.wait_ge(q_rs, s + 1)
                    if s >= 1:
                        dve.wait_ge(q_tp, s)
                    V_.tensor_tensor(qn[:, :, :, :].rearrange("p i g d -> p g i d"),
                                     aqs[s % 2][:, :].rearrange("p (g i d) -> p g i d", g=KV, i=4),
                                     bcast(qrs[:, :].rearrange("p (g i) -> p g i", g=KV), HD),
                                     ALU.mult).then_inc(qn_ready, 1)
                if U >= UNITS:
                    j = U - UNITS
                    dve.wait_ge(wa_done, j + 1)
                    if j < T:
                        dve.wait_ge(rmix_ready, t + 1)
                        if t == 0:
                            dve.wait_ge(x1_s[0], 16 * 4)
                        if t == 4:
                            dve.wait_ge(x1_s[1], 16 * (T - 4))
                    xs = x1[:, t, (j // T) * N:(j // T + 1) * N]
                    V_.scalar_tensor_tensor(xs, bank[0][:, :], rmix[:, t, 0:1], xs, ALU.mult,
                                            ALU.add).then_inc(wa_free, 1)
                    dve.wait_ge(wa_free, j + 1)
                    dve.wait_ge(wb_done, j + 1)
                    V_.scalar_tensor_tensor(xs, bank[1][:, :], rmix[:, t, 1:2], xs, ALU.mult,
                                            ALU.add).then_inc(x1_ready, 1)
                s = U - 6 * T
                if s == 1:
                    dve.wait_ge(gf_s, 16)
                if s >= 1:
                    normed(h2buf, x1[:, s - 1, :], s - 1, r2_ready, h2_tp, h2_ready)
                if s >= 2:
                    low_part(s - 2, h2_hi, h2_split)

            normed(h2buf, x1[:, T - 1, :], T - 1, r2_ready, h2_tp, h2_ready)
            low_part(T - 2, h2_hi, h2_split)
            low_part(T - 1, h2_hi, h2_split)

            def product_half(half, count, his):
                dve.wait_ge(silu_done, count)
                dve.wait_ge(up_done, count)
                if his is not None:
                    dve.wait_ge(act_ready, his)
                V_.tensor_tensor(prod[:, half * N:(half + 1) * N], bank[2 * half + 1][:, :], silu[half][:, :],
                                 ALU.mult).then_inc(prod_done, 1)

            def low_strip(j, count):
                dve.wait_ge(act_hi_s, count)
                V_.tensor_tensor(act_lo[j][:, :], prod[:, :], act_hi[j][:, :].bitcast(F32),
                                 ALU.subtract).then_inc(act_ready, 1)

            def add_down(count):
                for half in range(2):
                    for t in range(T):
                        m = half * T + t
                        dve.wait_ge(down_mm, count + m + 1)
                        xs = x1[:, t, half * N:(half + 1) * N]
                        V_.tensor_tensor(xs, bank[4 + m % 4][:, :], xs, ALU.add).then_inc(down_add, 1)

            product_half(0, 1, None)
            product_half(1, 2, None)
            low_strip(0, 1)
            product_half(0, 3, 1)
            product_half(1, 4, 1)
            low_strip(1, 2)
            with dve.Fori(1, PAIRS) as i:
                product_half(0, 4 * i + 1, 2 * i)
                product_half(1, 4 * i + 2, 2 * i)
                add_down((i - 1) * (2 * T))
                low_strip(0, 2 * i + 1)
                product_half(0, 4 * i + 3, 2 * i + 1)
                product_half(1, 4 * i + 4, 2 * i + 1)
                low_strip(1, 2 * i + 2)
            dve.wait_ge(act_ready, 2 * PAIRS)
            add_down(2 * T * (PAIRS - 1))


NAMES = ["x", "g_mix", "w_in", "b_gates", "conv_qk", "q_norm_gain", "k_norm_gain", "attn_sinks",
         "g_attn_out", "g_mlstm_out", "w_out", "g_ffn", "w_gate", "w_up", "w_down"]


def kernel(**inputs):
    import concourse.bacc as bacc
    from concourse.bass_utils import run_bass_kernel_spmd

    nc = bacc.Bacc("TRN2", target_bir_lowering=False, num_devices=1, dynamic_dma_scratch_size=1024)
    arrays, args = {}, []
    for name in NAMES:
        a = np.ascontiguousarray(inputs[name])
        arrays[f"in_{name}"] = a
        args.append(nc.dram_tensor(f"in_{name}", a.shape, mybir.dt.from_np(a.dtype), kind="ExternalInput").ap())
    arrays["consts"] = constants()
    args.append(nc.dram_tensor("consts", arrays["consts"].shape, F32, kind="ExternalInput").ap())
    out = nc.dram_tensor("out", inputs["x"].shape, F32, kind="ExternalOutput").ap()
    hymba_block(nc, *args, out)
    r = run_bass_kernel_spmd(nc, [arrays], core_ids=[0])
    return r.results[0]["out"]
```

```python
from contextlib import ExitStack

import numpy as np

import concourse.bass as bass
from concourse import mybir

ALU = mybir.AluOpType
ACT = mybir.ActivationFunctionType
AX = mybir.AxisListType
F32 = mybir.dt.float32
F32R = mybir.dt.float32r

P = 128
CHUNK = 64
HEADS = 8
KV = 2
HD = 64
MH = 4
DK = 64
DV = 128
TAPS = 4
EPS = 1e-6
NEG = -1.0e30

C_ID, C_TRI, C_BIAS, C_FIRST, C_END = 0, 128, 256, 768, 1280
G_CONV, G_ATT, G_K, G_Q, G_ROWS = 0, 16, 20, 21, 22


def constants():
    c = np.zeros((P, C_END), np.float32)
    c[:, C_ID:C_ID + P] = np.eye(P)
    c[:, C_TRI:C_TRI + P] = np.triu(np.ones((P, P)))
    row = np.arange(P)
    q, i2 = row % CHUNK, row // CHUNK
    key = np.arange(P)
    dist = np.abs(q[:, None] + CHUNK - key[None, :])
    for kv in range(KV):
        for b in range(2):
            slope = 2.0 ** -(kv * 4 + b * 2 + i2 + 1.0)
            blk = -slope[:, None] * dist
            a = (kv * 2 + b) * P
            c[:, C_BIAS + a:C_BIAS + a + P] = blk
            c[:, C_FIRST + a:C_FIRST + a + P] = np.where(key[None, :] < CHUNK, NEG, blk)
    return c


def hymba_block(nc, x, g_mix, w_in, b_gates, conv_qk, q_gain, k_gain, sinks,
                g_att, g_ml, w_out, g_ffn, w_gate, w_up, w_down, consts, out):
    S, D = x.shape[1], x.shape[2]
    DFF = w_gate.shape[2]
    T = S // P
    K = D // P
    N = 512
    F = DFF // P
    PAIRS = F // 2
    AQ, AK = 0, HEADS * HD
    MQ = AK + 2 * KV * HD
    MV = MQ + 2 * MH * DK
    MO = MV + MH * DV
    GATES = MO + MH * DV
    NKV = 2 * MH + 2 * KV * HD
    RING, RAW = 16, 2
    GROUPS = 7
    UNITS = 5 * T
    ALL = GROUPS * T
    assert T == 8 and K == 8 and F % 2 == 0 and MQ + 512 == MV

    x_t = x.rearrange("a (t p) d -> t p (a d)", p=P)
    out_t = out.rearrange("a (t p) d -> t p (a d)", p=P)
    w_in_k = w_in.rearrange("a (k p) n -> k p (a n)", p=P)
    w_out_k = w_out.rearrange("a (k p) n -> k p (a n)", p=P)
    w_gate_k = w_gate.rearrange("a (k p) n -> p (a k) n", p=P)
    w_up_k = w_up.rearrange("a (k p) n -> p (a k) n", p=P)
    w_down_r = w_down.rearrange("a f n -> (a f) n")

    ctx = ExitStack()
    with ctx:
        base = [(nc.sbuf_base + 31) // 32 * 32]

        def place(name, shape, dt=F32, at=None):
            size = 4 * int(np.prod(shape[1:]))
            start = base[0] if at is None else at
            assert start + size <= nc.sbuf_usable_end, (name, start + size - nc.sbuf_usable_end)
            t = nc.alloc_sbuf_tensor_at(name, list(shape), dt, offset=start)
            end = (start + size + 31) // 32 * 32
            if at is None:
                base[0] = end
            return t, end

        def sem(name):
            return ctx.enter_context(nc.semaphore(name))

        actT_hi, _ = place("actT_hi", [P, K, S], F32R)
        actT_lo, _ = place("actT_lo", [P, K, S], F32R)
        w_hi, _ = place("w_hi", [P, RING, N], F32R)
        w_lo, _ = place("w_lo", [P, RING, N], F32R)
        w_raw, _ = place("w_raw", [P, RAW, N])
        ident, _ = place("ident", [P, P])
        tri, _ = place("tri", [P, P])
        ones, _ = place("ones", [P, P])
        cols, _ = place("cols", [P, G_ROWS + 2])
        bias_g, _ = place("bias_g", [P, 8])
        sinks8, _ = place("sinks8", [P, 8])
        sink_b, _ = place("sink_b", [P, 8])
        g_row, _ = place("g_row", [P, D])
        stat, _ = place("stat", [P, T])
        rstd, _ = place("rstd", [P, T])
        ss2, _ = place("ss2", [P, T, 2])
        rmix, _ = place("rmix", [P, T, 2])
        gate8, _ = place("gate8", [P, T, 8])
        small = {}
        for name in ("absf", "expf", "lf", "u", "mlast", "aold", "wexp", "enm", "maxu_b"):
            small[name], _ = place(name, [P, T * MH])
        absf, expf, lf, u_col = small["absf"], small["expf"], small["lf"], small["u"]
        mlast, aold, wexp, enm = small["mlast"], small["aold"], small["wexp"], small["enm"]
        gm, maxu_b = absf, small["maxu_b"]
        bg, _ = place("bg", [P, 2 * T * MH])
        mm, _ = place("mm", [P, T + 1, MH])
        aold2, _ = place("aold2", [P, T, 2])
        den4, _ = place("den4", [P, MH])
        smx, _ = place("smx", [P, 8])
        nmx, _ = place("nmx", [P, 8])
        dsum, _ = place("dsum", [P, 8])
        esk, _ = place("esk", [P, 8])
        qss, _ = place("qss", [P, 8])
        qrs, _ = place("qrs", [P, 8])
        kss, _ = place("kss", [P, 2 * T])
        krs, _ = place("krs", [P, 2 * T])

        J = base[0]
        w0_raw, j_end = place("w0_raw", [P, K, N], at=J)
        ksq, _ = place("ksq", [P, T, P], at=J)
        cm, e = place("cm", [32, P], at=J + 4096)
        uT, e = place("uT", [32, P], at=e)
        nM, e = place("nM", [32, P], at=e)
        diag, e = place("diag", [32, 32], at=e)
        mcol, e = place("mcol", [32, 1], at=e)
        mwork = e
        dmat, e = place("dmat", [P, MH, P], at=mwork)
        scd, e = place("scd", [P, MH, P], at=e)
        itr, e = place("itr", [P, 2, P], at=e)
        kw, e = place("kw", [P, MH, DK], at=e)
        qi, e = place("qi", [P, 2, P], at=e)
        cst, e = place("cst", [P, 2, DV + 1], at=e)
        msq, e = place("msq", [P, MH * DV], at=e)
        sig0, _ = place("sig0", [P, N], at=J)
        sig1, _ = place("sig1", [P, N], at=J + 2048)
        sig = [sig0, sig1]
        assert e <= j_end, (e, j_end)
        G = j_end
        rawT, g_end = place("rawT", [P, 4, 3 + S], at=G)
        mh, _ = place("mh", [P, T, MH * DV], at=G)
        x1, _ = place("x1", [P, T, D], at=J)
        assert J + 4 * T * D <= g_end
        V = g_end
        kvs, e = place("kvs", [P, T, NKV], at=V)
        v_prev, e = place("v_prev", [P, T, KV * HD], at=e)
        kT, v_end = place("kT", [P, CHUNK + S], at=e)
        h2buf0, e = place("h2buf0", [P, D], at=V)
        h2buf1, e = place("h2buf1", [P, D], at=e)
        junk2, e = place("junk2", [P, D], at=e)
        h2buf = [h2buf0, h2buf1]
        assert e <= v_end
        E = v_end
        x_in0, e = place("x_in0", [P, D], at=E)
        x_in1, e = place("x_in1", [P, D], at=e)
        h_buf0, e = place("h_buf0", [P, D], at=e)
        h_buf1, e = place("h_buf1", [P, D], at=e)
        junk, e = place("junk", [P, D], at=e)
        mqraw0, e = place("mqraw0", [P, N], at=e)
        mqraw1, e = place("mqraw1", [P, N], at=e)
        prow, e = place("prow", [G_ROWS, P], at=e)
        x_in, h_buf, mqraw = [x_in0, x_in1], [h_buf0, h_buf1], [mqraw0, mqraw1]
        qkT, e = place("qkT", [P, 4, S], at=E)
        mvx, e = place("mvx", [P, T, MH, DV + 1], at=e)
        mhs, e = place("mhs", [P, MH * DV], at=e)
        bias, e = place("bias", [P, 2, N], at=E)
        qT0, e = place("qT0", [P, 4, P], at=e)
        qT1, e = place("qT1", [P, 4, P], at=e)
        prob0, e = place("prob0", [P, 8, P], at=e)
        prob1, e = place("prob1", [P, 8, P], at=e)
        pT0, e = place("pT0", [P, 8, P], at=e)
        aq0, e = place("aq0", [P, N], at=e)
        aq1, e = place("aq1", [P, N], at=e)
        qn, e = place("qn", [P, 4, KV, HD], at=e)
        sqb, e = place("sqb", [P, N], at=e)
        pq, e = place("pq", [P, N], at=e)
        pT1, e = place("pT1", [P, 8, P], at=e)
        qT, prob, pT, aqs = [qT0, qT1], [prob0, prob1], [pT0, pT1], [aq0, aq1]
        act_hi = [None, None]
        act_lo = [None, None]
        act_hi[0], e = place("act_hi0", [P, S], F32R, at=E)
        act_lo[0], e = place("act_lo0", [P, S], F32R, at=e)
        act_hi[1], e = place("act_hi1", [P, S], F32R, at=e)
        act_lo[1], e = place("act_lo1", [P, S], F32R, at=e)
        prod, e = place("prod", [P, S], at=e)
        silu0, e = place("silu0", [P, N], at=e)
        silu1, e = place("silu1", [P, N], at=e)
        silu = [silu0, silu1]

        bank = [ctx.enter_context(nc.psum_tensor(f"bank{i}", [P, N], F32)) for i in range(8)]

        x_in_s = [sem("x_loaded0"), sem("x_loaded1")]
        ident_s = sem("ident_loaded")
        gmix_s = sem("g_mix_loaded")
        par_s = sem("params_loaded")
        late_s = sem("late_params_loaded")
        raw_s = [sem(f"raw_loaded{i}") for i in range(RAW)]
        w0_s = [sem(f"w0_loaded{i}") for i in range(K)]
        x1_s = [sem(f"x1_loaded{i}") for i in range(2)]
        gf_s = sem("g_ffn_loaded")
        out_s = sem("out_stored")
        ones_set = sem("ones_set")
        w0_hi = sem("w0_hi")
        w0_even = sem("w0_even_split")
        w0_odd = sem("w0_odd_split")
        w_hi_s = sem("w_hi_done")
        w_ready = sem("w_ready")
        unit_done = sem("unit_done")
        acc_free = [sem("acc_free0"), sem("acc_free1")]
        dve_step = sem("dve_step")
        act_step = sem("act_step")
        pe_step = sem("pe_step")
        rstd_ready = sem("rstd_ready")
        h_ready = sem("h_ready")
        h_tp = sem("h_transposed")
        h_hi = sem("h_hi")
        h_split = sem("h_split")
        cols_tp = sem("cols_transposed")
        cols_ready = sem("cols_ready")
        mq_tp = sem("mq_transposed")
        mq_evac = sem("mq_evac")
        conv_ready = sem("conv_ready")
        qk_ready = sem("qk_ready")
        kv_stat = sem("kv_stat")
        kv_rs = sem("kv_rs")
        kn_ready = sem("kn_ready")
        gate_mm = sem("gate_mm")
        kT_tp = sem("kT_transposed")
        gate_v = sem("gate_v")
        gate_a = sem("gate_a")
        bc_done = sem("bc_done")
        sc_done = sem("sc_done")
        kt_done = sem("kt_done")
        d_exp = sem("d_exp")
        it_exp = sem("it_exp")
        d_masked = sem("d_masked")
        kw_ready = sem("kw_ready")
        scd_ready = sem("scd_ready")
        num_done = sem("num_done")
        cup_done = sem("cup_done")
        c_ready = sem("c_ready")
        h_done = sem("mlstm_h_done")
        sig_ready = sem("sig_ready")
        mh_ready = sem("mh_ready")
        ssb_done = sem("ssb_done")
        aq_ready = sem("aq_ready")
        q_stat = sem("q_stat")
        q_rs = sem("q_rs")
        qn_ready = sem("qn_ready")
        q_tp = sem("q_transposed")
        mh_tp = sem("mh_transposed")
        qT_ready = sem("qT_ready")
        mixb_hi = sem("mixb_hi")
        mixb_ready = sem("mixb_ready")
        s_kv0 = sem("scores_kv0")
        s_kv1 = sem("scores_kv1")
        s_evac = sem("scores_evac")
        s_max = sem("scores_max")
        p_exp = sem("p_exp")
        p_inv = sem("p_inverse_sum")
        p_ready = sem("p_ready")
        pt_done = sem("p_transposed")
        pTa = sem("pT_act")
        pTd = sem("pT_dve")
        pv_done = sem("pv_done")
        v_zero = sem("v_zero")
        v_moved = sem("v_moved")
        sqa_done = sem("sqa_done")
        mixa_hi = sem("mixa_hi")
        mixa_ready = sem("mixa_ready")
        ssa_mm = sem("ssa_mm")
        ssa_ready = sem("ssa_ready")
        rmix_ready = sem("rmix_ready")
        wa_done = sem("wa_done")
        wb_done = sem("wb_done")
        wa_free = sem("wa_free")
        x1_ready = sem("x1_ready")
        r2_ready = sem("r2_ready")
        h2_ready = sem("h2_ready")
        h2_tp = sem("h2_transposed")
        h2_hi = sem("h2_hi")
        h2_split = sem("h2_split")
        gate_done = sem("gate_done")
        up_done = sem("up_done")
        silu_done = sem("silu_done")
        prod_done = sem("prod_done")
        act_hi_s = sem("act_hi_done")
        act_ready = sem("act_ready")
        down_mm = sem("down_mm")
        down_add = sem("down_add")

        def slice_source(n):
            g, k = 1 + n // K, n % K
            if g == 1:
                return [((0, 8), w_in_k[k, :, GATES:GATES + 8]),
                        ((8, NKV), w_in_k[k, :, AK:AK + 2 * KV * HD])]
            if g < 5:
                c = {2: MV, 3: MO, 4: AQ}[g]
                return [((0, N), w_in_k[k, :, c:c + N])]
            return [((0, N), w_out_k[k, :, (g - 5) * N:(g - 4) * N])]

        NS = 6 * K

        def raw_count(n):
            return sum(16 * len(slice_source(m)) for m in range(n % RAW, n + 1, RAW))

        SILU_AT = (T + 4, T + 6, 2 * T, 2 * T + 1)
        PARAMS = 9
        RAW_BASE = [raw_count(NS - RAW + r) for r in range(RAW)]
        FFN_RING = {"even": 8, "odd": 12, "down": 0}

        def strip_pieces(f, s):
            w = w_gate_k if s < 2 else w_up_k
            return w[:, 4 * (s % 2):4 * (s % 2) + 4, bass.ds(f * P, P)]

        def down_piece(f, half):
            return w_down_r[bass.ds(f * P, P), half * N:(half + 1) * N]

        def bcast(ap, n):
            return ap.unsqueeze(len(ap.shape)).to_broadcast(list(ap.shape) + [n])

        block = ctx.enter_context(nc.Block())

        @block.sync
        def _(sp):
            def load_x(t):
                if t >= 2:
                    sp.wait_ge(h_ready, t - 1)
                sp.dma_start(x_in[t % 2][:, :], x_t[t]).then_inc(x_in_s[t % 2], 16)

            load_x(0)
            sp.dma_start(ident[:, :], consts[:, C_ID:C_ID + P]).then_inc(ident_s, 16)
            sp.dma_start(g_row[:, :], g_mix[0:1, :].to_broadcast([P, D])).then_inc(gmix_s, 16)
            for k in range(K):
                sp.dma_start(w0_raw[:, k, :], w_in_k[k, :, MQ:MQ + N]).then_inc(w0_s[k], 16)
                if k == 1:
                    load_x(1)
            sp.dma_start(tri[:, :], consts[:, C_TRI:C_TRI + P]).then_inc(par_s, 16)
            sp.dma_start(prow[G_CONV:G_CONV + 16, :],
                         conv_qk.rearrange("a i (f p) -> (a i f) p", p=P)).then_inc(par_s, 16)
            sp.dma_start(prow[G_ATT:G_ATT + 4, :], g_att.rearrange("a (k p) -> (a k) p", p=P)).then_inc(par_s, 16)
            for half in range(2):
                sp.dma_start(prow[G_K:G_K + 1, half * HD:(half + 1) * HD], k_gain).then_inc(par_s, 16)
                sp.dma_start(prow[G_Q:G_Q + 1, half * HD:(half + 1) * HD], q_gain).then_inc(par_s, 16)
            sp.dma_start(bias_g[:, :], b_gates[0:1, :].to_broadcast([P, 8])).then_inc(par_s, 16)
            sp.dma_start(sinks8[:, :], sinks[0:1, :].to_broadcast([P, 8])).then_inc(par_s, 16)

            xt = 2
            for n in range(NS):
                if n >= RAW:
                    sp.wait_ge(w_ready, n - RAW + 1)
                for (a, b), src in slice_source(n):
                    sp.dma_start(w_raw[:, n % RAW, a:b], src).then_inc(raw_s[n % RAW], 16)
                if xt < T:
                    load_x(xt)
                    xt += 1
                if n == 2 * K + 4:
                    sp.wait_ge(h_ready, T)
                    sp.dma_start(g_row[:, 0:MH * DV], g_ml[0:1, :].to_broadcast([P, MH * DV])).then_inc(late_s, 16)
                if n == 4 * K + 4:
                    sp.wait_ge(mh_ready, T)
                    sp.wait_ge(cup_done, T)
                    for i, c in enumerate((C_FIRST, C_BIAS)):
                        sp.dma_start(bias[:, i, :], consts[:, c:c + N]).then_inc(late_s, 16)
                    sp.wait_ge(ssb_done, T)
                    for t in range(4):
                        sp.dma_start(x1[:, t, :], x_t[t]).then_inc(x1_s[0], 16)
                    sp.dma_start(g_row[:, :], g_ffn[0:1, :].to_broadcast([P, D])).then_inc(gf_s, 16)
            sp.wait_ge(mh_tp, T)
            for t in range(4, T):
                sp.dma_start(x1[:, t, :], x_t[t]).then_inc(x1_s[1], 16)

            def ffn_load(source, m, count):
                sp.wait_ge(w_ready, count + (m - RAW + 1))
                dst = w_raw[:, m % RAW, :]
                if len(source.shape) == 3:
                    dst = dst.rearrange("p (k n) -> p k n", k=4)
                sp.dma_start(dst, source).then_inc(raw_s[m % RAW], 16)

            for f in range(2):
                for s in range(4):
                    ffn_load(strip_pieces(f, s), 4 * f + s, NS)
            with sp.Fori(1, PAIRS) as i:
                count = NS + 8 + (i - 1) * 12
                for s in range(4):
                    ffn_load(strip_pieces(2 * i, s), s, count)
                for s in range(4):
                    ffn_load(down_piece(2 * i - 2 + s % 2, s // 2), 4 + s, count)
                for s in range(4):
                    ffn_load(strip_pieces(2 * i + 1, s), 8 + s, count)
            for s in range(4):
                ffn_load(down_piece(F - 2 + s % 2, s // 2), s, NS + 8 + 12 * (PAIRS - 1))

            for m in range(2 * T):
                sp.wait_ge(down_add, 2 * T * (PAIRS - 1) + m + 1)
                t, half = m % T, m // T
                sp.dma_start(out_t[t, :, half * N:(half + 1) * N],
                             x1[:, t, half * N:(half + 1) * N]).then_inc(out_s, 16)
            sp.wait_ge(out_s, 16 * 2 * T)

        @block.gpsimd
        def _(pool):
            def split(ring, raw, width, loaded, n):
                pool.wait_ge(raw_s[raw], loaded)
                nc.gpsimd.tensor_tensor(w_hi[:, ring, 0:width], w_raw[:, raw, 0:width],
                                        ones[:, 0:1].to_broadcast([P, width]), ALU.mult).then_inc(w_hi_s, 1)
                pool.wait_ge(w_hi_s, n + 1)
                nc.gpsimd.tensor_tensor(w_lo[:, ring, 0:width], w_raw[:, raw, 0:width],
                                        w_hi[:, ring, 0:width].bitcast(F32), ALU.subtract).then_inc(w_ready, 1)

            def mask(t):
                pool.wait_ge(d_exp, t + 1)
                nc.gpsimd.affine_select(out=dmat[:, :, :], in_=dmat[:, :, :], pattern=[[0, MH], [1, P]],
                                        compare_op=ALU.is_ge, fill=0.0, base=0,
                                        channel_multiplier=-1).then_inc(d_masked, 1)

            def normalise(t):
                pool.wait_ge(p_inv, t + 1)
                nc.gpsimd.tensor_tensor(prob[t % 2][:, :, :], prob[t % 2][:, :, :], bcast(dsum[:, :], P),
                                        ALU.mult).then_inc(p_ready, 1)

            for k in range(1, K, 2):
                pool.wait_ge(w0_hi, k + 1)
                nc.gpsimd.tensor_tensor(w_lo[:, k, :], w0_raw[:, k, :], w_hi[:, k, :].bitcast(F32),
                                        ALU.subtract).then_inc(w0_odd, 1)
            pool.wait_ge(ones_set, 1)
            for n in range(NS):
                g = 1 + n // K
                if g >= 2 and n % K == 0:
                    pool.wait_ge(unit_done, (g - 1) * T)
                split((g * K + n % K) % RING, n % RAW, NKV if g == 1 else N, raw_count(n), n)
                if g == 4:
                    mask(n % K)
                if 0 <= n - 4 * K - 2 < T:
                    normalise(n - 4 * K - 2)

            def ffn_split(kind, s, m, base_n, loads):
                split(FFN_RING[kind] + s, m % RAW, N, RAW_BASE[m % RAW] + 16 * (loads + m // RAW + 1),
                      base_n + m)

            pool.wait_ge(wb_done, T)
            for f in range(2):
                for s in range(4):
                    ffn_split(("even", "odd")[f], s, 4 * f + s, NS, 0)
            pool.wait_ge(wb_done, 2 * T)
            pool.wait_ge(up_done, 3)
            with pool.Fori(1, PAIRS) as i:
                base_n = NS + 8 + (i - 1) * 12
                loads = 4 + (i - 1) * 6
                pool.wait_ge(up_done, 4 * i - 2)
                for s in range(4):
                    ffn_split("even", s, s, base_n, loads)
                pool.wait_ge(up_done, 4 * i - 1)
                for s in range(4):
                    ffn_split("down", s, 4 + s, base_n, loads)
                pool.wait_ge(up_done, 4 * i)
                for s in range(4):
                    ffn_split("odd", s, 8 + s, base_n, loads)
            pool.wait_ge(down_mm, 2 * T * (PAIRS - 1))
            for s in range(4):
                ffn_split("down", s, s, NS + 8 + 12 * (PAIRS - 1), 4 + 6 * (PAIRS - 1))

        @block.tensor
        def _(pe):
            steps = [0]

            def fence(ins):
                steps[0] += 1
                ins.then_inc(pe_step, 1)
                pe.wait_ge(pe_step, steps[0])

            def three(ps, x_hi, x_lo, wh, wl, first, last):
                nc.tensor.matmul(ps, x_hi, wh, start=first, stop=False)
                nc.tensor.matmul(ps, x_hi, wl, start=False, stop=False)
                return nc.tensor.matmul(ps, x_lo, wh, start=False, stop=last)

            def transpose_h(src, t, ready, tp, split_s):
                pe.wait_ge(ready, t + 1)
                for b in range(2):
                    if t >= 1:
                        pe.wait_ge(split_s, 2 * (t - 1) + b + 1)
                    for j in range(4):
                        last = nc.tensor.transpose(bank[2 + b][:, j * P:(j + 1) * P],
                                                   src[t % 2][:, (4 * b + j) * P:(4 * b + j + 1) * P],
                                                   ident[:, :])
                    last.then_inc(tp, 1)

            def unit(U):
                g, t = U // T, U % T
                width = NKV if g == 1 else N
                ps = bank[U % 2][:, 0:width]
                if U >= 2:
                    pe.wait_ge(acc_free[U % 2], U // 2)
                if g == 0:
                    pe.wait_ge(h_split, 2 * t + 2)
                for k in range(K):
                    if U == 0 and k == K // 2:
                        transpose_h(h_buf, 1, h_ready, h_tp, h_split)
                    if t == 0:
                        if g == 0:
                            pe.wait_ge((w0_even, w0_odd)[k % 2], k // 2 + 1)
                        else:
                            pe.wait_ge(w_ready, (g - 1) * K + k + 1)
                    r = (g * K + k) % RING
                    a = slice(t * P, (t + 1) * P)
                    last = three(ps, actT_hi[:, k, a], actT_lo[:, k, a], w_hi[:, r, 0:width],
                                 w_lo[:, r, 0:width], k == 0, k == K - 1)
                last.then_inc(unit_done, 1)

            def mq_transposes(t):
                pe.wait_ge(acc_free[t % 2], t // 2 + 1)
                if t >= 1:
                    pe.wait_ge(mq_evac, t)
                for f in range(4):
                    last = nc.tensor.transpose(bank[4][:, f * P:(f + 1) * P],
                                               mqraw[t % 2][:, f * P:(f + 1) * P], ident[:, :])
                last.then_inc(mq_tp, 1)

            def mlstm_scores(t):
                if t >= 1:
                    pe.wait_ge(it_exp, t)
                for h in range(MH):
                    c = t * MH + h
                    last = nc.tensor.matmul(bank[4][:, h * P:(h + 1) * P],
                                            ident[0:32, c:c + 1].to_broadcast([32, P]), nM[:, :],
                                            start=True, stop=True)
                last.then_inc(bc_done, 1)
                if t >= 1:
                    pe.wait_ge(scd_ready, t)
                a = slice(t * P, (t + 1) * P)
                for h in (0, 2, 1, 3):
                    rows = slice((h % 2) * DK, (h % 2 + 1) * DK)
                    last = nc.tensor.matmul(bank[5][:, h * P:(h + 1) * P], qkT[rows, 2 + h // 2, a],
                                            qkT[rows, h // 2, a], start=True, stop=True)
                    if h == 2:
                        fence(last)
                last.then_inc(sc_done, 1)
                if t >= 1:
                    pe.wait_ge(kw_ready, t)
                for p in range(2):
                    last = nc.tensor.transpose(bank[2][:, p * P:(p + 1) * P], qkT[:, 2 + p, a], ident[:, :])
                last.then_inc(kt_done, 1)

            def mlstm_products(t):
                pe.wait_ge(scd_ready, t + 1)
                pe.wait_ge(c_ready, t + 1)
                if t >= 1:
                    pe.wait_ge(h_done, t)
                for h in range(MH):
                    rows = slice((h % 2) * DK, (h % 2 + 1) * DK)
                    ps = bank[6 + h % 2][:, (h // 2) * (DV + 1):(h // 2 + 1) * (DV + 1)]
                    nc.tensor.matmul(ps, scd[:, h, :], mvx[:, t, h, :], start=True, stop=False)
                    last = nc.tensor.matmul(ps, qi[rows, h // 2, :], cst[rows, h // 2, :],
                                            start=False, stop=True)
                last.then_inc(num_done, 1)
                for h in range(MH):
                    rows = slice((h % 2) * DK, (h % 2 + 1) * DK)
                    last = nc.tensor.matmul(bank[3][rows, (h // 2) * (DV + 1):(h // 2 + 1) * (DV + 1)],
                                            kw[:, h, :], mvx[:, t, h, :], start=True, stop=True)
                last.then_inc(cup_done, 1)

            def att_sumsq(t):
                pe.wait_ge(sqa_done, t + 1)
                if t >= 1:
                    pe.wait_ge(ssa_ready, t)
                pe.wait_ge(mixb_ready, min(t + 5, T))
                for kk in range(4):
                    last = nc.tensor.matmul(bank[3][:, 0:1], sqb[:, kk * P:(kk + 1) * P], ones[:, 0:1],
                                            start=(kk == 0), stop=(kk == 3))
                last.then_inc(ssa_mm, 1)

            def att_transposes(t):
                pe.wait_ge(qn_ready, t + 1)
                if t >= 4:
                    pe.wait_ge(mixa_ready, t - 3)
                blocks = bank[2][:, :].rearrange("p (b c i n) -> p b c i n", b=2, c=2, i=2)
                for i in range(4):
                    last = nc.tensor.transpose(blocks[:, i // 2, :, i % 2, :],
                                               qn[:, i, :, :].rearrange("p a b -> p (a b)"), ident[:, :])
                last.then_inc(q_tp, 1)
                if t >= 1:
                    pe.wait_ge(mixb_ready, t)
                if t >= 5:
                    pe.wait_ge(ssa_ready, t - 4)
                for kk in range(4):
                    last = nc.tensor.transpose(bank[3][:, kk * P:(kk + 1) * P],
                                               mh[:, t, kk * P:(kk + 1) * P], ident[:, :])
                last.then_inc(mh_tp, 1)

            def att_scores(t):
                pe.wait_ge(qT_ready, t + 1)
                if t >= 1:
                    pe.wait_ge(s_evac, t)
                q = qT[t % 2]
                for kv, done in ((0, s_kv0), (1, s_kv1)):
                    rows = slice(kv * HD, (kv + 1) * HD)
                    for c2 in range(2):
                        start = t * P + c2 * CHUNK
                        for b in range(2):
                            o = (c2 * 2 + b) * P
                            last = nc.tensor.matmul(bank[4 + kv][:, o:o + P], q[rows, 2 * b + c2, :],
                                                    kT[rows, start:start + P], start=True, stop=True)
                    last.then_inc(done, 1)

            def att_prob_transposes(t):
                pe.wait_ge(p_ready, t + 1)
                for kv in range(KV):
                    if t >= 1:
                        pe.wait_ge((pTa, pTd)[kv], t)
                    for j in range(4):
                        last = nc.tensor.transpose(bank[6 + kv][:, j * P:(j + 1) * P],
                                                   prob[t % 2][:, kv * 4 + j, :], ident[:, :])
                last.then_inc(pt_done, 1)

            def att_values(t):
                pe.wait_ge(pTa, t + 1)
                pe.wait_ge(pTd, t + 1)
                if t == 0:
                    pe.wait_ge(v_zero, 1)
                    pe.wait_ge(v_moved, 16 * 2)
                pe.wait_ge(qT_ready, min(t + 4, T))
                if t >= 1:
                    pe.wait_ge(mixa_ready, t)
                for c2 in range(2):
                    for kv in range(KV):
                        if c2 == 0:
                            v = v_prev[:, t, kv * HD:(kv + 1) * HD]
                        else:
                            v = kvs[:, t, 2 * MH + (KV + kv) * HD:2 * MH + (KV + kv + 1) * HD]
                        for i2 in range(2):
                            rows = slice(i2 * HD, (i2 + 1) * HD)
                            b0 = kv * 4 + c2 * 2
                            rhs = pT[t % 2][:, b0:b0 + 2, i2 * CHUNK:(i2 + 1) * CHUNK]
                            o = bank[2][rows, kv * 2 * P:(kv + 1) * 2 * P].rearrange("p (b n) -> p b n", b=2)
                            last = nc.tensor.matmul(o[:, :, c2 * CHUNK:(c2 + 1) * CHUNK], v, rhs,
                                                    start=True, stop=True)
                last.then_inc(pv_done, 1)

            def out_unit(U):
                j = U - UNITS
                g, t = U // T, U % T
                pe.wait_ge(mixa_ready, t + 1)
                pe.wait_ge(mixb_ready, t + 1)
                a = slice(t * P, (t + 1) * P)
                for part, done in ((0, wa_done), (1, wb_done)):
                    if j == 0:
                        pe.wait_ge(acc_free[part], UNITS // 2)
                    else:
                        pe.wait_ge((wa_free, x1_ready)[part], j)
                    for kk in range(4):
                        k = part * 4 + kk
                        if t == 0:
                            pe.wait_ge(w_ready, (g - 1) * K + k + 1)
                        r = (g * K + k) % RING
                        last = three(bank[part][:, :], actT_hi[:, k, a], actT_lo[:, k, a], w_hi[:, r, :],
                                     w_lo[:, r, :], kk == 0, kk == 3)
                    last.then_inc(done, 1)

            pe.wait_ge(ident_s, 16)
            transpose_h(h_buf, 0, h_ready, h_tp, h_split)
            for U in range(ALL):
                g, t = U // T, U % T
                if U < UNITS:
                    unit(U)
                else:
                    out_unit(U)
                if U + 2 < T:
                    transpose_h(h_buf, U + 2, h_ready, h_tp, h_split)
                if U == 0:
                    pe.wait_ge(par_s, 16 * PARAMS)
                    nc.tensor.transpose(bank[4][:, 0:G_ROWS], prow[:, :],
                                        ident[0:G_ROWS, 0:G_ROWS]).then_inc(cols_tp, 1)
                if U == 1:
                    pe.wait_ge(cols_ready, 1)
                if 1 <= U <= T:
                    mq_transposes(U - 1)
                if U == 2 * T + 2:
                    pe.wait_ge(kn_ready, 1)
                    for b in range(2):
                        for j in range(4):
                            last = nc.tensor.transpose(bank[2 + b][:, j * P:(j + 1) * P],
                                                       kvs[:, 4 * b + j, 2 * MH:2 * MH + KV * HD], ident[:, :])
                    last.then_inc(kT_tp, 1)
                    pe.wait_ge(gate_v, 2)
                    nc.tensor.matmul(bank[5][:, 0:32], tri[:, :], lf[:, :], start=True, stop=True)
                    nc.tensor.matmul(bank[5][:, 32:64], ones[:, :], lf[:, :], start=True,
                                     stop=True).then_inc(gate_mm, 1)
                if U == 2 * T + 3:
                    pe.wait_ge(gate_v, 3)
                    nc.tensor.transpose(bank[6][0:32, 0:P], u_col[:, :], ident[:, :]).then_inc(gate_mm, 1)
                if U == 2 * T + 4:
                    pe.wait_ge(gate_v, 4)
                    nc.tensor.matmul(bank[7][:, 0:32], ones[0:32, :], diag[:, :], start=True,
                                     stop=True).then_inc(gate_mm, 1)
                if U == 2 * T + 5:
                    pe.wait_ge(gate_v, 5)
                    nc.tensor.transpose(bank[6][:, 0:32], nM[:, :], ident[0:32, 0:32]).then_inc(gate_mm, 1)
                s = U - 3 * T
                if s == 0:
                    pe.wait_ge(gate_v, 6)
                    pe.wait_ge(qk_ready, 4)
                    pe.wait_ge(acc_free[1], 3 * T // 2)
                if 1 <= s <= T:
                    mlstm_products(s - 1)
                if 0 <= s < T:
                    mlstm_scores(s)
                s = U - 4 * T
                if s == 1:
                    pe.wait_ge(c_ready, T + 1)
                    pe.wait_ge(mh_ready, T)
                if 0 <= s - 1 < T:
                    att_transposes(s - 1)
                if 0 <= s - 2 < T:
                    att_scores(s - 2)
                if 0 <= s - 3 < T:
                    att_prob_transposes(s - 3)
                if 0 <= s - 5 < T:
                    att_sumsq(s - 5)
                if 0 <= s - 4 < T:
                    att_values(s - 4)
                s = U - 6 * T
                if s == 2:
                    pe.wait_ge(ssa_ready, T)
                if 0 <= s - 2:
                    transpose_h(h2buf, s - 2, h2_ready, h2_tp, h2_split)

            def strip(kind, half, m, w_ready_at, free_at):
                free, done = ((silu_done, gate_done), (prod_done, up_done))[m]
                if free_at is not None:
                    pe.wait_ge(free, free_at)
                a = slice(half * N, (half + 1) * N)
                for k in range(K):
                    r = FFN_RING[kind] + 2 * m + k // 4
                    if half == 0 and k % 4 == 0:
                        pe.wait_ge(w_ready, w_ready_at + 2 * m + k // 4 + 1)
                    c = slice((k % 4) * P, (k % 4 + 1) * P)
                    last = three(bank[2 * half + m][:, :], w_hi[:, r, c], w_lo[:, r, c], actT_hi[:, k, a],
                                 actT_lo[:, k, a], k == 0, k == K - 1)
                last.then_inc(done, 1)

            def down(count, w_ready_at, ready):
                for half in range(2):
                    for t in range(T):
                        m = half * T + t
                        ps = bank[4 + m % 4][:, :]
                        if half == 0 and t % 4 == 0:
                            pe.wait_ge(act_ready, ready + t // 4 - 1)
                        if m >= 4:
                            pe.wait_ge(down_add, count + m - 3)
                        a = slice(t * P, (t + 1) * P)
                        for j in range(2):
                            r = FFN_RING["down"] + 2 * half + j
                            if t == 0:
                                pe.wait_ge(w_ready, w_ready_at + 2 * half + j + 1)
                            last = three(ps, act_hi[j][:, a], act_lo[j][:, a], w_hi[:, r, :], w_lo[:, r, :],
                                         j == 0, j == 1)
                        last.then_inc(down_mm, 1)

            pe.wait_ge(x1_ready, 2 * T)
            pe.wait_ge(h2_split, T)
            strip("even", 0, 0, NS, None)
            transpose_h(h2buf, T - 2, h2_ready, h2_tp, h2_split)
            strip("even", 0, 1, NS, None)
            strip("odd", 0, 0, NS + 4, 1)
            transpose_h(h2buf, T - 1, h2_ready, h2_tp, h2_split)
            strip("odd", 0, 1, NS + 4, 1)
            pe.wait_ge(h2_split, 2 * T)
            for m in range(2):
                strip("even", 1, m, NS, None)
            for m in range(2):
                strip("odd", 1, m, NS + 4, 3)
            with pe.Fori(1, PAIRS) as i:
                w_at = NS + 8 + (i - 1) * 12
                for half in range(2):
                    for m in range(2):
                        strip("even", half, m, w_at, 4 * i + half - 1)
                down((i - 1) * (2 * T), w_at + 4, 4 * i)
                for half in range(2):
                    for m in range(2):
                        strip("odd", half, m, w_at + 8, 4 * i + half + 1)
            down(2 * T * (PAIRS - 1), NS + 8 + 12 * (PAIRS - 1), 4 * PAIRS)

        @block.scalar
        def _(act):
            steps = [0]

            def step(ins):
                steps[0] += 1
                ins.then_inc(act_step, 1)

            def link(ins):
                step(ins)
                act.wait_ge(act_step, steps[0])

            def settle():
                act.wait_ge(act_step, steps[0])

            def inverse_root(out_, sumsq, n):
                link(nc.scalar.activation(out_, sumsq, ACT.Ln, bias=eps_t[0:sumsq.shape[0], 0:1], scale=1.0 / n))
                return nc.scalar.activation(out_, out_, ACT.Exp, scale=-0.5)

            eps_t = cols[:, G_ROWS:G_ROWS + 1]

            def stats(t):
                act.wait_ge(x_in_s[t % 2], 16 * (t // 2 + 1))
                if t == 0:
                    act.wait_ge(gate_v, 1)
                link(nc.scalar.activation(junk[:, :], x_in[t % 2][:, :], ACT.Square, accum_out=stat[:, t:t + 1]))
                inverse_root(rstd[:, t:t + 1], stat[:, t:t + 1], D).then_inc(rstd_ready, 1)

            def high_part(t, tp, done):
                for b in range(2):
                    act.wait_ge(tp, 2 * t + b + 1)
                    nc.scalar.activation(actT_hi[:, 4 * b:4 * b + 4, t * P:(t + 1) * P],
                                         bank[2 + b][:, :].rearrange("p (k n) -> p k n", k=4),
                                         ACT.Copy).then_inc(done, 1)

            def w0_high(k):
                act.wait_ge(w0_s[k], 16)
                nc.scalar.activation(w_hi[:, k, :], w0_raw[:, k, :], ACT.Copy).then_inc(w0_hi, 1)

            nc.scalar.preload_act_table_set("natural_log_exp_and_others")
            stats(0)
            w0_high(0)
            w0_high(1)
            high_part(0, h_tp, h_hi)
            w0_high(2)
            w0_high(3)
            stats(1)
            w0_high(4)
            w0_high(5)
            high_part(1, h_tp, h_hi)
            w0_high(6)
            w0_high(7)

            def evacuate(U):
                g, t = U // T, U % T
                ps = bank[U % 2]
                act.wait_ge(unit_done, U + 1)
                free = acc_free[U % 2]
                if g == 0:
                    if t >= 2:
                        act.wait_ge(mq_tp, t - 1)
                    nc.scalar.activation(mqraw[t % 2][:, :], ps[:, :], ACT.Copy).then_inc(free, 1)
                elif g == 1:
                    nc.scalar.activation(kvs[:, t, :], ps[:, 0:NKV], ACT.Copy).then_inc(free, 1)
                elif g == 2:
                    if t == 0:
                        act.wait_ge(mq_tp, T)
                        act.wait_ge(h_tp, 2 * T)
                    nc.scalar.activation(mvx[:, t, :, 0:DV], ps[:, :].rearrange("p (h d) -> p h d", h=MH),
                                         ACT.Copy).then_inc(free, 1)
                elif g == 3:
                    if t == 0:
                        act.wait_ge(gate_v, 6)
                    if t >= 2:
                        act.wait_ge(h_done, t - 1)
                    nc.scalar.activation(sig[t % 2][:, :], ps[:, :], ACT.Exp, scale=-1.0).then_inc(free, 1)
                else:
                    if t == 0:
                        act.wait_ge(mh_ready, T)
                        act.wait_ge(cup_done, T)
                    if t >= 1:
                        act.wait_ge(q_stat, t)
                    step(nc.scalar.activation(pq[:, :], ps[:, :], ACT.Square))
                    if t >= 2:
                        act.wait_ge(qn_ready, t - 1)
                    nc.scalar.activation(aqs[t % 2][:, :], ps[:, :], ACT.Copy).then_inc(free, 1)

            for U in range(ALL):
                g, t = U // T, U % T
                if U + 2 < T:
                    stats(U + 2)
                if U < UNITS:
                    evacuate(U)
                if U + 2 < T:
                    high_part(U + 2, h_tp, h_hi)
                if U in SILU_AT:
                    f = SILU_AT.index(U)
                    act.wait_ge(conv_ready, f + 1)
                    nc.scalar.activation(qkT[:, f, :], qkT[:, f, :], ACT.Silu).then_inc(qk_ready, 1)
                if U == SILU_AT[-1]:
                    nc.scalar.preload_act_table_set("natural_log_exp_and_others")
                if U == 2 * T:
                    vcols = slice(2 * MH + KV * HD, 2 * MH + 2 * KV * HD)
                    act.wait_ge(acc_free[0], T)
                    act.wait_ge(acc_free[1], T)
                    act.dma_start(v_prev[CHUNK:P, :, :], kvs[0:CHUNK, :, vcols]).then_inc(v_moved, 16)
                    act.dma_start(v_prev[0:CHUNK, 1:T, :], kvs[CHUNK:P, 0:T - 1, vcols]).then_inc(v_moved, 16)
                if U == 2 * T + 1:
                    act.wait_ge(kv_stat, 1)
                    inverse_root(krs[:, :], kss[:, :], HD).then_inc(kv_rs, 1)
                    act.wait_ge(kv_stat, 2)
                    link(nc.scalar.activation(expf[:, :], absf[:, :], ACT.Exp, scale=-1.0))
                    nc.scalar.activation(expf[:, :], expf[:, :], ACT.Ln, bias=1.0).then_inc(gate_a, 1)
                if U == 2 * T + 5:
                    act.wait_ge(gate_v, 5)
                    step(nc.scalar.activation(aold[:, :], aold[:, :], ACT.Exp))
                    nc.scalar.activation(wexp[:, :], wexp[:, :], ACT.Exp).then_inc(gate_a, 1)
                if U == 2 * T + 6:
                    act.wait_ge(kv_stat, 3)
                    nc.scalar.activation(enm[:, :], enm[:, :], ACT.Exp).then_inc(gate_a, 1)
                s = U - 3 * T
                if 0 <= s < T:
                    act.wait_ge(bc_done, s + 1)
                    if s >= 1:
                        act.wait_ge(scd_ready, s)
                    for h in range(MH):
                        c = s * MH + h
                        last = nc.scalar.activation(dmat[:, h, :], bank[4][:, h * P:(h + 1) * P], ACT.Exp,
                                                    bias=u_col[:, c:c + 1])
                    last.then_inc(d_exp, 1)
                    for h in range(MH):
                        rows = slice((h % 2) * DK, (h % 2 + 1) * DK)
                        last = nc.scalar.activation(itr[rows, h // 2, :], bank[4][rows, h * P:(h + 1) * P],
                                                    ACT.Exp, bias=mm[rows, s, h:h + 1])
                    last.then_inc(it_exp, 1)
                if 1 <= s <= T:
                    act.wait_ge(mh_ready, s)
                    if s == 1:
                        act.wait_ge(it_exp, s)
                    nc.scalar.activation(msq[:, :], mhs[:, :], ACT.Square,
                                         accum_out=ss2[:, s - 1, 1:2]).then_inc(ssb_done, 1)
                    act.wait_ge(ssb_done, s)
                s = U - 4 * T
                if 0 <= s - 1 < T:
                    tt = s - 1
                    act.wait_ge(q_tp, tt + 1)
                    if tt >= 2:
                        act.wait_ge(s_kv1, tt - 1)
                    nc.scalar.activation(qT[tt % 2][:, :, :], bank[2][:, :].rearrange("p (k n) -> p k n", k=4),
                                         ACT.Copy, scale=cols[:, G_Q:G_Q + 1]).then_inc(qT_ready, 1)
                    act.wait_ge(mh_tp, tt + 1)
                    nc.scalar.activation(actT_hi[:, 4:8, tt * P:(tt + 1) * P],
                                         bank[3][:, :].rearrange("p (k n) -> p k n", k=4),
                                         ACT.Copy).then_inc(mixb_hi, 1)
                if 0 <= s - 3 < T:
                    tt = s - 3
                    act.wait_ge(pt_done, tt + 1)
                    if tt >= 2:
                        act.wait_ge(pv_done, tt - 1)
                    nc.scalar.activation(pT[tt % 2][:, 0:4, :], bank[6][:, :].rearrange("p (k n) -> p k n", k=4),
                                         ACT.Copy).then_inc(pTa, 1)
                if 0 <= s - 4 < T:
                    tt = s - 4
                    act.wait_ge(pv_done, tt + 1)
                    if tt >= 1:
                        act.wait_ge(ssa_mm, tt)
                    nc.scalar.activation(sqb[:, :], bank[2][:, :], ACT.Square).then_inc(sqa_done, 1)
                    for kk in range(4):
                        last = nc.scalar.activation(actT_hi[:, kk, tt * P:(tt + 1) * P],
                                                    bank[2][:, kk * P:(kk + 1) * P], ACT.Copy,
                                                    scale=cols[:, G_ATT + kk:G_ATT + kk + 1])
                    last.then_inc(mixa_hi, 1)
                if 0 <= s - 2 < T:
                    tt = s - 2
                    act.wait_ge(s_max, tt + 1)
                    if tt >= 1:
                        act.wait_ge(p_ready, tt)
                    for j in range(8):
                        step(nc.scalar.activation(prob[tt % 2][:, j, :], prob[tt % 2][:, j, :], ACT.Exp, bias=nmx[:, j:j + 1],
                                                  accum_out=dsum[:, j:j + 1]))
                    nc.scalar.activation(esk[:, :], esk[:, :], ACT.Exp).then_inc(p_exp, 1)
                if 0 <= s < T:
                    act.wait_ge(q_stat, s + 1)
                    if s >= 1:
                        act.wait_ge(qn_ready, s)
                    inverse_root(qrs[:, :], qss[:, :], HD).then_inc(q_rs, 1)
                if 0 <= s - 6 < T:
                    tt = s - 6
                    act.wait_ge(ssa_ready, tt + 1)
                    inverse_root(rmix[:, tt, :], ss2[:, tt, :], N).then_inc(rmix_ready, 1)
                s = U - 6 * T
                if s >= 0:
                    act.wait_ge(x1_ready, T + s + 1)
                    if s == 0:
                        act.wait_ge(pv_done, T)
                    link(nc.scalar.activation(junk2[:, :], x1[:, s, :], ACT.Square, accum_out=stat[:, s:s + 1]))
                    inverse_root(rstd[:, s:s + 1], stat[:, s:s + 1], D).then_inc(r2_ready, 1)
                    if s >= 2:
                        high_part(s - 2, h2_tp, h2_hi)

            def silu_half(half, count, read=None):
                act.wait_ge(gate_done, count)
                if read is not None:
                    act.wait_ge(prod_done, read)
                nc.scalar.activation(silu[half][:, :], bank[2 * half][:, :], ACT.Silu).then_inc(silu_done, 1)

            def high_half(j, half, count):
                act.wait_ge(prod_done, count)
                a = slice(half * N, (half + 1) * N)
                nc.scalar.activation(act_hi[j][:, a], prod[:, a], ACT.Copy).then_inc(act_hi_s, 1)

            act.wait_ge(mixa_ready, T)
            silu_half(0, 1)
            high_part(T - 2, h2_tp, h2_hi)
            high_half(0, 0, 1)
            silu_half(0, 2, 1)
            high_part(T - 1, h2_tp, h2_hi)
            high_half(1, 0, 2)
            silu_half(1, 3)
            high_half(0, 1, 3)
            silu_half(1, 4, 3)
            high_half(1, 1, 4)
            with act.Fori(1, PAIRS) as i:
                silu_half(0, 4 * i + 1, 4 * i - 1)
                silu_half(1, 4 * i + 2, 4 * i)
                act.wait_ge(down_mm, 2 * T * i)
                high_half(0, 0, 4 * i + 1)
                high_half(0, 1, 4 * i + 2)
                silu_half(0, 4 * i + 3, 4 * i + 1)
                high_half(1, 0, 4 * i + 3)
                silu_half(1, 4 * i + 4, 4 * i + 2)
                high_half(1, 1, 4 * i + 4)

        @block.vector
        def _(dve):
            steps = [0]
            V_ = nc.vector

            def step(ins):
                steps[0] += 1
                ins.then_inc(dve_step, 1)

            def link(ins):
                step(ins)
                dve.wait_ge(dve_step, steps[0])

            def low_part(t, hi_s, done):
                for b in range(2):
                    dve.wait_ge(hi_s, 2 * t + b + 1)
                    V_.tensor_tensor(actT_lo[:, 4 * b:4 * b + 4, t * P:(t + 1) * P],
                                     bank[2 + b][:, :].rearrange("p (k n) -> p k n", k=4),
                                     actT_hi[:, 4 * b:4 * b + 4, t * P:(t + 1) * P].bitcast(F32),
                                     ALU.subtract).then_inc(done, 1)

            def normed(dst, src, t, r_s, tp, done):
                dve.wait_ge(r_s, t + 1)
                if t >= 2:
                    dve.wait_ge(tp, 2 * (t - 1))
                V_.scalar_tensor_tensor(dst[t % 2][:, :], src, rstd[:, t:t + 1], g_row[:, :],
                                        ALU.mult, ALU.mult).then_inc(done, 1)

            def w0_low(k):
                dve.wait_ge(w0_hi, k + 1)
                V_.tensor_tensor(w_lo[:, k, :], w0_raw[:, k, :], w_hi[:, k, :].bitcast(F32),
                                 ALU.subtract).then_inc(w0_even, 1)

            V_.memset(cols[:, G_ROWS:G_ROWS + 1], EPS).then_inc(gate_v, 1)
            V_.memset(ones[:, :], 1.0).then_inc(ones_set, 1)
            step(V_.memset(rawT[:, :, 0:3], 0.0))
            step(V_.memset(mm[:, 0, :], 0.0))
            dve.wait_ge(gmix_s, 16)
            normed(h_buf, x_in[0][:, :], 0, rstd_ready, h_tp, h_ready)
            w0_low(0)
            low_part(0, h_hi, h_split)
            w0_low(2)
            normed(h_buf, x_in[1][:, :], 1, rstd_ready, h_tp, h_ready)
            w0_low(4)
            w0_low(6)
            low_part(1, h_hi, h_split)

            def convolution(f):
                y = qkT[:, f, :]
                link(V_.tensor_scalar(y, rawT[:, f, 0:S], cols[:, f:f + 1], None, ALU.mult))
                for i in range(1, TAPS):
                    ins = V_.scalar_tensor_tensor(y, rawT[:, f, i:i + S], cols[:, 4 * i + f:4 * i + f + 1], y,
                                                  ALU.mult, ALU.add)
                    if i < TAPS - 1:
                        link(ins)
                ins.then_inc(conv_ready, 1)

            kview = kvs[:, :, 2 * MH:2 * MH + KV * HD]
            tril32 = ident[0:32, 0:32]

            for U in range(ALL):
                g, t = U // T, U % T
                if U + 2 < T:
                    normed(h_buf, x_in[t % 2][:, :], U + 2, rstd_ready, h_tp, h_ready)
                if 1 <= U <= T:
                    dve.wait_ge(mq_tp, U)
                    V_.tensor_copy(rawT[:, :, 3 + (U - 1) * P:3 + U * P],
                                   bank[4][:, :].rearrange("p (k n) -> p k n", k=4)).then_inc(mq_evac, 1)
                if U + 2 < T:
                    low_part(U + 2, h_hi, h_split)
                if U == 0:
                    dve.wait_ge(cols_tp, 1)
                    link(V_.tensor_copy(cols[:, 0:G_ROWS], bank[4][:, 0:G_ROWS]))
                    V_.tensor_scalar(cols[:, G_Q:G_Q + 1], cols[:, G_Q:G_Q + 1], HD ** -0.5, None,
                                     ALU.mult).then_inc(cols_ready, 1)
                    dve.wait_ge(cols_ready, 1)
                    dve.wait_ge(par_s, 16 * PARAMS)
                    for i2 in range(2):
                        rows = slice(i2 * CHUNK, (i2 + 1) * CHUNK)
                        heads = sinks8[rows, :].rearrange("p (g b i) -> p g b i", g=KV, i=2)[:, :, :, i2]
                        link(V_.tensor_copy(sink_b[rows, :].rearrange("p (g c b) -> p g c b", g=KV, c=2),
                                            heads.unsqueeze(2).to_broadcast([CHUNK, KV, 2, 2])))
                if U == T + 1:
                    dve.wait_ge(mq_evac, T)
                    dve.wait_ge(h_tp, 2 * T)
                    step(V_.memset(mvx[:, :, :, DV:DV + 1], 1.0))
                if T + 1 <= U < T + 5:
                    convolution(U - T - 1)
                if U == 2 * T:
                    dve.wait_ge(acc_free[0], T)
                    dve.wait_ge(acc_free[1], T)
                    V_.memset(v_prev[0:CHUNK, 0, :], 0.0).then_inc(v_zero, 1)
                    step(V_.memset(kT[:, 0:CHUNK], 0.0))
                    link(V_.tensor_tensor(ksq[:, :, :], kview, kview, ALU.mult))
                    V_.tensor_reduce(kss[:, :], ksq[:, :, :].rearrange("p t (g d) -> p (t g) d", g=KV),
                                     AX.X, ALU.add).then_inc(kv_stat, 1)
                    link(V_.tensor_tensor(gate8[:, :, :], kvs[:, :, 0:8],
                                          bias_g[:, :].unsqueeze(1).to_broadcast([P, T, 8]), ALU.add))
                    fpre = gate8[:, :, MH:2 * MH]
                    absf3 = absf[:, :].rearrange("p (t h) -> p t h", h=MH)
                    V_.scalar_tensor_tensor(absf3, fpre, -1.0, fpre, ALU.mult, ALU.max).then_inc(kv_stat, 1)
                if U == 2 * T + 1:
                    dve.wait_ge(kv_rs, 1)
                    for gg in range(KV):
                        kk_ = kvs[:, :, 2 * MH + gg * HD:2 * MH + (gg + 1) * HD]
                        ins = V_.tensor_tensor(kk_, kk_,
                                               bcast(krs[:, :].rearrange("p (t g) -> p t g", g=KV)[:, :, gg], HD),
                                               ALU.mult)
                        if gg == 0:
                            step(ins)
                    ins.then_inc(kn_ready, 1)
                    dve.wait_ge(gate_a, 1)
                    V_.scalar_tensor_tensor(lf[:, :].rearrange("p (t h) -> p t h", h=MH), fpre, 0.0,
                                            expf[:, :].rearrange("p (t h) -> p t h", h=MH),
                                            ALU.min, ALU.subtract).then_inc(gate_v, 1)
                if U == 2 * T + 2:
                    dve.wait_ge(kT_tp, 1)
                    for b in range(2):
                        step(V_.tensor_scalar(kT[:, CHUNK + b * N:CHUNK + (b + 1) * N], bank[2 + b][:, :],
                                              cols[:, G_K:G_K + 1], None, ALU.mult))
                    dve.wait_ge(gate_mm, 1)
                    link(V_.tensor_copy(bg[:, :], bank[5][:, 0:64]))
                    V_.tensor_tensor(u_col[:, :].rearrange("p (t h) -> p t h", h=MH), gate8[:, :, 0:MH],
                                     bg[:, 0:32].rearrange("p (t h) -> p t h", h=MH),
                                     ALU.subtract).then_inc(gate_v, 1)
                if U == 2 * T + 3:
                    dve.wait_ge(gate_mm, 2)
                    link(V_.tensor_copy(uT[:, :], bank[6][0:32, 0:P]))
                    link(V_.tensor_tensor_scan(cm[:, :], uT[:, :], uT[:, :], -3.0e38, ALU.max, ALU.max))
                    V_.tensor_scalar(diag[:, :], tril32, cm[:, P - 1:P], None, ALU.mult).then_inc(gate_v, 1)
                if U == 2 * T + 4:
                    dve.wait_ge(gate_mm, 3)
                    link(V_.tensor_copy(maxu_b[:, :], bank[7][:, 0:32]))
                    link(V_.tensor_tensor(gm[:, :], bg[:, 32:64], maxu_b[:, :], ALU.add))
                    tot = bg[:, 32:64].rearrange("p (t h) -> p t h", h=MH)
                    gm3 = gm[:, :].rearrange("p (t h) -> p t h", h=MH)
                    for h in range(MH):
                        ins = V_.tensor_tensor_scan(mm[:, 1:T + 1, h], tot[:, :, h], gm3[:, :, h], 0.0,
                                                    ALU.add, ALU.max)
                        step(ins)
                    dve.wait_ge(dve_step, steps[0])
                    mprev = mm[:, 0:T, :].rearrange("p t h -> p (t h)")
                    link(V_.tensor_tensor(mlast[:, :], mprev, maxu_b[:, :], ALU.max))
                    step(V_.tensor_tensor(aold[:, :], mprev, mlast[:, :], ALU.subtract))
                    step(V_.tensor_tensor(wexp[:, :], u_col[:, :], mlast[:, :], ALU.subtract))
                    link(V_.tensor_tensor(diag[:, :], mm[0:32, 0:T, :].rearrange("p t h -> p (t h)"), tril32,
                                          ALU.mult))
                    link(V_.tensor_reduce(mcol[:, :], diag[:, :], AX.X, ALU.add))
                    V_.tensor_scalar(nM[:, :], cm[:, :], mcol[:, 0:1], -1.0, ALU.max, ALU.mult).then_inc(gate_v, 1)
                if U == 2 * T + 5:
                    dve.wait_ge(gate_a, 2)
                    step(V_.tensor_scalar(wexp[:, :], wexp[:, :], DK ** -0.5, None, ALU.mult))
                    a4 = aold[:, :].rearrange("p (t a b) -> p t a b", a=2, b=2)
                    step(V_.tensor_copy(aold2[0:DK, :, :], a4[0:DK, :, :, 0]))
                    step(V_.tensor_copy(aold2[DK:P, :, :], a4[DK:P, :, :, 1]))
                    dve.wait_ge(gate_mm, 4)
                    V_.tensor_tensor(enm[:, :], bank[6][:, 0:32], bg[:, 0:32], ALU.subtract).then_inc(kv_stat, 1)
                    step(V_.memset(cst[:, :, :], 0.0))
                    dve.wait_ge(dve_step, steps[0])
                    V_.memset(den4[:, :], 0.0).then_inc(c_ready, 1)
                    dve.wait_ge(c_ready, 1)
                    dve.wait_ge(kv_stat, 3)
                    V_.memset(den4[:, :], 0.0).then_inc(gate_v, 1)
                s = U - 3 * T
                if 1 <= s <= T:
                    tt = s - 1
                    dve.wait_ge(cup_done, tt + 1)
                    step(V_.scalar_tensor_tensor(cst[:, 0, :], cst[:, 0, :], aold2[:, tt, 0:1],
                                                 bank[3][:, 0:DV + 1], ALU.mult, ALU.add))
                    V_.scalar_tensor_tensor(cst[:, 1, :], cst[:, 1, :], aold2[:, tt, 1:2],
                                            bank[3][:, DV + 1:2 * (DV + 1)], ALU.mult,
                                            ALU.add).then_inc(c_ready, 1)
                    if tt == 0:
                        dve.wait_ge(gate_a, 3)
                    for p in range(2):
                        step(V_.tensor_copy(
                            den4[:, :].rearrange("p (a b) -> p b a", b=2)[:, p, :],
                            bank[6 + p][:, 0:2 * (DV + 1)].rearrange("p (h d) -> p h d", h=2)[:, :, DV]))
                    dve.wait_ge(dve_step, steps[0])
                    link(V_.scalar_tensor_tensor(den4[:, :], den4[:, :], -1.0, den4[:, :], ALU.mult, ALU.max))
                    link(V_.tensor_tensor(den4[:, :], den4[:, :], enm[:, tt * MH:(tt + 1) * MH], ALU.max))
                    link(V_.reciprocal(den4[:, :], den4[:, :]))
                    if tt >= 1:
                        dve.wait_ge(ssb_done, tt)
                    for h in range(MH):
                        ins = V_.scalar_tensor_tensor(
                            mhs[:, h * DV:(h + 1) * DV],
                            bank[6 + h % 2][:, (h // 2) * (DV + 1):(h // 2) * (DV + 1) + DV],
                            den4[:, h:h + 1], sig[tt % 2][:, h * DV:(h + 1) * DV], ALU.mult, ALU.mult)
                        if h < MH - 1:
                            step(ins)
                    ins.then_inc(h_done, 1)
                    dve.wait_ge(h_done, tt + 1)
                    if tt == 0:
                        dve.wait_ge(late_s, 16)
                    V_.tensor_tensor(mh[:, tt, :], mhs[:, :], g_row[:, 0:MH * DV], ALU.mult).then_inc(mh_ready, 1)
                if 0 <= s < T:
                    dve.wait_ge(kt_done, s + 1)
                    V_.tensor_tensor(kw[:, :, :], bank[2][:, 0:MH * DK].rearrange("p (h d) -> p h d", h=MH),
                                     bcast(wexp[:, s * MH:(s + 1) * MH], DK), ALU.mult).then_inc(kw_ready, 1)
                    dve.wait_ge(it_exp, s + 1)
                    step(V_.tensor_tensor(qi[:, :, :], qkT[:, 0:2, s * P:(s + 1) * P], itr[:, :, :], ALU.mult))
                    dve.wait_ge(d_masked, s + 1)
                    dve.wait_ge(sc_done, s + 1)
                    V_.scalar_tensor_tensor(scd[:, :, :].rearrange("p h n -> p (h n)"), bank[5][:, :], DK ** -0.5,
                                            dmat[:, :, :].rearrange("p h n -> p (h n)"), ALU.mult,
                                            ALU.mult).then_inc(scd_ready, 1)
                    dve.wait_ge(acc_free[U % 2], U // 2 + 1)
                    link(V_.tensor_scalar(sig[s % 2][:, :], sig[s % 2][:, :], 1.0, None, ALU.add))
                    link(V_.reciprocal(sig[s % 2][:, :], sig[s % 2][:, :]))
                if U >= UNITS:
                    j = U - UNITS
                    dve.wait_ge(wa_done, j + 1)
                    if j < T:
                        dve.wait_ge(rmix_ready, t + 1)
                        if t == 0:
                            dve.wait_ge(x1_s[0], 16 * 4)
                        if t == 4:
                            dve.wait_ge(x1_s[1], 16 * (T - 4))
                    xs = x1[:, t, (j // T) * N:(j // T + 1) * N]
                    V_.scalar_tensor_tensor(xs, bank[0][:, :], rmix[:, t, 0:1], xs, ALU.mult,
                                            ALU.add).then_inc(wa_free, 1)
                    dve.wait_ge(wa_free, j + 1)
                    dve.wait_ge(wb_done, j + 1)
                    V_.scalar_tensor_tensor(xs, bank[1][:, :], rmix[:, t, 1:2], xs, ALU.mult,
                                            ALU.add).then_inc(x1_ready, 1)
                s = U - 4 * T
                if 0 <= s - 1 < T:
                    tt = s - 1
                    dve.wait_ge(mixb_hi, tt + 1)
                    V_.tensor_tensor(actT_lo[:, 4:8, tt * P:(tt + 1) * P],
                                     bank[3][:, :].rearrange("p (k n) -> p k n", k=4),
                                     actT_hi[:, 4:8, tt * P:(tt + 1) * P].bitcast(F32),
                                     ALU.subtract).then_inc(mixb_ready, 1)
                if 0 <= s - 2 < T:
                    tt = s - 2
                    if tt == 0:
                        dve.wait_ge(late_s, 16 * 3)
                    if tt >= 2:
                        dve.wait_ge(pt_done, tt - 1)
                    for kv, done, out_s_ in ((0, s_kv0, dve_step), (1, s_kv1, s_evac)):
                        cols_ = slice(kv * 2 * P, (kv + 1) * 2 * P)
                        if tt == 0:
                            penalty = bias[:, :, cols_]
                        else:
                            penalty = bias[:, 1, cols_].unsqueeze(1).to_broadcast([P, 2, 2 * P])
                        dve.wait_ge(done, tt + 1)
                        V_.tensor_tensor(prob[tt % 2][:, 4 * kv:4 * kv + 4, :].rearrange("p (c b) n -> p c (b n)", c=2),
                                         bank[4 + kv][:, :].rearrange("p (c n) -> p c n", c=2), penalty,
                                         ALU.add).then_inc(out_s_, 1)
                    steps[0] += 1
                    dve.wait_ge(s_evac, tt + 1)
                    link(V_.tensor_reduce(smx[:, :], prob[tt % 2][:, :, :], AX.X, ALU.max))
                    link(V_.tensor_tensor(smx[:, :], smx[:, :], sink_b[:, :], ALU.max))
                    link(V_.tensor_scalar(nmx[:, :], smx[:, :], -1.0, None, ALU.mult))
                    V_.tensor_tensor(esk[:, :], sink_b[:, :], nmx[:, :], ALU.add).then_inc(s_max, 1)
                if 0 <= s - 5 < T:
                    tt = s - 5
                    dve.wait_ge(ssa_mm, tt + 1)
                    V_.tensor_copy(ss2[:, tt, 0:1], bank[3][:, 0:1]).then_inc(ssa_ready, 1)
                if 0 <= s < T:
                    dve.wait_ge(acc_free[U % 2], U // 2 + 1)
                    if s >= 1:
                        dve.wait_ge(q_rs, s)
                    V_.tensor_reduce(qss[:, :], pq[:, :].rearrange("p (h d) -> p h d", h=HEADS), AX.X,
                                     ALU.add).then_inc(q_stat, 1)
                if 0 <= s - 4 < T:
                    tt = s - 4
                    dve.wait_ge(mixa_hi, tt + 1)
                    for kk in range(4):
                        ins = V_.scalar_tensor_tensor(
                            actT_lo[:, kk, tt * P:(tt + 1) * P], bank[2][:, kk * P:(kk + 1) * P],
                            cols[:, G_ATT + kk:G_ATT + kk + 1],
                            actT_hi[:, kk, tt * P:(tt + 1) * P].bitcast(F32), ALU.mult, ALU.subtract)
                        if kk < 3:
                            step(ins)
                    ins.then_inc(mixa_ready, 1)
                if 0 <= s - 3 < T:
                    tt = s - 3
                    dve.wait_ge(pt_done, tt + 1)
                    if tt >= 2:
                        dve.wait_ge(pv_done, tt - 1)
                    V_.tensor_copy(pT[tt % 2][:, 4:8, :],
                                   bank[7][:, :].rearrange("p (k n) -> p k n", k=4)).then_inc(pTd, 1)
                if 0 <= s - 2 < T:
                    tt = s - 2
                    dve.wait_ge(p_exp, tt + 1)
                    link(V_.tensor_tensor(dsum[:, :], dsum[:, :], esk[:, :], ALU.add))
                    V_.reciprocal(dsum[:, :], dsum[:, :]).then_inc(p_inv, 1)
                if 0 <= s < T:
                    dve.wait_ge(q_rs, s + 1)
                    if s >= 1:
                        dve.wait_ge(q_tp, s)
                    V_.tensor_tensor(qn[:, :, :, :].rearrange("p i g d -> p g i d"),
                                     aqs[s % 2][:, :].rearrange("p (g i d) -> p g i d", g=KV, i=4),
                                     bcast(qrs[:, :].rearrange("p (g i) -> p g i", g=KV), HD),
                                     ALU.mult).then_inc(qn_ready, 1)
                s = U - 6 * T
                if s == 1:
                    dve.wait_ge(gf_s, 16)
                if s >= 1:
                    normed(h2buf, x1[:, s - 1, :], s - 1, r2_ready, h2_tp, h2_ready)
                if s >= 2:
                    low_part(s - 2, h2_hi, h2_split)

            normed(h2buf, x1[:, T - 1, :], T - 1, r2_ready, h2_tp, h2_ready)
            low_part(T - 2, h2_hi, h2_split)

            def product_half(half, count, split=None):
                dve.wait_ge(silu_done, count)
                dve.wait_ge(up_done, count)
                if split is not None:
                    dve.wait_ge(act_ready, split)
                V_.tensor_tensor(prod[:, half * N:(half + 1) * N], bank[2 * half + 1][:, :], silu[half][:, :],
                                 ALU.mult).then_inc(prod_done, 1)

            def low_half(j, half, count):
                dve.wait_ge(act_hi_s, count)
                a = slice(half * N, (half + 1) * N)
                V_.tensor_tensor(act_lo[j][:, a], prod[:, a], act_hi[j][:, a].bitcast(F32),
                                 ALU.subtract).then_inc(act_ready, 1)

            def add_down(count):
                for half in range(2):
                    for t in range(T):
                        m = half * T + t
                        dve.wait_ge(down_mm, count + m + 1)
                        xs = x1[:, t, half * N:(half + 1) * N]
                        V_.tensor_tensor(xs, bank[4 + m % 4][:, :], xs, ALU.add).then_inc(down_add, 1)

            product_half(0, 1)
            low_half(0, 0, 1)
            low_part(T - 1, h2_hi, h2_split)
            product_half(0, 2, 1)
            low_half(1, 0, 2)
            product_half(1, 3)
            low_half(0, 1, 3)
            product_half(1, 4, 3)
            low_half(1, 1, 4)
            with dve.Fori(1, PAIRS) as i:
                product_half(0, 4 * i + 1, 4 * i - 1)
                product_half(1, 4 * i + 2, 4 * i)
                add_down((i - 1) * (2 * T))
                low_half(0, 0, 4 * i + 1)
                low_half(0, 1, 4 * i + 2)
                product_half(0, 4 * i + 3, 4 * i + 1)
                low_half(1, 0, 4 * i + 3)
                product_half(1, 4 * i + 4, 4 * i + 2)
                low_half(1, 1, 4 * i + 4)
            dve.wait_ge(act_ready, 4 * PAIRS)
            add_down(2 * T * (PAIRS - 1))


NAMES = ["x", "g_mix", "w_in", "b_gates", "conv_qk", "q_norm_gain", "k_norm_gain", "attn_sinks",
         "g_attn_out", "g_mlstm_out", "w_out", "g_ffn", "w_gate", "w_up", "w_down"]


def kernel(**inputs):
    import concourse.bacc as bacc
    from concourse.bass_utils import run_bass_kernel_spmd

    nc = bacc.Bacc("TRN2", target_bir_lowering=False, num_devices=1, dynamic_dma_scratch_size=1024)
    arrays, args = {}, []
    for name in NAMES:
        a = np.ascontiguousarray(inputs[name])
        arrays[f"in_{name}"] = a
        args.append(nc.dram_tensor(f"in_{name}", a.shape, mybir.dt.from_np(a.dtype), kind="ExternalInput").ap())
    arrays["consts"] = constants()
    args.append(nc.dram_tensor("consts", arrays["consts"].shape, F32, kind="ExternalInput").ap())
    out = nc.dram_tensor("out", inputs["x"].shape, F32, kind="ExternalOutput").ap()
    hymba_block(nc, *args, out)
    r = run_bass_kernel_spmd(nc, [arrays], core_ids=[0])
    return r.results[0]["out"]
```

```python
from contextlib import ExitStack

import numpy as np

import concourse.bass as bass
from concourse import mybir

ALU = mybir.AluOpType
ACT = mybir.ActivationFunctionType
AX = mybir.AxisListType
F32 = mybir.dt.float32
F32R = mybir.dt.float32r

P = 128
CHUNK = 64
HEADS = 8
KV = 2
HD = 64
MH = 4
DK = 64
DV = 128
TAPS = 4
EPS = 1e-6
NEG = -1.0e30

C_ID, C_TRI, C_BIAS, C_FIRST, C_END = 0, 128, 256, 768, 1280
G_CONV, G_OUT, G_K, G_Q, G_ROWS = 0, 16, 24, 25, 26
G_MIX, G_EPS, G_COLS = 26, 34, 35


def constants():
    c = np.zeros((P, C_END), np.float32)
    c[:, C_ID:C_ID + P] = np.eye(P)
    c[:, C_TRI:C_TRI + P] = np.triu(np.ones((P, P)))
    row = np.arange(P)
    q, i2 = row % CHUNK, row // CHUNK
    key = np.arange(P)
    dist = np.abs(q[:, None] + CHUNK - key[None, :])
    for kv in range(KV):
        for b in range(2):
            slope = 2.0 ** -(kv * 4 + b * 2 + i2 + 1.0)
            blk = -slope[:, None] * dist
            a = (kv * 2 + b) * P
            c[:, C_BIAS + a:C_BIAS + a + P] = blk
            c[:, C_FIRST + a:C_FIRST + a + P] = np.where(key[None, :] < CHUNK, NEG, blk)
    return c


def hymba_block(nc, x, g_mix, w_in, b_gates, conv_qk, q_gain, k_gain, sinks,
                g_att, g_ml, w_out, g_ffn, w_gate, w_up, w_down, consts, out):
    S, D = x.shape[1], x.shape[2]
    DFF = w_gate.shape[2]
    T = S // P
    K = D // P
    N = 512
    F = DFF // P
    PAIRS = F // 2
    AQ, AK = 0, HEADS * HD
    MQ = AK + 2 * KV * HD
    MV = MQ + 2 * MH * DK
    MO = MV + MH * DV
    GATES = MO + MH * DV
    NKV = 2 * MH + 2 * KV * HD
    RING, RAW = 16, 2
    GROUPS = 7
    UNITS = 5 * T
    ALL = GROUPS * T
    assert T == 8 and K == 8 and F % 2 == 0 and MQ + 512 == MV

    x_t = x.rearrange("a (t p) d -> t p (a d)", p=P)
    out_t = out.rearrange("a (t p) d -> t p (a d)", p=P)
    w_in_k = w_in.rearrange("a (k p) n -> k p (a n)", p=P)
    w_out_k = w_out.rearrange("a (k p) n -> k p (a n)", p=P)
    w_gate_k = w_gate.rearrange("a (k p) n -> p (a k) n", p=P)
    w_up_k = w_up.rearrange("a (k p) n -> p (a k) n", p=P)
    w_down_r = w_down.rearrange("a f n -> (a f) n")

    ctx = ExitStack()
    with ctx:
        base = [(nc.sbuf_base + 31) // 32 * 32]

        def place(name, shape, dt=F32, at=None):
            size = 4 * int(np.prod(shape[1:]))
            start = base[0] if at is None else at
            assert start + size <= nc.sbuf_usable_end, (name, start + size - nc.sbuf_usable_end)
            t = nc.alloc_sbuf_tensor_at(name, list(shape), dt, offset=start)
            end = (start + size + 31) // 32 * 32
            if at is None:
                base[0] = end
            return t, end

        def sem(name):
            return ctx.enter_context(nc.semaphore(name))

        actT_hi, _ = place("actT_hi", [P, K, S], F32R)
        actT_lo, _ = place("actT_lo", [P, K, S], F32R)
        w_hi, _ = place("w_hi", [P, RING, N], F32R)
        w_lo, _ = place("w_lo", [P, RING, N], F32R)
        w_raw, _ = place("w_raw", [P, RAW, N])
        ident, _ = place("ident", [P, P])
        tri, _ = place("tri", [P, P])
        ones, _ = place("ones", [P, P])
        cols, _ = place("cols", [P, G_COLS])
        bias_g, _ = place("bias_g", [P, 8])
        sinks8, _ = place("sinks8", [P, 8])
        sink_b, _ = place("sink_b", [P, 8])
        g_row, _ = place("g_row", [P, D])
        nm_b0, _ = place("nm_b0", [P, N], at=base[0] - 4 * D)
        nm_b1, _ = place("nm_b1", [P, N], at=base[0] - 2 * D)
        nm_b = [nm_b0, nm_b1]
        stat, _ = place("stat", [P, T])
        rstd, _ = place("rstd", [P, T])
        nrstd, _ = place("nrstd", [P, T])
        ss2, _ = place("ss2", [P, T, 2])
        rmix, _ = place("rmix", [P, T, 2])
        gate8, _ = place("gate8", [P, T, 8])
        small = {}
        for name in ("absf", "expf", "lf", "u", "mlast", "aold", "wexp", "enm", "maxu_b"):
            small[name], _ = place(name, [P, T * MH])
        absf, expf, lf, u_col = small["absf"], small["expf"], small["lf"], small["u"]
        mlast, aold, wexp, enm = small["mlast"], small["aold"], small["wexp"], small["enm"]
        gm, maxu_b = absf, small["maxu_b"]
        bg, _ = place("bg", [P, 2 * T * MH])
        mm, _ = place("mm", [P, T + 1, MH])
        aold2, _ = place("aold2", [P, T, 2])
        den4, _ = place("den4", [P, MH])
        smx, _ = place("smx", [P, 8])
        nmx, _ = place("nmx", [P, 8])
        dsum, _ = place("dsum", [P, 8])
        esk, _ = place("esk", [P, 8])
        qss, _ = place("qss", [P, 8])
        qrs, _ = place("qrs", [P, 8])
        kss, _ = place("kss", [P, 2 * T])
        krs, _ = place("krs", [P, 2 * T])

        J = base[0]
        w0_raw, j_end = place("w0_raw", [P, K, N], at=J)
        ksq, _ = place("ksq", [P, T, P], at=J)
        cm, e = place("cm", [32, P], at=J + 4096)
        uT, e = place("uT", [32, P], at=e)
        nM, e = place("nM", [32, P], at=e)
        diag, e = place("diag", [32, 32], at=e)
        mcol, e = place("mcol", [32, 1], at=e)
        mwork = e
        dmat, e = place("dmat", [P, MH, P], at=mwork)
        scd, e = place("scd", [P, MH, P], at=e)
        itr, e = place("itr", [P, 2, P], at=e)
        kw, e = place("kw", [P, MH, DK], at=e)
        qi, e = place("qi", [P, 2, P], at=e)
        cst, e = place("cst", [P, 2, DV + 1], at=e)
        msq, e = place("msq", [P, MH * DV], at=e)
        sig0, _ = place("sig0", [P, N], at=J)
        sig1, _ = place("sig1", [P, N], at=J + 2048)
        sig = [sig0, sig1]
        assert e <= j_end, (e, j_end)
        G = j_end
        rawT, g_end = place("rawT", [P, 4, 3 + S], at=G)
        mh, _ = place("mh", [P, T, MH * DV], at=G)
        x1, _ = place("x1", [P, T, D], at=J)
        assert J + 4 * T * D <= g_end
        V = g_end
        kvs, e = place("kvs", [P, T, NKV], at=V)
        v_prev, e = place("v_prev", [P, T, KV * HD], at=e)
        kT, v_end = place("kT", [P, CHUNK + S], at=e)
        h2buf0, e = place("h2buf0", [P, D], at=V)
        h2buf1, e = place("h2buf1", [P, D], at=e)
        junk2, e = place("junk2", [P, D], at=e)
        h2buf = [h2buf0, h2buf1]
        assert e <= v_end
        E = v_end
        x_in0, e = place("x_in0", [P, D], at=E)
        x_in1, e = place("x_in1", [P, D], at=e)
        x_in2, e = place("x_in2", [P, D], at=e)
        x_in3, e = place("x_in3", [P, D], at=e)
        junk, e = place("junk", [P, D], at=e)
        mqraw0, e = place("mqraw0", [P, N], at=e)
        mqraw1, e = place("mqraw1", [P, N], at=e)
        prow, e = place("prow", [G_ROWS, P], at=e)
        grow, e = place("grow", [K, P], at=e)
        x_in, mqraw = [x_in0, x_in1, x_in2, x_in3], [mqraw0, mqraw1]
        qkT, e = place("qkT", [P, 4, S], at=E)
        mvx, e = place("mvx", [P, T, MH, DV + 1], at=e)
        bias, e = place("bias", [P, 2, N], at=E)
        qT0, e = place("qT0", [P, 4, P], at=e)
        qT1, e = place("qT1", [P, 4, P], at=e)
        prob0, e = place("prob0", [P, 8, P], at=e)
        prob1, e = place("prob1", [P, 8, P], at=e)
        pT0, e = place("pT0", [P, 8, P], at=e)
        aq0, e = place("aq0", [P, N], at=e)
        aq1, e = place("aq1", [P, N], at=e)
        qn, e = place("qn", [P, 4, KV, HD], at=e)
        sqb, e = place("sqb", [P, N], at=e)
        pq, e = place("pq", [P, N], at=e)
        pT1, e = place("pT1", [P, 8, P], at=e)
        qT, prob, pT, aqs = [qT0, qT1], [prob0, prob1], [pT0, pT1], [aq0, aq1]
        act_hi = [None, None]
        act_lo = [None, None]
        act_hi[0], e = place("act_hi0", [P, S], F32R, at=E)
        act_lo[0], e = place("act_lo0", [P, S], F32R, at=e)
        act_hi[1], e = place("act_hi1", [P, S], F32R, at=e)
        act_lo[1], e = place("act_lo1", [P, S], F32R, at=e)
        prod, e = place("prod", [P, S], at=e)
        silu0, e = place("silu0", [P, N], at=e)
        silu1, e = place("silu1", [P, N], at=e)
        silu = [silu0, silu1]

        bank = [ctx.enter_context(nc.psum_tensor(f"bank{i}", [P, N], F32)) for i in range(8)]

        x_half_s = sem("x_first_half_loaded")
        x_in_s = [sem(f"x_loaded{i}") for i in range(4)]
        ident_s = sem("ident_loaded")
        gmix_s = sem("g_mix_loaded")
        par_s = sem("params_loaded")
        late_s = sem("late_params_loaded")
        raw_s = [sem(f"raw_loaded{i}") for i in range(RAW)]
        w0_s = [sem(f"w0_loaded{i}") for i in range(K)]
        x1_s = [sem(f"x1_loaded{i}") for i in range(2)]
        gf_s = sem("g_ffn_loaded")
        out_s = sem("out_stored")
        ones_set = sem("ones_set")
        w0_hi = sem("w0_hi")
        w0_ready = sem("w0_ready")
        w_gained = sem("w_gained")
        w_hi_s = sem("w_hi_done")
        w_ready = sem("w_ready")
        unit_done = sem("unit_done")
        acc_free = [sem("acc_free0"), sem("acc_free1")]
        dve_step = sem("dve_step")
        act_step = sem("act_step")
        rstd_ready = sem("rstd_ready")
        nrstd_ready = sem("nrstd_ready")
        mix_tp = sem("g_mix_transposed")
        mix_ready = sem("g_mix_ready")
        h_tp = sem("h_transposed")
        h_hi = sem("h_hi")
        h_split = sem("h_split")
        cols_tp = sem("cols_transposed")
        cols_ready = sem("cols_ready")
        mq_tp = sem("mq_transposed")
        mq_evac = sem("mq_evac")
        conv_ready = sem("conv_ready")
        qk_ready = sem("qk_ready")
        kv_stat = sem("kv_stat")
        kv_rs = sem("kv_rs")
        kn_ready = sem("kn_ready")
        gate_mm = sem("gate_mm")
        kT_tp = sem("kT_transposed")
        gate_v = sem("gate_v")
        gate_a = sem("gate_a")
        nm_stored = sem("nm_stored")
        nm_s = [sem(f"nm_loaded{i}") for i in range(2)]
        sc_done = sem("sc_done")
        kt_done = sem("kt_done")
        d_exp = sem("d_exp")
        it_exp = sem("it_exp")
        d_masked = sem("d_masked")
        kw_ready = sem("kw_ready")
        scd_ready = sem("scd_ready")
        num_done = sem("num_done")
        cup_done = sem("cup_done")
        c_ready = sem("c_ready")
        sig_ready = sem("sig_ready")
        mh_ready = sem("mh_ready")
        ssb_done = sem("ssb_done")
        aq_ready = sem("aq_ready")
        q_stat = sem("q_stat")
        q_rs = sem("q_rs")
        qn_ready = sem("qn_ready")
        q_tp = sem("q_transposed")
        mh_tp = sem("mh_transposed")
        qT_ready = sem("qT_ready")
        mixb_hi = sem("mixb_hi")
        mixb_ready = sem("mixb_ready")
        s_kv0 = sem("scores_kv0")
        s_kv1 = sem("scores_kv1")
        s_evac = sem("scores_evac")
        s_max = sem("scores_max")
        p_exp = sem("p_exp")
        p_inv = sem("p_inverse_sum")
        p_ready = [sem("p_ready_kv0"), sem("p_ready_kv1")]
        pt_done = sem("p_transposed")
        pTa = sem("pT_act")
        pTd = sem("pT_dve")
        pv_done = sem("pv_done")
        v_zero = sem("v_zero")
        v_moved = sem("v_moved")
        sqa_done = sem("sqa_done")
        sqa_half = sem("sqa_half")
        sqa_added = sem("sqa_added")
        mixa_hi = sem("mixa_hi")
        mixa_ready = sem("mixa_ready")
        ssa_mm = sem("ssa_mm")
        ssa_ready = sem("ssa_ready")
        rmix_ready = sem("rmix_ready")
        wa_done = sem("wa_done")
        wb_done = sem("wb_done")
        wa_free = sem("wa_free")
        x1_ready = sem("x1_ready")
        r2_ready = sem("r2_ready")
        h2_ready = sem("h2_ready")
        h2_tp = sem("h2_transposed")
        h2_hi = sem("h2_hi")
        h2_split = sem("h2_split")
        gate_done = sem("gate_done")
        up_done = sem("up_done")
        silu_done = sem("silu_done")
        prod_done = sem("prod_done")
        act_hi_s = sem("act_hi_done")
        act_ready = sem("act_ready")
        down_mm = sem("down_mm")
        down_add = sem("down_add")

        def slice_source(n):
            g, k = 1 + n // K, n % K
            if g == 1:
                return [((0, 8), w_in_k[k, :, GATES:GATES + 8]),
                        ((8, NKV), w_in_k[k, :, AK:AK + 2 * KV * HD])]
            if g < 5:
                c = {2: MV, 3: MO, 4: AQ}[g]
                return [((0, N), w_in_k[k, :, c:c + N])]
            return [((0, N), w_out_k[k, :, (g - 5) * N:(g - 4) * N])]

        NS = 6 * K

        def raw_count(n):
            return sum(16 * len(slice_source(m)) for m in range(n % RAW, n + 1, RAW))

        SILU_AT = (T + 4, T + 6, 2 * T, 2 * T + 1)
        PARAMS = 10
        RAW_BASE = [raw_count(NS - RAW + r) for r in range(RAW)]
        FFN_RING = {"even": 8, "odd": 12, "down": 0}

        def strip_pieces(f, s):
            w = w_gate_k if s < 2 else w_up_k
            return w[:, 4 * (s % 2):4 * (s % 2) + 4, bass.ds(f * P, P)]

        def down_piece(f, half):
            return w_down_r[bass.ds(f * P, P), half * N:(half + 1) * N]

        def bcast(ap, n):
            return ap.unsqueeze(len(ap.shape)).to_broadcast(list(ap.shape) + [n])

        nm_dram = nc.dram_tensor("nm_rows", [T, MH * P], F32, kind="Internal").ap()

        block = ctx.enter_context(nc.Block())

        @block.sync
        def _(sp):
            def load_x(t):
                if t >= 4:
                    sp.wait_ge(h_tp, 2 * (t - 3))
                    sp.wait_ge(rstd_ready, t - 3)
                sp.dma_start(x_in[t % 4][:, :], x_t[t]).then_inc(x_in_s[t % 4], 16)

            sp.dma_start(ident[:, :], consts[:, C_ID:C_ID + P]).then_inc(ident_s, 16)
            sp.dma_start(x_in[0][:, 0:N], x_t[0][:, 0:N]).then_inc(x_half_s, 16)
            sp.dma_start(x_in[0][:, N:D], x_t[0][:, N:D]).then_inc(x_in_s[0], 16)
            sp.dma_start(grow[:, :], g_mix.rearrange("a (k p) -> (a k) p", p=P)).then_inc(gmix_s, 16)
            for k in range(K):
                sp.dma_start(w0_raw[:, k, :], w_in_k[k, :, MQ:MQ + N]).then_inc(w0_s[k], 16)
                if k in (3, 7):
                    load_x(1 + k // 4)
            sp.dma_start(tri[:, :], consts[:, C_TRI:C_TRI + P]).then_inc(par_s, 16)
            sp.dma_start(prow[G_CONV:G_CONV + 16, :],
                         conv_qk.rearrange("a i (f p) -> (a i f) p", p=P)).then_inc(par_s, 16)
            for i, g in enumerate((g_att, g_ml)):
                rows = slice(G_OUT + 4 * i, G_OUT + 4 * i + 4)
                sp.dma_start(prow[rows, :], g.rearrange("a (k p) -> (a k) p", p=P)).then_inc(par_s, 16)
            for half in range(2):
                sp.dma_start(prow[G_K:G_K + 1, half * HD:(half + 1) * HD], k_gain).then_inc(par_s, 16)
                sp.dma_start(prow[G_Q:G_Q + 1, half * HD:(half + 1) * HD], q_gain).then_inc(par_s, 16)
            sp.dma_start(bias_g[:, :], b_gates[0:1, :].to_broadcast([P, 8])).then_inc(par_s, 16)
            sp.dma_start(sinks8[:, :], sinks[0:1, :].to_broadcast([P, 8])).then_inc(par_s, 16)

            xt = 3
            def load_nm(t):
                if t >= 2:
                    sp.wait_ge(it_exp, t - 1)
                sp.dma_start(nm_b[t % 2][:, :], nm_dram[t:t + 1, :].to_broadcast([P, MH * P])).then_inc(nm_s[t % 2], 16)

            for n in range(NS):
                if n == 3 * K:
                    sp.wait_ge(gate_v, 5)
                    sp.dma_start(nm_dram.rearrange("t (h n) -> (t h) n", h=MH), nM[:, :]).then_inc(nm_stored, 16)
                    sp.wait_ge(nm_stored, 16)
                    load_nm(0)
                    load_nm(1)
                if 2 <= n - 3 * K < T:
                    load_nm(n - 3 * K)
                if n >= RAW:
                    sp.wait_ge(w_ready, n - RAW + 1)
                for (a, b), src in slice_source(n):
                    sp.dma_start(w_raw[:, n % RAW, a:b], src).then_inc(raw_s[n % RAW], 16)
                if xt < T:
                    load_x(xt)
                    xt += 1
                if n == 5 * K + 2:
                    sp.wait_ge(mh_tp, T)
                    for t in range(4, T):
                        sp.dma_start(x1[:, t, :], x_t[t]).then_inc(x1_s[1], 16)
                if n == 4 * K + 4:
                    sp.wait_ge(mh_ready, T)
                    sp.wait_ge(num_done, T)
                    for i, c in enumerate((C_FIRST, C_BIAS)):
                        sp.dma_start(bias[:, i, :], consts[:, c:c + N]).then_inc(late_s, 16)
                    sp.wait_ge(ssb_done, T)
                    for t in range(4):
                        sp.dma_start(x1[:, t, :], x_t[t]).then_inc(x1_s[0], 16)
                    sp.dma_start(g_row[:, :], g_ffn[0:1, :].to_broadcast([P, D])).then_inc(gf_s, 16)

            def ffn_load(source, m, count):
                sp.wait_ge(w_ready, count + (m - RAW + 1))
                dst = w_raw[:, m % RAW, :]
                if len(source.shape) == 3:
                    dst = dst.rearrange("p (k n) -> p k n", k=4)
                sp.dma_start(dst, source).then_inc(raw_s[m % RAW], 16)

            for f in range(2):
                for s in range(4):
                    ffn_load(strip_pieces(f, s), 4 * f + s, NS)
            with sp.Fori(1, PAIRS) as i:
                count = NS + 8 + (i - 1) * 12
                for s in range(4):
                    ffn_load(strip_pieces(2 * i, s), s, count)
                for s in range(4):
                    ffn_load(down_piece(2 * i - 2 + s % 2, s // 2), 4 + s, count)
                for s in range(4):
                    ffn_load(strip_pieces(2 * i + 1, s), 8 + s, count)
            for s in range(4):
                ffn_load(down_piece(F - 2 + s % 2, s // 2), s, NS + 8 + 12 * (PAIRS - 1))

            for m in range(2 * T):
                sp.wait_ge(down_add, 2 * T * (PAIRS - 1) + m + 1)
                t, half = m % T, m // T
                sp.dma_start(out_t[t, :, half * N:(half + 1) * N],
                             x1[:, t, half * N:(half + 1) * N]).then_inc(out_s, 16)
            sp.wait_ge(out_s, 16 * 2 * T)

        @block.gpsimd
        def _(pool):
            def split(ring, raw, width, loaded, n, gain=None):
                pool.wait_ge(raw_s[raw], loaded)
                if gain is not None:
                    nc.gpsimd.tensor_tensor(w_raw[:, raw, 0:width], w_raw[:, raw, 0:width],
                                            gain.to_broadcast([P, width]), ALU.mult).then_inc(w_gained, 1)
                    pool.wait_ge(w_gained, n + 1)
                nc.gpsimd.tensor_tensor(w_hi[:, ring, 0:width], w_raw[:, raw, 0:width],
                                        ones[:, 0:1].to_broadcast([P, width]), ALU.mult).then_inc(w_hi_s, 1)
                pool.wait_ge(w_hi_s, n + 1)
                nc.gpsimd.tensor_tensor(w_lo[:, ring, 0:width], w_raw[:, raw, 0:width],
                                        w_hi[:, ring, 0:width].bitcast(F32), ALU.subtract).then_inc(w_ready, 1)

            def mask(t):
                pool.wait_ge(d_exp, t + 1)
                nc.gpsimd.affine_select(out=dmat[:, :, :], in_=dmat[:, :, :], pattern=[[0, MH], [1, P]],
                                        compare_op=ALU.is_ge, fill=0.0, base=0,
                                        channel_multiplier=-1).then_inc(d_masked, 1)

            def normalise(t):
                pool.wait_ge(p_inv, t + 1)
                nc.gpsimd.tensor_tensor(prob[t % 2][:, 0:4, :], prob[t % 2][:, 0:4, :], bcast(dsum[:, 0:4], P),
                                        ALU.mult).then_inc(p_ready[0], 1)

            def add_squares(t):
                pool.wait_ge(sqa_done, t + 1)
                nc.gpsimd.tensor_tensor(sqb[:, 0:2 * P], sqb[:, 0:2 * P], sqb[:, 2 * P:4 * P],
                                        ALU.add).then_inc(sqa_half, 1)
                pool.wait_ge(sqa_half, t + 1)
                nc.gpsimd.tensor_tensor(sqb[:, 0:P], sqb[:, 0:P], sqb[:, P:2 * P],
                                        ALU.add).then_inc(sqa_added, 1)

            pool.wait_ge(ones_set, 1)
            pool.wait_ge(mix_ready, 1)
            for n in range(NS):
                g = 1 + n // K
                if g >= 2 and n % K == 0:
                    pool.wait_ge(unit_done, (g - 1) * T)
                c = (G_OUT if g >= 5 else G_MIX) + n % K
                gain = cols[:, c:c + 1]
                if n == 4 * K:
                    pool.wait_ge(cols_ready, 1)
                split((g * K + n % K) % RING, n % RAW, NKV if g == 1 else N, raw_count(n), n, gain)
                if g == 4:
                    mask(n % K)
                if 0 <= n - 4 * K - 2 < T:
                    normalise(n - 4 * K - 2)
                if 0 <= n - 4 * K - 4 < T:
                    add_squares(n - 4 * K - 4)

            def ffn_split(kind, s, m, base_n, loads):
                split(FFN_RING[kind] + s, m % RAW, N, RAW_BASE[m % RAW] + 16 * (loads + m // RAW + 1),
                      base_n + m)

            pool.wait_ge(wb_done, T)
            for f in range(2):
                for s in range(4):
                    ffn_split(("even", "odd")[f], s, 4 * f + s, NS, 0)
            pool.wait_ge(wb_done, 2 * T)
            pool.wait_ge(up_done, 3)
            with pool.Fori(1, PAIRS) as i:
                base_n = NS + 8 + (i - 1) * 12
                loads = 4 + (i - 1) * 6
                pool.wait_ge(up_done, 4 * i - 2)
                for s in range(4):
                    ffn_split("even", s, s, base_n, loads)
                pool.wait_ge(up_done, 4 * i - 1)
                for s in range(4):
                    ffn_split("down", s, 4 + s, base_n, loads)
                pool.wait_ge(up_done, 4 * i)
                for s in range(4):
                    ffn_split("odd", s, 8 + s, base_n, loads)
            pool.wait_ge(down_mm, 2 * T * (PAIRS - 1))
            for s in range(4):
                ffn_split("down", s, s, NS + 8 + 12 * (PAIRS - 1), 4 + 6 * (PAIRS - 1))

        @block.tensor
        def _(pe):
            def three(ps, x_hi, x_lo, wh, wl, first, last):
                nc.tensor.matmul(ps, x_hi, wh, start=first, stop=False)
                nc.tensor.matmul(ps, x_hi, wl, start=False, stop=False)
                return nc.tensor.matmul(ps, x_lo, wh, start=False, stop=last)

            def transpose_tile(src, t, tp, split_s):
                for b in range(2):
                    if t >= 1:
                        pe.wait_ge(split_s, 2 * (t - 1) + b + 1)
                    if tp is h_tp:
                        if t == 0 and b == 0:
                            pe.wait_ge(x_half_s, 16)
                        else:
                            pe.wait_ge(x_in_s[t % 4], 16 * (t // 4 + 1))
                    elif b == 0:
                        pe.wait_ge(h2_ready, t + 1)
                    for j in range(4):
                        last = nc.tensor.transpose(bank[2 + b][:, j * P:(j + 1) * P],
                                                   src[t % len(src)][:, (4 * b + j) * P:(4 * b + j + 1) * P],
                                                   ident[:, :])
                    last.then_inc(tp, 1)

            def unit(U):
                g, t = U // T, U % T
                width = NKV if g == 1 else N
                ps = bank[U % 2][:, 0:width]
                if U >= 2:
                    pe.wait_ge(acc_free[U % 2], U // 2)
                for k in range(K):
                    if g == 0 and k % 4 == 0:
                        pe.wait_ge(h_split, 2 * t + k // 4 + 1)
                    if U == 0 and k == K // 2:
                        transpose_tile(x_in, 1, h_tp, h_split)
                    if t == 0:
                        if g == 0:
                            pe.wait_ge(w0_ready, k + 1)
                        else:
                            pe.wait_ge(w_ready, (g - 1) * K + k + 1)
                    r = (g * K + k) % RING
                    a = slice(t * P, (t + 1) * P)
                    last = three(ps, actT_hi[:, k, a], actT_lo[:, k, a], w_hi[:, r, 0:width],
                                 w_lo[:, r, 0:width], k == 0, k == K - 1)
                last.then_inc(unit_done, 1)

            def mq_transposes(t):
                pe.wait_ge(acc_free[t % 2], t // 2 + 1)
                if t >= 1:
                    pe.wait_ge(mq_evac, t)
                for f in range(4):
                    last = nc.tensor.transpose(bank[4][:, f * P:(f + 1) * P],
                                               mqraw[t % 2][:, f * P:(f + 1) * P], ident[:, :])
                last.then_inc(mq_tp, 1)

            def mlstm_scores(t):
                if t >= 1:
                    pe.wait_ge(scd_ready, t)
                a = slice(t * P, (t + 1) * P)
                for h in range(MH):
                    rows = slice((h % 2) * DK, (h % 2 + 1) * DK)
                    last = nc.tensor.matmul(bank[4 + h % 2][:, (h // 2) * P:(h // 2 + 1) * P],
                                            qkT[rows, 2 + h // 2, a], qkT[rows, h // 2, a], start=True, stop=True)
                last.then_inc(sc_done, 1)
                if t == T - 1:
                    return
                if t >= 1:
                    pe.wait_ge(kw_ready, t)
                for p in range(2):
                    last = nc.tensor.transpose(bank[2][:, p * P:(p + 1) * P], qkT[:, 2 + p, a], ident[:, :])
                last.then_inc(kt_done, 1)

            def mlstm_products(t):
                pe.wait_ge(scd_ready, t + 1)
                pe.wait_ge(c_ready, t + 1)
                if t >= 1:
                    pe.wait_ge(mh_ready, t)
                for h in range(MH):
                    rows = slice((h % 2) * DK, (h % 2 + 1) * DK)
                    ps = bank[6 + h % 2][:, (h // 2) * (DV + 1):(h // 2 + 1) * (DV + 1)]
                    last = nc.tensor.matmul(ps, scd[:, h, :], mvx[:, t, h, :], start=True, stop=t == 0)
                    if t >= 1:
                        last = nc.tensor.matmul(ps, qi[rows, h // 2, :], cst[rows, h // 2, :],
                                                start=False, stop=True)
                last.then_inc(num_done, 1)
                if t == T - 1:
                    return
                for h in range(MH):
                    rows = slice((h % 2) * DK, (h % 2 + 1) * DK)
                    last = nc.tensor.matmul(bank[3][rows, (h // 2) * (DV + 1):(h // 2 + 1) * (DV + 1)],
                                            kw[:, h, :], mvx[:, t, h, :], start=True, stop=True)
                last.then_inc(cup_done, 1)

            def att_sumsq(t):
                pe.wait_ge(sqa_added, t + 1)
                if t >= 1:
                    pe.wait_ge(ssa_ready, t)
                pe.wait_ge(mixb_ready, min(t + 5, T))
                nc.tensor.matmul(bank[3][:, 0:1], sqb[:, 0:P], ones[:, 0:1], start=True,
                                 stop=True).then_inc(ssa_mm, 1)

            def att_transposes(t):
                pe.wait_ge(qn_ready, t + 1)
                if t >= 4:
                    pe.wait_ge(mixa_ready, t - 3)
                blocks = bank[2][:, :].rearrange("p (b c i n) -> p b c i n", b=2, c=2, i=2)
                for i in range(4):
                    last = nc.tensor.transpose(blocks[:, i // 2, :, i % 2, :],
                                               qn[:, i, :, :].rearrange("p a b -> p (a b)"), ident[:, :])
                last.then_inc(q_tp, 1)
                if t >= 1:
                    pe.wait_ge(mixb_ready, t)
                if t >= 5:
                    pe.wait_ge(ssa_ready, t - 4)
                for kk in range(4):
                    last = nc.tensor.transpose(bank[3][:, kk * P:(kk + 1) * P],
                                               mh[:, t, kk * P:(kk + 1) * P], ident[:, :])
                last.then_inc(mh_tp, 1)

            def att_scores(t):
                pe.wait_ge(qT_ready, t + 1)
                if t >= 1:
                    pe.wait_ge(s_evac, t)
                q = qT[t % 2]
                for c2 in range(2):
                    start = t * P + c2 * CHUNK
                    for b in range(2):
                        o = (c2 * 2 + b) * P
                        for kv, done in ((0, s_kv0), (1, s_kv1)):
                            rows = slice(kv * HD, (kv + 1) * HD)
                            last = nc.tensor.matmul(bank[4 + kv][:, o:o + P], q[rows, 2 * b + c2, :],
                                                    kT[rows, start:start + P], start=True, stop=True)
                            if (c2, b) == (1, 1):
                                last.then_inc(done, 1)

            def att_prob_transposes(t):
                for kv in range(KV):
                    pe.wait_ge(p_ready[kv], t + 1)
                    if t >= 1:
                        pe.wait_ge((pTa, pTd)[kv], t)
                    for j in range(4):
                        last = nc.tensor.transpose(bank[6 + kv][:, j * P:(j + 1) * P],
                                                   prob[t % 2][:, kv * 4 + j, :], ident[:, :])
                last.then_inc(pt_done, 1)

            def att_values(t):
                pe.wait_ge(pTa, t + 1)
                pe.wait_ge(pTd, t + 1)
                if t == 0:
                    pe.wait_ge(v_zero, 1)
                    pe.wait_ge(v_moved, 16 * 2)
                pe.wait_ge(qT_ready, min(t + 4, T))
                if t >= 1:
                    pe.wait_ge(mixa_ready, t)
                for c2 in range(2):
                    for kv in range(KV):
                        if c2 == 0:
                            v = v_prev[:, t, kv * HD:(kv + 1) * HD]
                        else:
                            v = kvs[:, t, 2 * MH + (KV + kv) * HD:2 * MH + (KV + kv + 1) * HD]
                        for i2 in range(2):
                            rows = slice(i2 * HD, (i2 + 1) * HD)
                            b0 = kv * 4 + c2 * 2
                            rhs = pT[t % 2][:, b0:b0 + 2, i2 * CHUNK:(i2 + 1) * CHUNK]
                            o = bank[2][rows, kv * 2 * P:(kv + 1) * 2 * P].rearrange("p (b n) -> p b n", b=2)
                            last = nc.tensor.matmul(o[:, :, c2 * CHUNK:(c2 + 1) * CHUNK], v, rhs,
                                                    start=True, stop=True)
                last.then_inc(pv_done, 1)

            def out_unit(U):
                j = U - UNITS
                g, t = U // T, U % T
                pe.wait_ge(mixa_ready, t + 1)
                pe.wait_ge(mixb_ready, t + 1)
                a = slice(t * P, (t + 1) * P)
                for part, done in ((0, wa_done), (1, wb_done)):
                    if j == 0:
                        pe.wait_ge(acc_free[part], UNITS // 2)
                    else:
                        pe.wait_ge((wa_free, x1_ready)[part], j)
                    for kk in range(4):
                        k = part * 4 + kk
                        if t == 0:
                            pe.wait_ge(w_ready, (g - 1) * K + k + 1)
                        r = (g * K + k) % RING
                        last = three(bank[part][:, :], actT_hi[:, k, a], actT_lo[:, k, a], w_hi[:, r, :],
                                     w_lo[:, r, :], kk == 0, kk == 3)
                    last.then_inc(done, 1)

            def keep_warm(n):
                for _ in range(n):
                    nc.tensor.matmul(bank[7][:, 0:P], ones[:, :], ones[:, :], start=True, stop=True)

            pe.wait_ge(ones_set, 1)
            keep_warm(6)
            pe.wait_ge(ident_s, 16)
            transpose_tile(x_in, 0, h_tp, h_split)
            pe.wait_ge(gmix_s, 16)
            nc.tensor.transpose(bank[4][:, 0:K], grow[:, :], ident[0:K, 0:K]).then_inc(mix_tp, 1)
            keep_warm(5)
            for U in range(ALL):
                g, t = U // T, U % T
                if U < UNITS:
                    unit(U)
                else:
                    out_unit(U)
                if U + 2 < T:
                    transpose_tile(x_in, U + 2, h_tp, h_split)
                if U == 0:
                    pe.wait_ge(mix_ready, 1)
                    pe.wait_ge(par_s, 16 * PARAMS)
                    nc.tensor.transpose(bank[4][:, 0:G_ROWS], prow[:, :],
                                        ident[0:G_ROWS, 0:G_ROWS]).then_inc(cols_tp, 1)
                if U == 1:
                    pe.wait_ge(cols_ready, 1)
                if 1 <= U <= T:
                    mq_transposes(U - 1)
                if U == 2 * T + 2:
                    pe.wait_ge(kn_ready, 1)
                    for b in range(2):
                        for j in range(4):
                            last = nc.tensor.transpose(bank[2 + b][:, j * P:(j + 1) * P],
                                                       kvs[:, 4 * b + j, 2 * MH:2 * MH + KV * HD], ident[:, :])
                    last.then_inc(kT_tp, 1)
                    pe.wait_ge(gate_v, 2)
                    nc.tensor.matmul(bank[5][:, 0:32], tri[:, :], lf[:, :], start=True, stop=True)
                    nc.tensor.matmul(bank[5][:, 32:64], ones[:, :], lf[:, :], start=True,
                                     stop=True).then_inc(gate_mm, 1)
                if U == 2 * T + 3:
                    pe.wait_ge(gate_v, 3)
                    nc.tensor.transpose(bank[6][0:32, 0:P], u_col[:, :], ident[:, :]).then_inc(gate_mm, 1)
                if U == 2 * T + 4:
                    pe.wait_ge(gate_v, 4)
                    nc.tensor.matmul(bank[7][:, 0:32], ones[0:32, :], diag[:, :], start=True,
                                     stop=True).then_inc(gate_mm, 1)
                if U == 2 * T + 5:
                    pe.wait_ge(gate_v, 5)
                    nc.tensor.transpose(bank[6][:, 0:32], nM[:, :], ident[0:32, 0:32]).then_inc(gate_mm, 1)
                s = U - 3 * T
                if s == 0:
                    pe.wait_ge(gate_v, 6)
                    pe.wait_ge(qk_ready, 4)
                    pe.wait_ge(acc_free[1], 3 * T // 2)
                if 1 <= s <= T:
                    mlstm_products(s - 1)
                if 0 <= s < T:
                    mlstm_scores(s)
                s = U - 4 * T
                if s == 1:
                    pe.wait_ge(c_ready, T)
                    pe.wait_ge(mh_ready, T)
                if 0 <= s - 1 < T:
                    att_transposes(s - 1)
                if 0 <= s - 2 < T:
                    att_scores(s - 2)
                if 0 <= s - 3 < T:
                    att_prob_transposes(s - 3)
                if 0 <= s - 5 < T:
                    att_sumsq(s - 5)
                if 0 <= s - 4 < T:
                    att_values(s - 4)
                s = U - 6 * T
                if s == 2:
                    pe.wait_ge(ssa_ready, T)
                if 0 <= s - 2:
                    transpose_tile(h2buf, s - 2, h2_tp, h2_split)

            def strip(kind, half, m, w_ready_at, free_at):
                free, done = ((silu_done, gate_done), (prod_done, up_done))[m]
                if free_at is not None:
                    pe.wait_ge(free, free_at)
                a = slice(half * N, (half + 1) * N)
                for k in range(K):
                    r = FFN_RING[kind] + 2 * m + k // 4
                    if half == 0 and k % 4 == 0:
                        pe.wait_ge(w_ready, w_ready_at + 2 * m + k // 4 + 1)
                    c = slice((k % 4) * P, (k % 4 + 1) * P)
                    last = three(bank[2 * half + m][:, :], w_hi[:, r, c], w_lo[:, r, c], actT_hi[:, k, a],
                                 actT_lo[:, k, a], k == 0, k == K - 1)
                last.then_inc(done, 1)

            def down(count, w_ready_at, ready):
                for half in range(2):
                    for t in range(T):
                        m = half * T + t
                        ps = bank[4 + m % 4][:, :]
                        if half == 0 and t % 4 == 0:
                            pe.wait_ge(act_ready, ready + t // 4 - 1)
                        if m >= 4:
                            pe.wait_ge(down_add, count + m - 3)
                        a = slice(t * P, (t + 1) * P)
                        for j in range(2):
                            r = FFN_RING["down"] + 2 * half + j
                            if t == 0:
                                pe.wait_ge(w_ready, w_ready_at + 2 * half + j + 1)
                            last = three(ps, act_hi[j][:, a], act_lo[j][:, a], w_hi[:, r, :], w_lo[:, r, :],
                                         j == 0, j == 1)
                        last.then_inc(down_mm, 1)

            pe.wait_ge(x1_ready, 2 * T)
            pe.wait_ge(h2_split, T)
            strip("even", 0, 0, NS, None)
            transpose_tile(h2buf, T - 2, h2_tp, h2_split)
            strip("even", 0, 1, NS, None)
            strip("odd", 0, 0, NS + 4, 1)
            transpose_tile(h2buf, T - 1, h2_tp, h2_split)
            strip("odd", 0, 1, NS + 4, 1)
            pe.wait_ge(h2_split, 2 * T)
            for m in range(2):
                strip("even", 1, m, NS, None)
            for m in range(2):
                strip("odd", 1, m, NS + 4, 3)
            with pe.Fori(1, PAIRS) as i:
                w_at = NS + 8 + (i - 1) * 12
                for half in range(2):
                    for m in range(2):
                        strip("even", half, m, w_at, 4 * i + half - 1)
                down((i - 1) * (2 * T), w_at + 4, 4 * i)
                for half in range(2):
                    for m in range(2):
                        strip("odd", half, m, w_at + 8, 4 * i + half + 1)
            down(2 * T * (PAIRS - 1), NS + 8 + 12 * (PAIRS - 1), 4 * PAIRS)

        @block.scalar
        def _(act):
            steps = [0]

            def step(ins):
                steps[0] += 1
                ins.then_inc(act_step, 1)

            def link(ins):
                step(ins)
                act.wait_ge(act_step, steps[0])

            def settle():
                act.wait_ge(act_step, steps[0])

            def inverse_root(out_, sumsq, n):
                link(nc.scalar.activation(out_, sumsq, ACT.Ln, bias=eps_t[0:sumsq.shape[0], 0:1], scale=1.0 / n))
                return nc.scalar.activation(out_, out_, ACT.Exp, scale=-0.5)

            eps_t = cols[:, G_EPS:G_EPS + 1]

            def stats(t):
                act.wait_ge(x_in_s[t % 4], 16 * (t // 4 + 1))
                if t == 0:
                    act.wait_ge(x_half_s, 16)
                    act.wait_ge(gate_v, 1)
                link(nc.scalar.activation(junk[:, :], x_in[t % 4][:, :], ACT.Square, accum_out=stat[:, t:t + 1]))
                inverse_root(rstd[:, t:t + 1], stat[:, t:t + 1], D).then_inc(rstd_ready, 1)

            def high_bank(t, b, tp, done):
                act.wait_ge(tp, 2 * t + b + 1)
                nc.scalar.activation(actT_hi[:, 4 * b:4 * b + 4, t * P:(t + 1) * P],
                                     bank[2 + b][:, :].rearrange("p (k n) -> p k n", k=4),
                                     ACT.Copy).then_inc(done, 1)

            def high_part(t, tp, done):
                for b in range(2):
                    high_bank(t, b, tp, done)

            def w0_high(k):
                act.wait_ge(w0_s[k], 16)
                nc.scalar.activation(w_hi[:, k, :], w0_raw[:, k, :], ACT.Copy,
                                     scale=cols[:, G_MIX + k:G_MIX + k + 1]).then_inc(w0_hi, 1)

            nc.scalar.preload_act_table_set("natural_log_exp_and_others")
            high_bank(0, 0, h_tp, h_hi)
            act.wait_ge(mix_ready, 1)
            w0_high(0)
            w0_high(1)
            high_bank(0, 1, h_tp, h_hi)
            for k in range(2, K):
                w0_high(k)
            high_part(1, h_tp, h_hi)
            stats(0)
            stats(1)

            def evacuate(U):
                g, t = U // T, U % T
                ps = bank[U % 2]
                act.wait_ge(unit_done, U + 1)
                free = acc_free[U % 2]
                if g == 0:
                    act.wait_ge(rstd_ready, t + 1)
                r_ = rstd[:, t:t + 1]
                if g == 0:
                    if t >= 2:
                        act.wait_ge(mq_tp, t - 1)
                    nc.scalar.activation(mqraw[t % 2][:, :], ps[:, :], ACT.Copy, scale=r_).then_inc(free, 1)
                elif g == 1:
                    nc.scalar.activation(kvs[:, t, :], ps[:, 0:NKV], ACT.Copy, scale=r_).then_inc(free, 1)
                elif g == 2:
                    if t == 0:
                        act.wait_ge(mq_tp, T)
                        act.wait_ge(h_tp, 2 * T)
                    nc.scalar.activation(mvx[:, t, :, 0:DV], ps[:, :].rearrange("p (h d) -> p h d", h=MH),
                                         ACT.Copy, scale=r_).then_inc(free, 1)
                elif g == 3:
                    if t == 0:
                        act.wait_ge(gate_v, 6)
                    if t >= 2:
                        act.wait_ge(mh_ready, t - 1)
                    if t == 0:
                        act.wait_ge(nrstd_ready, 1)
                    nc.scalar.activation(sig[t % 2][:, :], ps[:, :], ACT.Exp, scale=nrstd[:, t:t + 1]).then_inc(free, 1)
                else:
                    if t == 0:
                        act.wait_ge(num_done, T)
                    if t >= 1:
                        act.wait_ge(q_stat, t)
                    step(nc.scalar.activation(pq[:, :], ps[:, :], ACT.Square, scale=r_))
                    if t >= 2:
                        act.wait_ge(qn_ready, t - 1)
                    nc.scalar.activation(aqs[t % 2][:, :], ps[:, :], ACT.Copy, scale=r_).then_inc(free, 1)

            for U in range(ALL):
                g, t = U // T, U % T
                if U < UNITS:
                    evacuate(U)
                if U + 2 < T:
                    high_part(U + 2, h_tp, h_hi)
                    stats(U + 2)
                if U in SILU_AT:
                    f = SILU_AT.index(U)
                    act.wait_ge(conv_ready, f + 1)
                    nc.scalar.activation(qkT[:, f, :], qkT[:, f, :], ACT.Silu).then_inc(qk_ready, 1)
                if U == SILU_AT[-1]:
                    nc.scalar.preload_act_table_set("natural_log_exp_and_others")
                if U == 2 * T:
                    vcols = slice(2 * MH + KV * HD, 2 * MH + 2 * KV * HD)
                    act.wait_ge(acc_free[0], T)
                    act.wait_ge(acc_free[1], T)
                    act.dma_start(v_prev[CHUNK:P, :, :], kvs[0:CHUNK, :, vcols]).then_inc(v_moved, 16)
                    act.dma_start(v_prev[0:CHUNK, 1:T, :], kvs[CHUNK:P, 0:T - 1, vcols]).then_inc(v_moved, 16)
                if U == 2 * T + 1:
                    act.wait_ge(kv_stat, 1)
                    inverse_root(krs[:, :], kss[:, :], HD).then_inc(kv_rs, 1)
                    act.wait_ge(kv_stat, 2)
                    link(nc.scalar.activation(expf[:, :], absf[:, :], ACT.Exp, scale=-1.0))
                    nc.scalar.activation(expf[:, :], expf[:, :], ACT.Ln, bias=1.0).then_inc(gate_a, 1)
                if U == 2 * T + 5:
                    act.wait_ge(gate_v, 5)
                    step(nc.scalar.activation(aold[:, :], aold[:, :], ACT.Exp))
                    nc.scalar.activation(wexp[:, :], wexp[:, :], ACT.Exp).then_inc(gate_a, 1)
                if U == 2 * T + 6:
                    act.wait_ge(kv_stat, 3)
                    nc.scalar.activation(enm[:, :], enm[:, :], ACT.Exp).then_inc(gate_a, 1)
                s = U - 3 * T
                if 0 <= s < T:
                    act.wait_ge(nm_s[s % 2], 16 * (s // 2 + 1))
                    if s >= 1:
                        act.wait_ge(scd_ready, s)
                    for h in range(MH):
                        c = s * MH + h
                        last = nc.scalar.activation(dmat[:, h, :], nm_b[s % 2][:, h * P:(h + 1) * P], ACT.Exp,
                                                    bias=u_col[:, c:c + 1])
                    last.then_inc(d_exp, 1)
                    for h in range(MH):
                        rows = slice((h % 2) * DK, (h % 2 + 1) * DK)
                        last = nc.scalar.activation(itr[rows, h // 2, :], nm_b[s % 2][rows, h * P:(h + 1) * P],
                                                    ACT.Exp, bias=mm[rows, s, h:h + 1])
                    last.then_inc(it_exp, 1)
                if 1 <= s <= T:
                    act.wait_ge(mh_ready, s)
                    if s == 1:
                        act.wait_ge(it_exp, s)
                    nc.scalar.activation(msq[:, :], mh[:, s - 1, :], ACT.Square,
                                         accum_out=ss2[:, s - 1, 1:2]).then_inc(ssb_done, 1)
                    act.wait_ge(ssb_done, s)
                s = U - 4 * T
                if 0 <= s - 1 < T:
                    tt = s - 1
                    act.wait_ge(q_tp, tt + 1)
                    if tt >= 2:
                        act.wait_ge(s_kv1, tt - 1)
                    nc.scalar.activation(qT[tt % 2][:, :, :], bank[2][:, :].rearrange("p (k n) -> p k n", k=4),
                                         ACT.Copy, scale=cols[:, G_Q:G_Q + 1]).then_inc(qT_ready, 1)
                    act.wait_ge(mh_tp, tt + 1)
                    nc.scalar.activation(actT_hi[:, 4:8, tt * P:(tt + 1) * P],
                                         bank[3][:, :].rearrange("p (k n) -> p k n", k=4),
                                         ACT.Copy).then_inc(mixb_hi, 1)
                if 0 <= s < T:
                    act.wait_ge(q_stat, s + 1)
                    if s >= 1:
                        act.wait_ge(qn_ready, s)
                    inverse_root(qrs[:, :], qss[:, :], HD).then_inc(q_rs, 1)
                if 0 <= s - 3 < T:
                    tt = s - 3
                    act.wait_ge(pt_done, tt + 1)
                    if tt >= 2:
                        act.wait_ge(pv_done, tt - 1)
                    nc.scalar.activation(pT[tt % 2][:, 0:4, :], bank[6][:, :].rearrange("p (k n) -> p k n", k=4),
                                         ACT.Copy).then_inc(pTa, 1)
                if 0 <= s - 4 < T:
                    tt = s - 4
                    act.wait_ge(pv_done, tt + 1)
                    if tt >= 1:
                        act.wait_ge(ssa_mm, tt)
                    nc.scalar.activation(sqb[:, :], bank[2][:, :], ACT.Square).then_inc(sqa_done, 1)
                    nc.scalar.activation(actT_hi[:, 0:4, tt * P:(tt + 1) * P],
                                         bank[2][:, :].rearrange("p (k n) -> p k n", k=4),
                                         ACT.Copy).then_inc(mixa_hi, 1)
                if 0 <= s - 2 < T:
                    tt = s - 2
                    act.wait_ge(s_max, tt + 1)
                    if tt >= 1:
                        act.wait_ge(p_ready[0], tt)
                        act.wait_ge(p_ready[1], tt)
                    for j in range(8):
                        step(nc.scalar.activation(prob[tt % 2][:, j, :], prob[tt % 2][:, j, :], ACT.Exp, bias=nmx[:, j:j + 1],
                                                  accum_out=dsum[:, j:j + 1]))
                    nc.scalar.activation(esk[:, :], esk[:, :], ACT.Exp).then_inc(p_exp, 1)
                if 0 <= s - 6 < T:
                    tt = s - 6
                    act.wait_ge(ssa_ready, tt + 1)
                    inverse_root(rmix[:, tt, :], ss2[:, tt, :], N).then_inc(rmix_ready, 1)
                s = U - 6 * T
                if s >= 0:
                    act.wait_ge(x1_ready, T + s + 1)
                    if s == 0:
                        act.wait_ge(pv_done, T)
                    link(nc.scalar.activation(junk2[:, :], x1[:, s, :], ACT.Square, accum_out=stat[:, s:s + 1]))
                    inverse_root(rstd[:, s:s + 1], stat[:, s:s + 1], D).then_inc(r2_ready, 1)
                    if s >= 2:
                        high_part(s - 2, h2_tp, h2_hi)

            def silu_half(half, count, read=None):
                act.wait_ge(gate_done, count)
                if read is not None:
                    act.wait_ge(prod_done, read)
                nc.scalar.activation(silu[half][:, :], bank[2 * half][:, :], ACT.Silu).then_inc(silu_done, 1)

            def high_half(j, half, count):
                act.wait_ge(prod_done, count)
                a = slice(half * N, (half + 1) * N)
                nc.scalar.activation(act_hi[j][:, a], prod[:, a], ACT.Copy).then_inc(act_hi_s, 1)

            act.wait_ge(mixa_ready, T)
            silu_half(0, 1)
            high_part(T - 2, h2_tp, h2_hi)
            high_half(0, 0, 1)
            silu_half(0, 2, 1)
            high_part(T - 1, h2_tp, h2_hi)
            high_half(1, 0, 2)
            silu_half(1, 3)
            high_half(0, 1, 3)
            silu_half(1, 4, 3)
            high_half(1, 1, 4)
            with act.Fori(1, PAIRS) as i:
                silu_half(0, 4 * i + 1, 4 * i - 1)
                silu_half(1, 4 * i + 2, 4 * i)
                act.wait_ge(down_mm, 2 * T * i)
                high_half(0, 0, 4 * i + 1)
                high_half(0, 1, 4 * i + 2)
                silu_half(0, 4 * i + 3, 4 * i + 1)
                high_half(1, 0, 4 * i + 3)
                silu_half(1, 4 * i + 4, 4 * i + 2)
                high_half(1, 1, 4 * i + 4)

        @block.vector
        def _(dve):
            steps = [0]
            V_ = nc.vector

            def step(ins):
                steps[0] += 1
                ins.then_inc(dve_step, 1)

            def link(ins):
                step(ins)
                dve.wait_ge(dve_step, steps[0])

            def low_bank(t, b, hi_s, done):
                dve.wait_ge(hi_s, 2 * t + b + 1)
                V_.tensor_tensor(actT_lo[:, 4 * b:4 * b + 4, t * P:(t + 1) * P],
                                 bank[2 + b][:, :].rearrange("p (k n) -> p k n", k=4),
                                 actT_hi[:, 4 * b:4 * b + 4, t * P:(t + 1) * P].bitcast(F32),
                                 ALU.subtract).then_inc(done, 1)

            def low_part(t, hi_s, done):
                for b in range(2):
                    low_bank(t, b, hi_s, done)

            def normed(t):
                dve.wait_ge(r2_ready, t + 1)
                if t >= 2:
                    dve.wait_ge(h2_tp, 2 * (t - 1))
                V_.scalar_tensor_tensor(h2buf[t % 2][:, :], x1[:, t, :], rstd[:, t:t + 1], g_row[:, :],
                                        ALU.mult, ALU.mult).then_inc(h2_ready, 1)

            def w0_low(k):
                dve.wait_ge(w0_hi, k + 1)
                V_.scalar_tensor_tensor(w_lo[:, k, :], w0_raw[:, k, :], cols[:, G_MIX + k:G_MIX + k + 1],
                                        w_hi[:, k, :].bitcast(F32), ALU.mult, ALU.subtract).then_inc(w0_ready, 1)

            V_.memset(cols[:, G_EPS:G_EPS + 1], EPS).then_inc(gate_v, 1)
            V_.memset(ones[:, :], 1.0).then_inc(ones_set, 1)
            step(V_.memset(rawT[:, :, 0:3], 0.0))
            step(V_.memset(mm[:, 0, :], 0.0))
            dve.wait_ge(mix_tp, 1)
            V_.tensor_copy(cols[:, G_MIX:G_MIX + K], bank[4][:, 0:K]).then_inc(mix_ready, 1)
            dve.wait_ge(mix_ready, 1)
            low_bank(0, 0, h_hi, h_split)
            w0_low(0)
            w0_low(1)
            low_bank(0, 1, h_hi, h_split)
            for k in range(2, K):
                w0_low(k)
            low_part(1, h_hi, h_split)

            def convolution(f):
                y = qkT[:, f, :]
                link(V_.tensor_scalar(y, rawT[:, f, 0:S], cols[:, f:f + 1], None, ALU.mult))
                for i in range(1, TAPS):
                    ins = V_.scalar_tensor_tensor(y, rawT[:, f, i:i + S], cols[:, 4 * i + f:4 * i + f + 1], y,
                                                  ALU.mult, ALU.add)
                    if i < TAPS - 1:
                        link(ins)
                ins.then_inc(conv_ready, 1)

            kview = kvs[:, :, 2 * MH:2 * MH + KV * HD]
            tril32 = ident[0:32, 0:32]

            for U in range(ALL):
                g, t = U // T, U % T
                if 1 <= U <= T:
                    dve.wait_ge(mq_tp, U)
                    V_.tensor_copy(rawT[:, :, 3 + (U - 1) * P:3 + U * P],
                                   bank[4][:, :].rearrange("p (k n) -> p k n", k=4)).then_inc(mq_evac, 1)
                if U + 2 < T:
                    low_part(U + 2, h_hi, h_split)
                if U == 0:
                    dve.wait_ge(cols_tp, 1)
                    link(V_.tensor_copy(cols[:, 0:G_ROWS], bank[4][:, 0:G_ROWS]))
                    V_.tensor_scalar(cols[:, G_Q:G_Q + 1], cols[:, G_Q:G_Q + 1], HD ** -0.5, None,
                                     ALU.mult).then_inc(cols_ready, 1)
                    dve.wait_ge(cols_ready, 1)
                    dve.wait_ge(par_s, 16 * PARAMS)
                    for i2 in range(2):
                        rows = slice(i2 * CHUNK, (i2 + 1) * CHUNK)
                        heads = sinks8[rows, :].rearrange("p (g b i) -> p g b i", g=KV, i=2)[:, :, :, i2]
                        link(V_.tensor_copy(sink_b[rows, :].rearrange("p (g c b) -> p g c b", g=KV, c=2),
                                            heads.unsqueeze(2).to_broadcast([CHUNK, KV, 2, 2])))
                if U == T + 1:
                    dve.wait_ge(rstd_ready, T)
                    V_.tensor_scalar(nrstd[:, :], rstd[:, :], -1.0, None, ALU.mult).then_inc(nrstd_ready, 1)
                    dve.wait_ge(mq_evac, T)
                    dve.wait_ge(h_tp, 2 * T)
                    step(V_.memset(mvx[:, :, :, DV:DV + 1], 1.0))
                if T + 1 <= U < T + 5:
                    convolution(U - T - 1)
                if U == 2 * T:
                    dve.wait_ge(acc_free[0], T)
                    dve.wait_ge(acc_free[1], T)
                    V_.memset(v_prev[0:CHUNK, 0, :], 0.0).then_inc(v_zero, 1)
                    step(V_.memset(kT[:, 0:CHUNK], 0.0))
                    link(V_.tensor_tensor(ksq[:, :, :], kview, kview, ALU.mult))
                    V_.tensor_reduce(kss[:, :], ksq[:, :, :].rearrange("p t (g d) -> p (t g) d", g=KV),
                                     AX.X, ALU.add).then_inc(kv_stat, 1)
                    link(V_.tensor_tensor(gate8[:, :, :], kvs[:, :, 0:8],
                                          bias_g[:, :].unsqueeze(1).to_broadcast([P, T, 8]), ALU.add))
                    fpre = gate8[:, :, MH:2 * MH]
                    absf3 = absf[:, :].rearrange("p (t h) -> p t h", h=MH)
                    V_.scalar_tensor_tensor(absf3, fpre, -1.0, fpre, ALU.mult, ALU.max).then_inc(kv_stat, 1)
                if U == 2 * T + 1:
                    dve.wait_ge(kv_rs, 1)
                    for gg in range(KV):
                        kk_ = kvs[:, :, 2 * MH + gg * HD:2 * MH + (gg + 1) * HD]
                        ins = V_.tensor_tensor(kk_, kk_,
                                               bcast(krs[:, :].rearrange("p (t g) -> p t g", g=KV)[:, :, gg], HD),
                                               ALU.mult)
                        if gg == 0:
                            step(ins)
                    ins.then_inc(kn_ready, 1)
                    dve.wait_ge(gate_a, 1)
                    V_.scalar_tensor_tensor(lf[:, :].rearrange("p (t h) -> p t h", h=MH), fpre, 0.0,
                                            expf[:, :].rearrange("p (t h) -> p t h", h=MH),
                                            ALU.min, ALU.subtract).then_inc(gate_v, 1)
                if U == 2 * T + 2:
                    dve.wait_ge(kT_tp, 1)
                    for b in range(2):
                        step(V_.tensor_scalar(kT[:, CHUNK + b * N:CHUNK + (b + 1) * N], bank[2 + b][:, :],
                                              cols[:, G_K:G_K + 1], None, ALU.mult))
                    dve.wait_ge(gate_mm, 1)
                    link(V_.tensor_copy(bg[:, :], bank[5][:, 0:64]))
                    V_.tensor_tensor(u_col[:, :].rearrange("p (t h) -> p t h", h=MH), gate8[:, :, 0:MH],
                                     bg[:, 0:32].rearrange("p (t h) -> p t h", h=MH),
                                     ALU.subtract).then_inc(gate_v, 1)
                if U == 2 * T + 3:
                    dve.wait_ge(gate_mm, 2)
                    link(V_.tensor_copy(uT[:, :], bank[6][0:32, 0:P]))
                    link(V_.tensor_tensor_scan(cm[:, :], uT[:, :], uT[:, :], -3.0e38, ALU.max, ALU.max))
                    V_.tensor_scalar(diag[:, :], tril32, cm[:, P - 1:P], None, ALU.mult).then_inc(gate_v, 1)
                if U == 2 * T + 4:
                    dve.wait_ge(gate_mm, 3)
                    link(V_.tensor_copy(maxu_b[:, :], bank[7][:, 0:32]))
                    link(V_.tensor_tensor(gm[:, :], bg[:, 32:64], maxu_b[:, :], ALU.add))
                    tot = bg[:, 32:64].rearrange("p (t h) -> p t h", h=MH)
                    gm3 = gm[:, :].rearrange("p (t h) -> p t h", h=MH)
                    for h in range(MH):
                        ins = V_.tensor_tensor_scan(mm[:, 1:T + 1, h], tot[:, :, h], gm3[:, :, h], 0.0,
                                                    ALU.add, ALU.max)
                        step(ins)
                    dve.wait_ge(dve_step, steps[0])
                    mprev = mm[:, 0:T, :].rearrange("p t h -> p (t h)")
                    link(V_.tensor_tensor(mlast[:, :], mprev, maxu_b[:, :], ALU.max))
                    step(V_.tensor_tensor(aold[:, :], mprev, mlast[:, :], ALU.subtract))
                    step(V_.tensor_tensor(wexp[:, :], u_col[:, :], mlast[:, :], ALU.subtract))
                    link(V_.tensor_tensor(diag[:, :], mm[0:32, 0:T, :].rearrange("p t h -> p (t h)"), tril32,
                                          ALU.mult))
                    link(V_.tensor_reduce(mcol[:, :], diag[:, :], AX.X, ALU.add))
                    V_.tensor_scalar(nM[:, :], cm[:, :], mcol[:, 0:1], -1.0, ALU.max, ALU.mult).then_inc(gate_v, 1)
                if U == 2 * T + 5:
                    dve.wait_ge(gate_a, 2)
                    step(V_.tensor_scalar(wexp[:, :], wexp[:, :], DK ** -0.5, None, ALU.mult))
                    a4 = aold[:, :].rearrange("p (t a b) -> p t a b", a=2, b=2)
                    step(V_.tensor_copy(aold2[0:DK, :, :], a4[0:DK, :, :, 0]))
                    step(V_.tensor_copy(aold2[DK:P, :, :], a4[DK:P, :, :, 1]))
                    dve.wait_ge(gate_mm, 4)
                    V_.tensor_tensor(enm[:, :], bank[6][:, 0:32], bg[:, 0:32], ALU.subtract).then_inc(kv_stat, 1)
                    step(V_.memset(cst[:, :, :], 0.0))
                    dve.wait_ge(dve_step, steps[0])
                    V_.memset(den4[:, :], 0.0).then_inc(c_ready, 1)
                    dve.wait_ge(c_ready, 1)
                    dve.wait_ge(kv_stat, 3)
                    V_.memset(den4[:, :], 0.0).then_inc(gate_v, 1)
                s = U - 3 * T
                if 1 <= s <= T:
                    tt = s - 1
                    if tt < T - 1:
                        dve.wait_ge(cup_done, tt + 1)
                        step(V_.scalar_tensor_tensor(cst[:, 0, :], cst[:, 0, :], aold2[:, tt, 0:1],
                                                     bank[3][:, 0:DV + 1], ALU.mult, ALU.add))
                        V_.scalar_tensor_tensor(cst[:, 1, :], cst[:, 1, :], aold2[:, tt, 1:2],
                                                bank[3][:, DV + 1:2 * (DV + 1)], ALU.mult,
                                                ALU.add).then_inc(c_ready, 1)
                    dve.wait_ge(num_done, tt + 1)
                    if tt == 0:
                        dve.wait_ge(gate_a, 3)
                    for p in range(2):
                        step(V_.tensor_copy(
                            den4[:, :].rearrange("p (a b) -> p b a", b=2)[:, p, :],
                            bank[6 + p][:, 0:2 * (DV + 1)].rearrange("p (h d) -> p h d", h=2)[:, :, DV]))
                    dve.wait_ge(dve_step, steps[0])
                    link(V_.scalar_tensor_tensor(den4[:, :], den4[:, :], -1.0, den4[:, :], ALU.mult, ALU.max))
                    link(V_.tensor_tensor(den4[:, :], den4[:, :], enm[:, tt * MH:(tt + 1) * MH], ALU.max))
                    link(V_.reciprocal(den4[:, :], den4[:, :]))
                    for h in range(MH):
                        ins = V_.scalar_tensor_tensor(
                            mh[:, tt, h * DV:(h + 1) * DV],
                            bank[6 + h % 2][:, (h // 2) * (DV + 1):(h // 2) * (DV + 1) + DV],
                            den4[:, h:h + 1], sig[tt % 2][:, h * DV:(h + 1) * DV], ALU.mult, ALU.mult)
                        if h < MH - 1:
                            step(ins)
                    ins.then_inc(mh_ready, 1)
                if 0 <= s < T:
                    if s < T - 1:
                        dve.wait_ge(kt_done, s + 1)
                        V_.tensor_tensor(kw[:, :, :], bank[2][:, 0:MH * DK].rearrange("p (h d) -> p h d", h=MH),
                                         bcast(wexp[:, s * MH:(s + 1) * MH], DK), ALU.mult).then_inc(kw_ready, 1)
                    dve.wait_ge(it_exp, s + 1)
                    step(V_.tensor_tensor(qi[:, :, :], qkT[:, 0:2, s * P:(s + 1) * P], itr[:, :, :], ALU.mult))
                    dve.wait_ge(d_masked, s + 1)
                    dve.wait_ge(sc_done, s + 1)
                    for b, done in ((0, dve_step), (1, scd_ready)):
                        V_.scalar_tensor_tensor(
                            scd[:, :, :].rearrange("p (a b) n -> p b a n", b=2)[:, b, :, :],
                            bank[4 + b][:, 0:2 * P].rearrange("p (a n) -> p a n", a=2), DK ** -0.5,
                            dmat[:, :, :].rearrange("p (a b) n -> p b a n", b=2)[:, b, :, :], ALU.mult,
                            ALU.mult).then_inc(done, 1)
                    steps[0] += 1
                    dve.wait_ge(acc_free[U % 2], U // 2 + 1)
                    link(V_.tensor_scalar(sig[s % 2][:, :], sig[s % 2][:, :], 1.0, None, ALU.add))
                    link(V_.reciprocal(sig[s % 2][:, :], sig[s % 2][:, :]))
                if U >= UNITS:
                    j = U - UNITS
                    dve.wait_ge(wa_done, j + 1)
                    if j < T:
                        dve.wait_ge(rmix_ready, t + 1)
                        if t == 0:
                            dve.wait_ge(x1_s[0], 16 * 4)
                        if t == 4:
                            dve.wait_ge(x1_s[1], 16 * (T - 4))
                    xs = x1[:, t, (j // T) * N:(j // T + 1) * N]
                    V_.scalar_tensor_tensor(xs, bank[0][:, :], rmix[:, t, 0:1], xs, ALU.mult,
                                            ALU.add).then_inc(wa_free, 1)
                    dve.wait_ge(wa_free, j + 1)
                    dve.wait_ge(wb_done, j + 1)
                    V_.scalar_tensor_tensor(xs, bank[1][:, :], rmix[:, t, 1:2], xs, ALU.mult,
                                            ALU.add).then_inc(x1_ready, 1)
                s = U - 4 * T
                if 0 <= s < T:
                    dve.wait_ge(acc_free[U % 2], U // 2 + 1)
                    if s >= 1:
                        dve.wait_ge(q_rs, s)
                    V_.tensor_reduce(qss[:, :], pq[:, :].rearrange("p (h d) -> p h d", h=HEADS), AX.X,
                                     ALU.add).then_inc(q_stat, 1)
                if 0 <= s - 1 < T:
                    tt = s - 1
                    dve.wait_ge(mixb_hi, tt + 1)
                    V_.tensor_tensor(actT_lo[:, 4:8, tt * P:(tt + 1) * P],
                                     bank[3][:, :].rearrange("p (k n) -> p k n", k=4),
                                     actT_hi[:, 4:8, tt * P:(tt + 1) * P].bitcast(F32),
                                     ALU.subtract).then_inc(mixb_ready, 1)
                if 0 <= s - 2 < T:
                    tt = s - 2
                    if tt == 0:
                        dve.wait_ge(late_s, 16 * 2)
                    if tt >= 2:
                        dve.wait_ge(pt_done, tt - 1)
                    for kv, done, out_s_ in ((0, s_kv0, dve_step), (1, s_kv1, s_evac)):
                        cols_ = slice(kv * 2 * P, (kv + 1) * 2 * P)
                        if tt == 0:
                            penalty = bias[:, :, cols_]
                        else:
                            penalty = bias[:, 1, cols_].unsqueeze(1).to_broadcast([P, 2, 2 * P])
                        dve.wait_ge(done, tt + 1)
                        V_.tensor_tensor(prob[tt % 2][:, 4 * kv:4 * kv + 4, :].rearrange("p (c b) n -> p c (b n)", c=2),
                                         bank[4 + kv][:, :].rearrange("p (c n) -> p c n", c=2), penalty,
                                         ALU.add).then_inc(out_s_, 1)
                    steps[0] += 1
                    dve.wait_ge(s_evac, tt + 1)
                    link(V_.tensor_reduce(smx[:, :], prob[tt % 2][:, :, :], AX.X, ALU.max))
                    link(V_.tensor_tensor(smx[:, :], smx[:, :], sink_b[:, :], ALU.max))
                    link(V_.tensor_scalar(nmx[:, :], smx[:, :], -1.0, None, ALU.mult))
                    V_.tensor_tensor(esk[:, :], sink_b[:, :], nmx[:, :], ALU.add).then_inc(s_max, 1)
                if 0 <= s - 5 < T:
                    tt = s - 5
                    dve.wait_ge(ssa_mm, tt + 1)
                    V_.tensor_copy(ss2[:, tt, 0:1], bank[3][:, 0:1]).then_inc(ssa_ready, 1)
                if 0 <= s < T:
                    dve.wait_ge(q_rs, s + 1)
                    if s >= 1:
                        dve.wait_ge(q_tp, s)
                    V_.tensor_tensor(qn[:, :, :, :].rearrange("p i g d -> p g i d"),
                                     aqs[s % 2][:, :].rearrange("p (g i d) -> p g i d", g=KV, i=4),
                                     bcast(qrs[:, :].rearrange("p (g i) -> p g i", g=KV), HD),
                                     ALU.mult).then_inc(qn_ready, 1)
                if 0 <= s - 4 < T:
                    tt = s - 4
                    dve.wait_ge(mixa_hi, tt + 1)
                    V_.tensor_tensor(actT_lo[:, 0:4, tt * P:(tt + 1) * P],
                                     bank[2][:, :].rearrange("p (k n) -> p k n", k=4),
                                     actT_hi[:, 0:4, tt * P:(tt + 1) * P].bitcast(F32),
                                     ALU.subtract).then_inc(mixa_ready, 1)
                if 0 <= s - 3 < T:
                    tt = s - 3
                    dve.wait_ge(pt_done, tt + 1)
                    if tt >= 2:
                        dve.wait_ge(pv_done, tt - 1)
                    V_.tensor_copy(pT[tt % 2][:, 4:8, :],
                                   bank[7][:, :].rearrange("p (k n) -> p k n", k=4)).then_inc(pTd, 1)
                if 0 <= s - 2 < T:
                    tt = s - 2
                    dve.wait_ge(p_exp, tt + 1)
                    link(V_.tensor_tensor(dsum[:, :], dsum[:, :], esk[:, :], ALU.add))
                    V_.reciprocal(dsum[:, :], dsum[:, :]).then_inc(p_inv, 1)
                    dve.wait_ge(p_inv, tt + 1)
                    V_.tensor_tensor(prob[tt % 2][:, 4:8, :], prob[tt % 2][:, 4:8, :], bcast(dsum[:, 4:8], P),
                                     ALU.mult).then_inc(p_ready[1], 1)
                s = U - 6 * T
                if s == 1:
                    dve.wait_ge(gf_s, 16)
                if s >= 1:
                    normed(s - 1)
                if s >= 2:
                    low_part(s - 2, h2_hi, h2_split)

            normed(T - 1)
            low_part(T - 2, h2_hi, h2_split)

            def product_half(half, count, split=None):
                dve.wait_ge(silu_done, count)
                dve.wait_ge(up_done, count)
                if split is not None:
                    dve.wait_ge(act_ready, split)
                V_.tensor_tensor(prod[:, half * N:(half + 1) * N], bank[2 * half + 1][:, :], silu[half][:, :],
                                 ALU.mult).then_inc(prod_done, 1)

            def low_half(j, half, count):
                dve.wait_ge(act_hi_s, count)
                a = slice(half * N, (half + 1) * N)
                V_.tensor_tensor(act_lo[j][:, a], prod[:, a], act_hi[j][:, a].bitcast(F32),
                                 ALU.subtract).then_inc(act_ready, 1)

            def add_down(count):
                for half in range(2):
                    for t in range(T):
                        m = half * T + t
                        dve.wait_ge(down_mm, count + m + 1)
                        xs = x1[:, t, half * N:(half + 1) * N]
                        V_.tensor_tensor(xs, bank[4 + m % 4][:, :], xs, ALU.add).then_inc(down_add, 1)

            product_half(0, 1)
            low_half(0, 0, 1)
            low_part(T - 1, h2_hi, h2_split)
            product_half(0, 2, 1)
            low_half(1, 0, 2)
            product_half(1, 3)
            low_half(0, 1, 3)
            product_half(1, 4, 3)
            low_half(1, 1, 4)
            with dve.Fori(1, PAIRS) as i:
                product_half(0, 4 * i + 1, 4 * i - 1)
                product_half(1, 4 * i + 2, 4 * i)
                add_down((i - 1) * (2 * T))
                low_half(0, 0, 4 * i + 1)
                low_half(0, 1, 4 * i + 2)
                product_half(0, 4 * i + 3, 4 * i + 1)
                low_half(1, 0, 4 * i + 3)
                product_half(1, 4 * i + 4, 4 * i + 2)
                low_half(1, 1, 4 * i + 4)
            dve.wait_ge(act_ready, 4 * PAIRS)
            add_down(2 * T * (PAIRS - 1))


NAMES = ["x", "g_mix", "w_in", "b_gates", "conv_qk", "q_norm_gain", "k_norm_gain", "attn_sinks",
         "g_attn_out", "g_mlstm_out", "w_out", "g_ffn", "w_gate", "w_up", "w_down"]


def kernel(**inputs):
    import concourse.bacc as bacc
    from concourse.bass_utils import run_bass_kernel_spmd

    nc = bacc.Bacc("TRN2", target_bir_lowering=False, num_devices=1, dynamic_dma_scratch_size=1024)
    arrays, args = {}, []
    for name in NAMES:
        a = np.ascontiguousarray(inputs[name])
        arrays[f"in_{name}"] = a
        args.append(nc.dram_tensor(f"in_{name}", a.shape, mybir.dt.from_np(a.dtype), kind="ExternalInput").ap())
    arrays["consts"] = constants()
    args.append(nc.dram_tensor("consts", arrays["consts"].shape, F32, kind="ExternalInput").ap())
    out = nc.dram_tensor("out", inputs["x"].shape, F32, kind="ExternalOutput").ap()
    hymba_block(nc, *args, out)
    r = run_bass_kernel_spmd(nc, [arrays], core_ids=[0])
    return r.results[0]["out"]
```
